# Optimizing a Trainium2 kernel written in Bass

```python
import math
import jax
import jax.numpy as jnp
from jax import lax
import numpy as np

D_MODEL = 1024
BATCH = 1
SEQ = 512
DEPTH = 2
DEC_BATCH = 8
DEC_SEQ = 16
PAST_LEN = 256

CHUNK = 64
Q_BLOCK = 128
EPS = 1e-6
GLA_HEADS = 4
GLA_DK = 64
GLA_DV = 128
GLA_GATE_RANK = 16
GLA_GATE_NORM = 16.0
MLA_HEADS = 8
MLA_Q_LORA = 384
MLA_KV_LORA = 256
MLA_NOPE = 64
MLA_ROPE = 32
MLA_V = 64
MLA_SCALE = 1.0 / math.sqrt(MLA_NOPE + MLA_ROPE)
ROPE_BASE = 10000.0
MIX_WIDTH = GLA_HEADS * GLA_DV + MLA_HEADS * MLA_V
D_FF = 2816
N_MOD = 9
SPLITS = (GLA_HEADS * GLA_DK, GLA_HEADS * GLA_DK, GLA_HEADS * GLA_DV, GLA_GATE_RANK,
          GLA_HEADS * GLA_DV, MLA_Q_LORA, MLA_KV_LORA, MLA_ROPE)
IN_COLS = GLA_HEADS * (2 * GLA_DK + 2 * GLA_DV) + GLA_GATE_RANK + MLA_Q_LORA + MLA_KV_LORA + MLA_ROPE

kernel_name = 'hymba_gla_mla_macaron_stream'

def rmsnorm(x, g):
    xf = x.astype(jnp.float32)
    y = xf * lax.rsqrt(jnp.mean(xf * xf, axis=-1, keepdims=True) + EPS)
    return (y * g.astype(jnp.float32)).astype(x.dtype)

def rope(x, pos):
    half = MLA_ROPE // 2
    inv = ROPE_BASE ** (-jnp.arange(half, dtype=jnp.float32) / half)
    ang = pos.astype(jnp.float32)[:, None] * inv[None, :]
    ang = ang.reshape(ang.shape[:1] + (1,) * (x.ndim - 3) + (half,))
    cos = jnp.cos(ang).astype(x.dtype)
    sin = jnp.sin(ang).astype(x.dtype)
    x1, x2 = x[..., :half], x[..., half:]
    return jnp.concatenate([x1 * cos - x2 * sin, x1 * sin + x2 * cos], axis=-1)

def swiglu(x, w_in, w_out):
    a, b = jnp.split(x @ w_in, 2, axis=-1)
    return (jax.nn.silu(a) * b) @ w_out

def modulate(x, g, shift, scale):
    return rmsnorm(x, g) * (1.0 + scale) + shift

def ada_mod(c, w, b):
    m = jax.nn.silu(c) @ w + b
    return jnp.split(m[:, None, :], N_MOD, axis=-1)

def split_cols(h):
    idx, acc = [], 0
    for w in SPLITS[:-1]:
        acc += w
        idx.append(acc)
    return jnp.split(h, idx, axis=-1)

def gla_block(q, k, v, logg, s0):
    C = q.shape[2]
    b = jnp.cumsum(logg, axis=2)
    causal = jnp.tril(jnp.ones((C, C), dtype=bool))
    diff = b[:, :, :, None, :] - b[:, :, None, :, :]
    decay = jnp.exp(jnp.where(causal[None, None, :, :, None], diff, -jnp.inf))
    att = jnp.einsum('bhtk,bhsk,bhtsk->bhts', q, k, decay)
    o = jnp.einsum('bhts,bhsv->bhtv', att, v) + jnp.einsum('bhtk,bhkv->bhtv', q * jnp.exp(b), s0)
    b_last = b[:, :, -1:, :]
    s1 = jnp.exp(b_last[:, :, 0, :])[..., None] * s0 + jnp.einsum('bhsk,bhsv->bhkv', k * jnp.exp(b_last - b), v)
    return o, s1

def gla_scan(q, k, v, logg, s0):
    B, H, L, _ = q.shape
    n = L // CHUNK

    def to_blocks(a):
        return jnp.moveaxis(a.reshape(B, H, n, CHUNK, a.shape[-1]), 2, 0)

    def step(s, blk):
        o, s = gla_block(blk[0], blk[1], blk[2], blk[3], s)
        return s, o

    s_final, o = lax.scan(step, s0, (to_blocks(q), to_blocks(k), to_blocks(v), to_blocks(logg)))
    o = jnp.moveaxis(o, 0, 2).reshape(B, H, L, v.shape[-1])
    return o, s_final

def gla_mixer(gq, gk, gv, glr, gog, w_gk2, b_gk2, norm_g, s0, blocked):
    B, L, _ = gq.shape

    def heads(a, d):
        return a.reshape(B, L, GLA_HEADS, d).transpose(0, 2, 1, 3).astype(jnp.float32)

    q = heads(gq, GLA_DK) * (GLA_DK ** -0.5)
    k = heads(gk, GLA_DK)
    v = heads(gv, GLA_DV)
    logg = heads(jax.nn.log_sigmoid((glr @ w_gk2 + b_gk2).astype(jnp.float32)) / GLA_GATE_NORM, GLA_DK)
    s0 = s0.astype(jnp.float32)
    if blocked:
        o, s1 = gla_scan(q, k, v, logg, s0)
    else:
        o, s1 = gla_block(q, k, v, logg, s0)
    o = o.transpose(0, 2, 1, 3).astype(gv.dtype)
    o = rmsnorm(o, norm_g) * jax.nn.silu(gog.reshape(B, L, GLA_HEADS, GLA_DV))
    return o.reshape(B, L, GLA_HEADS * GLA_DV), s1

def mla_project(cq, ckv_raw, kpe_raw, qnorm_g, w_uq, kvnorm_g, pos):
    B, L = cq.shape[:2]
    q = (rmsnorm(cq, qnorm_g) @ w_uq).reshape(B, L, MLA_HEADS, MLA_NOPE + MLA_ROPE)
    q_nope = q[..., :MLA_NOPE]
    q_pe = rope(q[..., MLA_NOPE:], pos)
    ckv = rmsnorm(ckv_raw, kvnorm_g)
    kpe = rope(kpe_raw, pos)
    return q_nope, q_pe, ckv, kpe

def mla_attend(q_nope, q_pe, q_pos, k_nope, k_pe, v, k_pos):
    s = jnp.einsum('bqhd,bkhd->bhqk', q_nope, k_nope) + jnp.einsum('bqhr,bkr->bhqk', q_pe, k_pe)
    s = s.astype(jnp.float32) * MLA_SCALE
    mask = (k_pos[None, :] // CHUNK) <= (q_pos[:, None] // CHUNK)
    s = jnp.where(mask[None, None], s, -jnp.inf)
    p = jax.nn.softmax(s, axis=-1).astype(v.dtype)
    return jnp.einsum('bhqk,bkhv->bqhv', p, v)

def mla_blocks(q_nope, q_pe, q_pos, k_nope, k_pe, v, k_pos):
    B, L = q_nope.shape[:2]
    nb = L // Q_BLOCK

    def blk(a):
        return jnp.swapaxes(a.reshape((B, nb, Q_BLOCK) + a.shape[2:]), 0, 1)

    out = lax.map(lambda t: mla_attend(t[0], t[1], t[2], k_nope, k_pe, v, k_pos),
                  (blk(q_nope), blk(q_pe), q_pos.reshape(nb, Q_BLOCK)))
    return jnp.swapaxes(out, 0, 1).reshape((B, L) + out.shape[3:])

def token_mixer(n, pos, p, l, gla_s0=None, past_ckv=None, past_kpe=None):
    B, L, _ = n.shape
    gq, gk, gv, glr, gog, cq, ckv_raw, kpe_raw = split_cols(n @ p['w_in'][l])
    stream = past_ckv is not None
    if gla_s0 is None:
        gla_s0 = jnp.zeros((B, GLA_HEADS, GLA_DK, GLA_DV), jnp.float32)
    o_gla, s_gla = gla_mixer(gq, gk, gv, glr, gog, p['w_gk2'][l], p['b_gk2'][l],
                             p['gla_norm_g'][l], gla_s0, not stream)
    q_nope, q_pe, ckv, kpe = mla_project(cq, ckv_raw, kpe_raw, p['mla_qnorm_g'][l], p['w_uq'][l],
                                         p['mla_kvnorm_g'][l], pos)
    if stream:
        ckv_all = jnp.concatenate([past_ckv.astype(ckv.dtype), ckv], axis=1)
        kpe_all = jnp.concatenate([past_kpe.astype(kpe.dtype), kpe], axis=1)
        k_pos = jnp.arange(ckv_all.shape[1])
    else:
        ckv_all, kpe_all, k_pos = ckv, kpe, pos
    kv = (ckv_all @ p['w_ukv'][l]).reshape(B, ckv_all.shape[1], MLA_HEADS, MLA_NOPE + MLA_V)
    k_nope, v = kv[..., :MLA_NOPE], kv[..., MLA_NOPE:]
    if stream:
        o_mla = mla_attend(q_nope, q_pe, pos, k_nope, kpe_all, v, k_pos)
    else:
        o_mla = mla_blocks(q_nope, q_pe, pos, k_nope, kpe_all, v, k_pos)
    o = jnp.concatenate([o_gla, o_mla.reshape(B, L, MLA_HEADS * MLA_V)], axis=-1) @ p['w_out'][l]
    return o, ckv, kpe, s_gla

def trunk(x, c, pos, p, gla_state=None, past_ckv=None, past_kpe=None):
    ckvs, kpes, states = [], [], []
    for l in range(DEPTH):
        sh1, sc1, g1, sh2, sc2, g2, sh3, sc3, g3 = ada_mod(c, p['w_ada'][l], p['b_ada'][l])
        x = x + 0.5 * (1.0 + g1) * swiglu(modulate(x, p['ln_g'][l, 0], sh1, sc1),
                                          p['w_ffn1_in'][l], p['w_ffn1_out'][l])
        n = modulate(x, p['ln_g'][l, 1], sh2, sc2)
        if past_ckv is None:
            mix, ckv, kpe, s = token_mixer(n, pos, p, l)
        else:
            mix, ckv, kpe, s = token_mixer(n, pos, p, l, gla_state[l], past_ckv[l], past_kpe[l])
        x = x + (1.0 + g2) * mix
        x = x + 0.5 * (1.0 + g3) * swiglu(modulate(x, p['ln_g'][l, 2], sh3, sc3),
                                          p['w_ffn2_in'][l], p['w_ffn2_out'][l])
        ckvs.append(ckv)
        kpes.append(kpe)
        states.append(s)
    y = rmsnorm(x, p['final_g'])
    return y, jnp.stack(ckvs), jnp.stack(kpes), jnp.stack(states).astype(x.dtype)

def setup_inputs(seed: int = 0) -> dict:
    key = jax.random.key(seed)
    ks = jax.random.split(key, 24)

    def nrm(k, shape, scale=1.0):
        return jax.random.normal(k, shape, jnp.float32) * scale

    return {
        'x_prompt': nrm(ks[0], (BATCH, SEQ, D_MODEL)),
        'x_sample': nrm(ks[1], (DEC_BATCH, DEC_SEQ, D_MODEL)),
        'cache_ckv': nrm(ks[2], (DEPTH, DEC_BATCH, PAST_LEN, MLA_KV_LORA)),
        'cache_kpe': nrm(ks[3], (DEPTH, DEC_BATCH, PAST_LEN, MLA_ROPE)),
        'state_gla': nrm(ks[4], (DEPTH, DEC_BATCH, GLA_HEADS, GLA_DK, GLA_DV), 0.5),
        'c_prompt': nrm(ks[5], (BATCH, D_MODEL)),
        'c_sample': nrm(ks[6], (DEC_BATCH, D_MODEL)),
        'ln_g': 1.0 + nrm(ks[7], (DEPTH, 3, D_MODEL), 0.02),
        'w_ada': nrm(ks[8], (DEPTH, D_MODEL, N_MOD * D_MODEL), 0.3 * D_MODEL ** -0.5),
        'b_ada': nrm(ks[9], (DEPTH, N_MOD * D_MODEL), 0.01),
        'w_ffn1_in': nrm(ks[10], (DEPTH, D_MODEL, 2 * D_FF), D_MODEL ** -0.5),
        'w_ffn1_out': nrm(ks[11], (DEPTH, D_FF, D_MODEL), D_FF ** -0.5),
        'w_ffn2_in': nrm(ks[12], (DEPTH, D_MODEL, 2 * D_FF), D_MODEL ** -0.5),
        'w_ffn2_out': nrm(ks[13], (DEPTH, D_FF, D_MODEL), D_FF ** -0.5),
        'w_in': nrm(ks[14], (DEPTH, D_MODEL, IN_COLS), D_MODEL ** -0.5),
        'w_gk2': nrm(ks[15], (DEPTH, GLA_GATE_RANK, GLA_HEADS * GLA_DK), GLA_GATE_RANK ** -0.5),
        'b_gk2': nrm(ks[16], (DEPTH, GLA_HEADS * GLA_DK), 0.01),
        'gla_norm_g': 1.0 + nrm(ks[17], (DEPTH, GLA_DV), 0.02),
        'mla_qnorm_g': 1.0 + nrm(ks[18], (DEPTH, MLA_Q_LORA), 0.02),
        'w_uq': nrm(ks[19], (DEPTH, MLA_Q_LORA, MLA_HEADS * (MLA_NOPE + MLA_ROPE)), MLA_Q_LORA ** -0.5),
        'mla_kvnorm_g': 1.0 + nrm(ks[20], (DEPTH, MLA_KV_LORA), 0.02),
        'w_ukv': nrm(ks[21], (DEPTH, MLA_KV_LORA, MLA_HEADS * (MLA_NOPE + MLA_V)), MLA_KV_LORA ** -0.5),
        'w_out': nrm(ks[22], (DEPTH, MIX_WIDTH, D_MODEL), MIX_WIDTH ** -0.5),
        'final_g': 1.0 + nrm(ks[23], (D_MODEL,), 0.02),
    }

def reference(x_prompt, x_sample, cache_ckv, cache_kpe, state_gla, c_prompt, c_sample,
              ln_g, w_ada, b_ada, w_ffn1_in, w_ffn1_out, w_ffn2_in, w_ffn2_out,
              w_in, w_gk2, b_gk2, gla_norm_g, mla_qnorm_g, w_uq, mla_kvnorm_g, w_ukv,
              w_out, final_g):
    p = {'ln_g': ln_g, 'w_ada': w_ada, 'b_ada': b_ada,
         'w_ffn1_in': w_ffn1_in, 'w_ffn1_out': w_ffn1_out,
         'w_ffn2_in': w_ffn2_in, 'w_ffn2_out': w_ffn2_out,
         'w_in': w_in, 'w_gk2': w_gk2, 'b_gk2': b_gk2, 'gla_norm_g': gla_norm_g,
         'mla_qnorm_g': mla_qnorm_g, 'w_uq': w_uq, 'mla_kvnorm_g': mla_kvnorm_g,
         'w_ukv': w_ukv, 'w_out': w_out, 'final_g': final_g}
    pos_p = jnp.arange(x_prompt.shape[1])
    y_prompt, ckv_p, kpe_p, gla_p = trunk(x_prompt, c_prompt, pos_p, p)
    past = cache_ckv.shape[2]
    pos_s = past + jnp.arange(x_sample.shape[1])
    y_sample, ckv_s, kpe_s, gla_s = trunk(x_sample, c_sample, pos_s, p, state_gla, cache_ckv, cache_kpe)
    return (y_prompt, y_sample, ckv_p, kpe_p, gla_p, ckv_s, kpe_s, gla_s)


_drawn_inputs = setup_inputs


def setup_inputs(seed=0):
    import zlib

    import numpy as np

    out = dict(_drawn_inputs(seed))
    spreads = {}
    factors = {'b_gk2': 8.0,
     'gla_norm_g': 4.926,
     'mla_qnorm_g': 8.0,
     'mla_kvnorm_g': 2.942,
     'final_g': 2.895}
    for name, (base, spread) in spreads.items():
        noise = np.random.default_rng([zlib.crc32(name.encode()), seed]).standard_normal(out[name].shape)
        drawn = base * np.exp(spread * noise) if base else spread * noise
        out[name] = jnp.asarray(drawn.astype(out[name].dtype))
    for name, factor in factors.items():
        out[name] = (out[name] * factor).astype(out[name].dtype)
    return out
```

```python
from contextlib import ExitStack

import concourse.bass as bass
from concourse import mybir

F32 = mybir.dt.float32
F32R = mybir.dt.float32r
ALU = mybir.AluOpType
ACT = mybir.ActivationFunctionType
AX = mybir.AxisListType

P = 128
D = 1024
DC = D // P
SEQ, NDEC, DSEQ, PAST = 512, 8, 16, 256
NT = SEQ + NDEC * DSEQ
HALF = NT // 2
HP1 = SEQ - HALF
NS = 1 + NDEC
DEPTH = 2
NFF = 22
PORT = (8, 8, 6)
PBASE = (0, 8, 16)
FFN_U = 2 * NFF + 3 * DC
MIX_U = 32
MIX_T = DC
OUT_T = 6 * DC + MIX_T
LAYER_U = 2 * FFN_U + MIX_U
TOTAL_U = DEPTH * LAYER_U
LEAD = 2
UW = 8 * P
DV_STEPS = 101
ADA_PRO = 7
ADA_IN = 11
NMOD = 72
EPS = 1e-6
CH, SUB = 64, 16
NCH, NSUB = SEQ // CH, CH // SUB
GH, GK, GV, GR = 4, 64, 128, 16
MH, NOPE, ROPE, MV = 8, 64, 32, 64
QL, KL = 3, 2
MLA_SCALE = (NOPE + ROPE) ** -0.5
GATE_NORM = 16.0
KHAT = [NCH * SUB * i * (i + 1) // 2 for i in range(NSUB + 1)]
SHARP = -1e30
T4 = NT * 4
NPB = 5
U_S, U_GQ, U_GK, U_GOG, U_GV, U_CQ, U_CKV, U_UQ, U_UK, U_UV, U_OUT = 0, 1, 3, 5, 9, 13, 16, 18, 22, 23, 24


class Signal:

    def __init__(self, sem, per_layer):
        self.sem, self.per_layer, self.sent = sem, per_layer, 0

    def send(self, ins):
        ins.then_inc(self.sem, 1)
        self.sent += 1

    def wait(self, eng, l, k):
        assert 0 <= k < self.per_layer
        eng.wait_ge(self.sem, l * self.per_layer + (k + 1))

    def last(self, eng, l):
        self.wait(eng, l, self.sent - 1)


def build(nc, xT, cT, lng, bada, fing, selc, wmain, wada, scanm, gk2_in, gains_in, tri_in, bd_in, seqm_in,
          ident_in, mrow_in, cs_in, ukT, wuv_in, past_kT, past_v, past_pe, s0_in,
          y_out, ckv_out, kpe_out, glap_out, glas_out):
    with ExitStack() as ctx:
        where = [16512]

        def sb(name, shape, dt=F32, at=None):
            n = 4
            for d in shape[1:]:
                n *= d
            if at is None:
                at = where[0]
                where[0] += (n + 31) // 32 * 32
            return nc.alloc_sbuf_tensor_at(name, shape, dt, offset=at), at + (n + 31) // 32 * 32

        def new(name, shape, dt=F32):
            return sb(name, shape, dt)[0]

        def sem(name):
            return ctx.enter_context(nc.semaphore(name))

        bank = [ctx.enter_context(nc.psum_tensor(f"bank{i}", [P, 512], F32)) for i in range(8)]
        ADA_ACC, ADA_SEL = bank[6], bank[7]
        ADA_FIRST = (bank[6], bank[5])

        x = new("x", [P, DC, NT])
        n_at = where[0]
        n_hi = new("n_hi", [P, DC, NT], F32R)
        n_lo = new("n_lo", [P, DC, NT], F32R)
        arena_a = where[0]
        h_hi = new("h_hi", [P, 8, NT], F32R)
        h_lo = new("h_lo", [P, 8, NT], F32R)
        raw = [new(f"raw{i}", [P, UW]) for i in range(2)]
        w_hi = [new(f"w_hi{i}", [P, 8, P], F32R) for i in range(4)]
        w_lo = [new(f"w_lo{i}", [P, 8, P], F32R) for i in range(4)]
        c_st = new("c_st", [P, DC, P], F32R)
        c_in = sb("c_in", [P, DC, NS], at=arena_a)[0]
        c_sil = sb("c_sil", [P, DC, NS], at=arena_a + 512)[0]
        sel = new("sel", [2 * NS, NS])
        ones = new("ones", [P, P])
        eps = new("eps", [P, 1])
        warm = new("warm", [P, 1])
        mods = new("mods", [P, DEPTH, NMOD, NS])
        b_ada = new("b_ada", [P, DEPTH, NMOD])
        ln_g = new("ln_g", [P, DEPTH, 3, DC])
        fin_g = new("fin_g", [P, DC])
        mod_a = new("mod_a", [P, DC, NS])
        mod_b = new("mod_b", [P, DC, NS])
        mod_g = new("mod_g", [P, DC, NS])
        gains = new("gains", [P, DEPTH, 8])
        gain = new("gain", [P, 8])
        tri = new("tri", [P, CH])
        bd = new("bd", [P, P])
        seqm = new("seqm", [P, NDEC])
        ident = new("ident", [P, P])
        mrow = new("mrow", [1, P + CH])
        elast = new("elast", [P, NCH + NDEC])
        mx = new("mx", [P, 4])
        psums = new("psums", [P, 4])
        psum2 = new("psum2", [P, 4])
        rsum = new("rsum", [P, 4])

        arena_b = where[0]
        araw = [new(f"araw{i}", [P, UW]) for i in range(2)]
        a_hi = [new(f"a_hi{i}", [P, 2, 512], F32R) for i in range(2)]
        a_lo = [new(f"a_lo{i}", [P, 2, 512], F32R) for i in range(2)]
        for i in (2, 3):
            at = arena_a + 1024 + 12288 * (i - 2)
            araw.append(sb(f"araw{i}", [P, UW], at=at)[0])
            a_hi.append(sb(f"a_hi{i}", [P, 2, 512], F32R, at=at + 4096)[0])
            a_lo.append(sb(f"a_lo{i}", [P, 2, 512], F32R, at=at + 8192)[0])
        sq_at = where[0]
        sq = [new(f"sq{i}", [P, NT]) for i in range(2)]
        us = sb("us", [P, DC, P], at=sq_at)[0]
        rms = new("rms", [P, NT])
        rstd = new("rstd", [P, NT])
        acc = new("acc", [P, NT])
        sil = [new(f"sil{i}", [P, HALF]) for i in range(2)]
        hf = [new(f"hf{i}", [P, HALF]) for i in range(2)]
        u = [new(f"u{i}", [P, HALF]) for i in range(3)]
        ev = new("ev", [2 * NS, 512])
        ytmp = new("ytmp", [P, NDEC, DSEQ])
        assert arena_b + 55296 <= 229368, arena_b + 55296
        y_sb = sb("y_sb", [P, DC, NT], at=n_at)[0]

        def in_a(name, shape, at, dt=F32):
            return sb(name, shape, dt, at=arena_a + at)[0]

        def in_b(name, shape, at, dt=F32):
            return sb(name, shape, dt, at=arena_b + at)[0]

        def in_n(name, shape, half, tiles, dt=F32):
            return sb(name, shape, dt, at=n_at + half * DC * T4 + tiles * T4)[0]

        cq = in_a("cq", [P, QL, NT], 0)
        ckv = in_a("ckv", [P, KL, NT], 8192)
        gq = in_a("gq", [P, 2, NT], 15360)
        gk = in_a("gk", [P, 2, NT], 20480)
        gb = in_a("gb", [P, 2, NT], 25600)
        gog = in_a("gog", [P, GH, NT], 30720)
        v_m = in_a("v_m", [P, 4, MH * MV], 13312)
        q_abs = in_a("q_abs", [P, KL, NDEC, MH * DSEQ], 21504)
        uk_t = in_a("uk_t", [NOPE, MH, KL * P], 30720)
        p_s = [in_a(f"p_s{i}", [P, 3 * P], 30720 + 1536 * i) for i in range(4)]
        pt_s = [in_a(f"pt_s{i}", [P, 3, P], 36864 + 1536 * i) for i in range(2)]
        cn_t = in_a("cn_t", [P, KL * P], 39936)
        o_lat = in_a("o_lat", [P, KL, MH, P], 0)
        pt_p = [in_a(f"pt_p{i}", [P, 4, P], 30720 + 2048 * i) for i in range(3)]
        v_g = in_b("v_g", [P, 5, GH * GV], 0)
        q_sub = in_b("q_sub", [P, 2, NT], 10240)
        q_blk = in_b("q_blk", [P, 2, NT], 15360)
        att = in_b("att", [P, 5, 2, P], 20480)
        kd_t = in_b("kd_t", [P, 4, 2, P], 25600)
        kd_s = in_b("kd_s", [P, NDEC, P], 29696)
        k_sub = in_b("k_sub", [P, KHAT[NSUB] + P], 33792)
        soft = in_b("soft", [P, 2, NT], 33792)
        k_dec = in_b("k_dec", [P, NT], 39424)
        scan_m = in_b("scan_m", [P, NT], 39424)
        e_b = in_b("e_b", [P, NT], 41984)
        s_p = in_b("s_p", [P, NCH, GV], 44544)
        w_gk = in_b("w_gk", [GR, 2 * P], 44544)
        s_s = in_b("s_s", [P, NDEC, GV], 48640)
        kg = in_b("kg", [P, NT], 52736)
        q_h = in_b("q_h", [96, MH, NT], 0)
        k_h = in_b("k_h", [96, MH, SEQ], 20480)
        cs = in_b("cs", [P, NT], 36864)
        w_uv = in_b("w_uv", [P, KL, MH * MV], 36864)
        p_p = [in_b(f"p_p{i}", [P, SEQ], 40960 + 2048 * i) for i in range(4)]
        r_t = in_b("r_t", [96, HALF], 51200)
        c_hi = in_n("c_hi", [P, KL, NT], 0, 0, F32R)
        c_lo = in_n("c_lo", [P, KL, NT], 1, 0, F32R)
        o_sq = in_n("o_sq", [P, 2 * NT], 0, 2)
        o_rs = in_n("o_rs", [P, 2 * NT], 1, 2)
        qn_hi = in_n("qn_hi", [P, QL, NT], 0, 4, F32R)
        qn_lo = in_n("qn_lo", [P, QL, NT], 1, 4, F32R)
        lat_sq = [in_n(f"lat_sq{i}", [P, NT], i, 7) for i in range(2)]
        past_at = [arena_b + 40960, arena_b + 46080, n_at + (DC + 6) * T4, n_at + 4 * T4, n_at + (DC + 4) * T4]
        pk_t = [sb(f"pk_t{i}", [P, KL, PAST], at=a)[0] for i, a in enumerate(past_at)]
        pv = [sb(f"pv{i}", [P, 2, KL * P], at=a + 2048)[0] for i, a in enumerate(past_at)]
        pp_t = [sb(f"pp_t{i}", [96, PAST], at=a + 4096)[0] for i, a in enumerate(past_at)]
        q_pe = in_n("q_pe", [96, NDEC, MH * DSEQ], 0, 6)
        o_hi = in_n("o_hi", [P, DC, NT], 0, 0, F32R)
        o_lo = in_n("o_lo", [P, DC, NT], 1, 0, F32R)

        raw_full = [sem(f"raw_full{i}") for i in range(2)]
        whi_done = sem("whi_done")
        wlo_done = sem("wlo_done")
        wslot_free = sem("wslot_free")
        ada_full = [sem(f"ada_full{i}") for i in range(4)]
        ahi_done = sem("ahi_done")
        alo_done = sem("alo_done")
        aslot_free = sem("aslot_free")
        ev_done = sem("ev_done")
        sel_done = sem("sel_done")
        mod_done = sem("mod_done")
        const_in = sem("const_in")
        x_in = sem("x_in")
        csil_done = sem("csil_done")
        cst_done = sem("cst_done")
        const_done = sem("const_done")
        gate_done = sem("gate_done")
        sil_done = sem("sil_done")
        gate_free = sem("gate_free")
        hhi_done = sem("hhi_done")
        h_ready = sem("h_ready")
        out_done = sem("out_done")
        y_free = sem("y_free")
        ytmp_done = sem("ytmp_done")
        x_done = sem("x_done")
        sq_done = sem("sq_done")
        acc_done = sem("acc_done")
        stat_done = sem("stat_done")
        rms_done = sem("rms_done")
        warm_done = sem("warm_done")
        rstd_done = sem("rstd_done")
        mab_done = sem("mab_done")
        modg_done = sem("modg_done")
        u_done = sem("u_done")
        us_step = sem("us_step")
        nhi_s_done = sem("nhi_s_done")
        ns_ready = sem("ns_ready")
        nhi_done = sem("nhi_done")
        n_ready = sem("n_ready")
        y_done = sem("y_done")
        y_stored = sem("y_stored")

        signals = []

        def signal(name, per_layer):
            signals.append(Signal(sem(name), per_layer))
            return signals[-1]

        cst_in = sem("cst_in")
        proj_mm = signal("proj_mm", 14)
        z_mm = signal("z_mm", 4)
        gv_mm = signal("gv_mm", 4)
        lat_mm = signal("lat_mm", 4)
        lat_mm_sq = signal("lat_mm_sq", 2)
        pv_mm = signal("pv_mm", 32)
        att_mm = signal("att_mm", 4)
        kdt_mm = signal("kdt_mm", 4)
        ds_mm = signal("ds_mm", 8)
        o_mm = signal("o_mm", 6)
        ost_mm = signal("ost_mm", 6)
        q_mm = signal("q_mm", 12)
        k_mm = signal("k_mm", 3)
        v_mm = signal("v_mm", 3)
        qa_mm = signal("qa_mm", 4)
        cn_mm = signal("cn_mm", 1)
        s_mm = signal("s_mm", 40)
        t_mm = signal("t_mm", 40)
        ol_mm = signal("ol_mm", 8)
        uv_mm = signal("uv_mm", 1)
        gqk_out = signal("gqk_out", 8)
        gog_out = signal("gog_out", 8)
        soft_e = signal("soft_e", 2)
        e_done = signal("e_done", 8)
        cq_out = signal("cq_out", 6)
        lsq = signal("lsq", 5)
        lrs = signal("lrs", 8)
        kdt_out = signal("kdt_out", 4)
        osq = signal("osq", 6)
        orn = signal("orn", 12)
        qh_out = signal("qh_out", 16)
        kh_out = signal("kh_out", 9)
        qa_out = signal("qa_out", 4)
        p_exp = signal("p_exp", 40)
        p_exp_a = signal("p_exp_a", 8)
        pt_out = signal("pt_out", 40)
        chi_out = signal("chi_out", 5)
        ohi_out = signal("ohi_out", 9)
        s_out = signal("s_out", 2)
        z_out = signal("z_out", 4)
        gv_out = signal("gv_out", 5)
        ckv_ev = signal("ckv_ev", 4)
        dv = signal("dv", DV_STEPS)
        zabs = signal("zabs", 1)
        scan_done = signal("scan_done", 2)
        kds_out = signal("kds_out", 2)
        dec = signal("dec", 6)
        qk_ready = signal("qk_ready", 8)
        zeroed = signal("zeroed", 1)
        att_out = signal("att_out", 4)
        ds_out = signal("ds_out", 8)
        o_mul = signal("o_mul", 6)
        gla_fin = signal("gla_fin", 6)
        lat_n = signal("lat_n", 10)
        clo = signal("clo", 5)
        rope_done = signal("rope_done", 16)
        kpe_done = signal("kpe_done", 2)
        qpe_out = signal("qpe_out", 1)
        vm_out = signal("vm_out", 4)
        cn_out = signal("cn_out", 1)
        p_max = signal("p_max", 40)
        p_norm = signal("p_norm", 40)
        ol_out = signal("ol_out", 8)
        olo = signal("olo", 9)
        scan_in, cs_ld, uk_in, uv_in, kv_st, gla_st, s_in = (
            sem(n) for n in ("scan_in", "cs_ld", "uk_in", "uv_in", "kv_st", "gla_st", "s_in"))
        past_in = [sem(f"past_in{i}") for i in range(NPB)]

        block = ctx.enter_context(nc.Block())

        def unit(l, f, p, k):
            at = 0 if f == 0 else FFN_U + MIX_U
            at += sum(2 * PORT[q] + DC for q in range(p))
            return l * LAYER_U + at + k

        def half_pair(l, f, p, c, s):
            return (l * 2 + f) * 2 * NFF + 2 * (PBASE[p] + c) + s

        def pair(l, f, p, c):
            return (l * 2 + f) * NFF + PBASE[p] + c

        OSPAN = ((0, 512), (512, 1024), (1024, 1280))
        GLA_BANKS = (dict(A=4, AS=5, KT=0, KTS=(7, 0), DS=(1, 2), DSS=(3, 6), O=(4, 5, 7), ST=(1, 2, 3)),
                     dict(A=0, AS=6, KT=1, KTS=(4, 0), DS=(2, 3), DSS=(1, 4), O=(5, 7, 0), ST=(2, 3, 6)))
        QBANKS = ((1, 4), (2, 3), (6, 5), (7, 0)) * 2
        SBANKS, TBANKS = (6, 5, 2, 3), (7, 0)

        def out_tile(l, f, p, m):
            return l * OUT_T + f * (3 * DC + MIX_T) + p * DC + m

        cols = (slice(0, HALF), slice(HALF, NT))

        @block.sync
        def _(sp):
            def load_main(at, s):
                sp.dma_start(raw[s][:], wmain[at]).then_inc(raw_full[s], 16)

            def load_next(at, s):
                sp.wait_ge(wlo_done, at - 1)
                load_main(at, s)

            def load_ada(at, s, ring):
                sp.wait_ge(alo_done, at + 5 - ring)
                sp.dma_start(araw[s][:], wada[at]).then_inc(ada_full[s], 16)

            sp.dma_start(c_in[:], cT).then_inc(const_in, 16)
            sp.dma_start(b_ada[:], bada).then_inc(const_in, 16)
            sp.dma_start(ln_g[:], lng).then_inc(const_in, 16)
            sp.dma_start(fin_g[:], fing).then_inc(const_in, 16)
            sp.dma_start(sel[:], selc).then_inc(const_in, 16)
            for k in range(8):
                load_ada(k, k % 4, 4)
            sp.dma_start(x[:], xT).then_inc(x_in, 16)
            load_main(0, 0)
            load_main(1, 1)
            for dst, src in ((gains, gains_in), (tri, tri_in), (bd, bd_in),
                             (seqm, seqm_in), (ident, ident_in), (mrow, mrow_in)):
                sp.dma_start(dst[:], src).then_inc(cst_in, 16)
            with sp.Fori(2, DEPTH * ADA_PRO) as t:
                for k in range(4):
                    load_ada(4 * t + k, k, 4)
            with sp.Fori(0, DEPTH) as l:
                for f in range(2):
                    for p in range(3):
                        with sp.Fori(0, PORT[p] // 2) as i:
                            for k in range(4):
                                if f == 0:
                                    load_ada(DEPTH * ADA_PRO * 4 + l * ADA_IN * 4 + (PBASE[p] * 2 + 4 * i) + k, k % 2, 2)
                                load_next(unit(l, f, p, 0) + 4 * i + k + LEAD, k % 2)
                        with sp.Fori(0, DC // 2) as i:
                            for k in range(2):
                                load_next(unit(l, f, p, 2 * PORT[p]) + 2 * i + k + LEAD, k)
                    if f == 0:
                        with sp.Fori(0, MIX_U // 2) as i:
                            for k in range(2):
                                load_next(l * LAYER_U + FFN_U + 2 * i + k + LEAD, k)
            sp.wait_ge(y_done, 2 * DC)
            sp.dma_start(y_out, y_sb[:]).then_inc(y_stored, 16)
            sp.wait_ge(y_stored, 16)
            sp.wait_ge(kv_st, 32 * DEPTH)
            sp.wait_ge(gla_st, 64 * DEPTH)

        @block.gpsimd
        def _(pool):
            def low(at, slot):
                pool.wait_ge(whi_done, at + 1)
                pool.tensor_tensor(w_lo[slot][:], raw[slot % 2][:].rearrange("p (c m) -> p c m", m=P),
                                   w_hi[slot][:].bitcast(F32), ALU.subtract).then_inc(wlo_done, 1)

            def norm_samples(g):
                sv = us[:].rearrange("p m (i t) -> p m i t", t=DSEQ)
                pool.wait_ge(rstd_done, 2 * g + 2)
                pool.tensor_tensor(us[:], x[:, :, SEQ:NT], rstd[:, SEQ:NT].unsqueeze(1).broadcast_to((P, DC, P)),
                                   ALU.mult).then_inc(us_step, 1)
                pool.wait_ge(mab_done, 3 * g + 3)
                pool.wait_ge(us_step, 3 * g + 1)
                pool.tensor_tensor(sv, sv, mod_a[:, :, 1:NS].unsqueeze(3).broadcast_to((P, DC, NDEC, DSEQ)),
                                   ALU.mult).then_inc(us_step, 1)
                pool.wait_ge(us_step, 3 * g + 2)
                pool.tensor_tensor(sv, sv, mod_b[:, :, 1:NS].unsqueeze(3).broadcast_to((P, DC, NDEC, DSEQ)),
                                   ALU.add).then_inc(us_step, 1)
                pool.wait_ge(nhi_s_done, g + 1)
                pool.tensor_tensor(n_lo[:, :, SEQ:NT], us[:], n_hi[:, :, SEQ:NT].bitcast(F32), ALU.subtract)\
                    .then_inc(ns_ready, 1)

            for k in range(LEAD):
                low(k, k)
            with pool.Fori(0, DEPTH) as l:
                for n, (first, count) in enumerate(((0, FFN_U), (FFN_U, MIX_U), (FFN_U + MIX_U, FFN_U))):
                    norm_samples(3 * l + n)
                    with pool.Fori(0, count // 4) as i:
                        for k in range(4):
                            low(l * LAYER_U + first + 4 * i + k + LEAD, (k + LEAD) % 4)

        @block.scalar
        def _(act):
            def split_hi(at, at2, slot):
                act.wait_ge(raw_full[slot % 2], 16 * (at2 + 1))
                act.wait_ge(wslot_free, at + 1)
                act.copy(w_hi[slot][:], raw[slot % 2][:].rearrange("p (c m) -> p c m", m=P)).then_inc(whi_done, 1)

            def ada_hi(at, nth, s, ring):
                act.wait_ge(ada_full[s], 16 * (nth + 1))
                act.wait_ge(aslot_free, at + 5 - ring)
                act.copy(a_hi[s][:], araw[s][:].rearrange("p (c m) -> p c m", m=512)).then_inc(ahi_done, 1)

            def square(g, m, wait_x):
                wait_x()
                if m >= 3:
                    act.wait_ge(acc_done, 7 * g + m - 2)
                dst = acc if m == 0 else sq[m % 2]
                act.activation(dst[:], x[:, m, :], ACT.Square).then_inc(sq_done, 1)

            def norm_rstd(g):
                act.wait_ge(warm_done, g + 1)
                act.activation(warm[:], eps[:], ACT.Sqrt).then_inc(warm_done, 1)
                for s in range(2):
                    act.wait_ge(stat_done, 2 * g + s + 1)
                    act.activation(rms[:, cols[s]], bank[4 + s][:, 0:HALF], ACT.Sqrt,
                                   bias=eps[:, 0:1], scale=1.0 / D).then_inc(rms_done, 1)

            def norm_hi(g):
                for k in range(2 * DC):
                    m, c = k % DC, slice(0, HALF) if k < DC else slice(HALF, SEQ)
                    act.wait_ge(u_done, 2 * DC * g + k + 1)
                    act.activation(n_hi[:, m, c], u[k % 3][:, 0:c.stop - c.start], ACT.Identity,
                                   bias=mod_b[:, m, 0:1]).then_inc(nhi_done, 1)
                act.wait_ge(us_step, 3 * g + 3)
                act.copy(n_hi[:, :, SEQ:NT], us[:]).then_inc(nhi_s_done, 1)

            def ffn(l, f):
                for p in range(3):
                    with act.Fori(0, PORT[p] // 2) as i:
                        for q in range(2):
                            if f == 0:
                                for k in range(2):
                                    a = 4 * i + 2 * q + k + l * ADA_IN * 4 + PBASE[p] * 2 + DEPTH * ADA_PRO * 4
                                    a2 = 2 * i + q + l * ADA_IN * 2 + PBASE[p] + DEPTH * ADA_PRO
                                    ada_hi(a, a2, k, 2)
                            for k in range(2):
                                split_hi(unit(l, f, p, 0) + 4 * i + 2 * q + k + LEAD,
                                         l * (LAYER_U // 2) + unit(0, f, p, 0) // 2 + 2 * i + q + 1, (2 * q + k + LEAD) % 4)
                            for s in range(2):
                                hp = half_pair(l, f, p, 2 * i + q, s)
                                if s == 0:
                                    act.wait_ge(gate_done, pair(l, f, p, 2 * i + q) + 1)
                                else:
                                    act.wait_ge(wslot_free, unit(l, f, p, 0) + 4 * i + 2 * q + 6)
                                act.wait_ge(gate_free, hp + 1)
                                act.activation(sil[s][:], bank[2 * s][:, 0:HALF], ACT.Silu).then_inc(sil_done, 1)
                    for m in range(DC):
                        k = 2 * PORT[p] + m
                        split_hi(unit(l, f, p, k) + LEAD, l * (LAYER_U // 2) + unit(0, f, p, k + LEAD) // 2, (k + LEAD) % 4)
                        if p == 2:
                            if m >= 1:
                                square(3 * l + 2 * f + 1, m - 1,
                                       lambda: act.wait_ge(x_done, out_tile(l, f, p, m - 1) + 2))
                square(3 * l + 2 * f + 1, DC - 1, lambda: act.wait_ge(x_done, out_tile(l, f, 2, DC - 1) + 2))


            def mix_act(l):
                def feed(k):
                    split_hi(l * LAYER_U + FFN_U + k + LEAD, l * (LAYER_U // 2) + (FFN_U + k + LEAD) // 2,
                             (k + LEAD) % 4)

                def tile_done(s, n, k):
                    if s == 0:
                        proj_mm.wait(act, l, n)
                    else:
                        act.wait_ge(wslot_free, l * LAYER_U + FFN_U + k + 5)

                def exp_decay(dst, src):
                    e_done.send(act.activation(dst, src, ACT.Exp, scale=1.0 / GATE_NORM))

                def query_exps(j):
                    scan_done.wait(act, l, j)
                    if j:
                        qk_ready.wait(act, l, 0)
                    exp_decay(e_b[:], gb[:, j, :])
                    dec.wait(act, l, 3 * j)
                    exp_decay(k_dec[:], k_dec[:])

                def key_exps(j):
                    dec.wait(act, l, 3 * j + 1)
                    exp_decay(k_sub[:], k_sub[:])
                    dec.wait(act, l, 3 * j + 2)
                    exp_decay(k_dec[:], k_dec[:])

                act.wait_ge(n_ready, 2 * DC * (3 * l + 1) + 2 * DC)
                act.wait_ge(ns_ready, 3 * l + 2)
                act.dma_start(scan_m[:], scanm).then_inc(scan_in, 16)
                act.dma_start(w_gk[:], gk2_in[bass.ds(l, 1)].rearrange("l r c -> (l r) c")).then_inc(scan_in, 16)
                act.dma_start(s_s[:], s0_in[bass.ds(2 * l, 1)].rearrange("l p i v -> (l p) i v")).then_inc(s_in, 16)
                feed(0)
                bank_of = {U_GQ: (2, 3), U_GQ + 1: (6, 7), U_GK: (4, 5), U_GK + 1: (0, 1)}
                for k in range(U_GQ, U_GOG):
                    feed(k)
                    dst, j = (gq, k - U_GQ) if k < U_GK else (gk, k - U_GK)
                    for s in range(2):
                        tile_done(s, k, k)
                        gqk_out.send(act.mul(dst[:, j, cols[s]], bank[bank_of[k][s]][:, 0:HALF],
                                             GK ** -0.5 if k < U_GK else 1.0))
                for h in range(GH):
                    feed(U_GOG + h)
                    for s in range(2):
                        tile_done(s, 5 + h, U_GOG + h)
                        b = ((2, 3), (6, 7), (4, 5), (0, 1))[h][s]
                        gog_out.send(act.activation(gog[:, h, cols[s]], bank[b][:, 0:HALF], ACT.Silu))
                feed(9)
                feed(10)
                zabs.wait(act, l, 0)
                soft_e.send(act.activation(soft[:], soft[:], ACT.Exp))
                soft_e.last(act, l)
                soft_e.send(act.activation(soft[:], soft[:], ACT.Ln, bias=ones[:, 0:1]))
                feed(11)
                feed(12)
                query_exps(0)
                feed(13)
                for c in range(QL):
                    if c:
                        feed(U_CQ + c)
                    for s in range(2):
                        tile_done(s, 9 + c, U_CQ + c)
                        b = ((3, 6), (7, 4), (5, 0))[c][s]
                        cq_out.send(act.copy(cq[:, c, cols[s]], bank[b][:, 0:HALF]))
                feed(U_CKV)
                key_exps(0)
                feed(U_CKV + 1)
                act.wait_ge(wslot_free, l * LAYER_U + FFN_U + U_CKV + 1 + 5)
                for c in range(QL + KL):
                    if c < QL:
                        cq_out.wait(act, l, 5)
                        src = cq[:, c, :]
                    else:
                        ckv_ev.wait(act, l, 3)
                        src = ckv[:, c - QL, :]
                    if c in (2, 3):
                        lat_mm_sq.wait(act, l, c - 2)
                    elif c == 4:
                        lat_mm.wait(act, l, 1)
                    lsq.send(act.activation(lat_sq[c % 2][:], src, ACT.Square))
                for i in range(4):
                    b = bank[(1, 2, 3, 6)[i]][:, 0:HALF]
                    lat_mm.wait(act, l, i)
                    lrs.send(act.activation(b, b, ACT.Ln, bias=eps[:, 0:1], scale=1.0 / ((QL if i < 2 else KL) * P)))
                for i in range(4):
                    b = bank[(1, 2, 3, 6)[i]][:, 0:HALF]
                    lrs.wait(act, l, i)
                    lrs.send(act.activation(b, b, ACT.Exp, scale=-0.5))
                feed(18)
                feed(19)
                for c in range(QL):
                    lat_n.wait(act, l, 2 * c + 1)
                    chi_out.send(act.copy(qn_hi[:, c, :], cq[:, c, :]))
                for c in range(KL):
                    lat_n.wait(act, l, 6 + 2 * c + 1)
                    chi_out.send(act.copy(c_hi[:, c, :], ckv[:, c, :]))
                lat_n.wait(act, l, 9)
                act.dma_start(ckv_out[bass.ds(l, 1)].rearrange("l p c n -> (l p) c n"), ckv[:]).then_inc(kv_st, 16)
                for j in range(2):
                    g = GLA_BANKS[j]
                    kt, (kts, ko) = bank[g["KT"]], g["KTS"]
                    kdt_mm.wait(act, l, 2 * j)
                    zeroed.wait(act, l, 0)
                    if j:
                        ds_mm.wait(act, l, 1)
                    src = kt[:, :].rearrange("p (t k) -> p t k", k=P)
                    kdt_out.send(act.copy(kd_t[0:CH, :, 0, :], src[0:CH]))
                    kdt_out.send(act.copy(kd_t[CH:P, :, 1, :], src[CH:P]))
                    if j == 0:
                        query_exps(1)
                        key_exps(1)
                    for i, (c0, c1) in enumerate(OSPAN):
                        o_mm.wait(act, l, 3 * j + i)
                        if j:
                            gla_fin.wait(act, l, i)
                        osq.send(act.activation(o_sq[:, c0:c1], bank[g["O"][i]][:, 0:c1 - c0], ACT.Square))
                    for i, (c0, c1) in enumerate(OSPAN):
                        ost_mm.wait(act, l, 3 * j + i)
                        if j:
                            o_mul.wait(act, l, i)
                        orn.send(act.activation(o_rs[:, c0:c1], bank[g["ST"][i]][:, 0:c1 - c0], ACT.Ln,
                                                bias=eps[:, 0:1], scale=1.0 / GV))
                    for i, (c0, c1) in enumerate(OSPAN):
                        orn.wait(act, l, 6 * j + i)
                        orn.send(act.activation(o_rs[:, c0:c1], o_rs[:, c0:c1], ACT.Exp, scale=-0.5))
                    ds_out.wait(act, l, 4 * j + 3)
                    at = bass.ds(2 * l + j, 1)
                    act.dma_start(glap_out[at].rearrange("l p v -> (l p) v"), s_p[:, NCH - 1, :]).then_inc(gla_st, 16)
                    act.dma_start(glas_out[at].rearrange("l p i v -> (l p) i v"), s_s[:]).then_inc(gla_st, 16)
                    if j == 0:
                        act.wait_ge(gla_st, 64 * l + 32)
                        act.dma_start(s_s[:], s0_in[bass.ds(2 * l + 1, 1)].rearrange("l p i v -> (l p) i v"))\
                            .then_inc(s_in, 16)
                ds_out.wait(act, l, 7)
                qk_ready.wait(act, l, 7)
                ds_mm.wait(act, l, 7)
                kdt_mm.wait(act, l, 3)
                att_mm.wait(act, l, 3)
                act.dma_start(cs[:], cs_in).then_inc(cs_ld, 16)
                for h in range(MH):
                    if h % 2 == 0:
                        feed(U_UQ + 2 + h // 2) if h < 4 else None
                    for s in range(2):
                        if h % 2 and s:
                            act.wait_ge(wslot_free, l * LAYER_U + FFN_U + U_UQ + h // 2 + 5)
                        else:
                            q_mm.wait(act, l, 3 * (h // 2) + 2 * (h % 2) + s)
                        if h == 0 and s == 0:
                            o_mm.wait(act, l, 5)
                        qh_out.send(act.mul(q_h[0:NOPE, h, cols[s]], bank[QBANKS[h][s]][0:NOPE, 0:HALF], MLA_SCALE))
                feed(22)
                for hp in range(4):
                    if hp < 3:
                        k_mm.wait(act, l, hp)
                    else:
                        act.wait_ge(wslot_free, l * LAYER_U + FFN_U + U_UK + 5)
                    b = bank[(1, 4, 2, 3)[hp]]
                    kh_out.send(act.copy(k_h[0:NOPE, 2 * hp, :], b[0:NOPE, :]))
                    kh_out.send(act.copy(k_h[0:NOPE, 2 * hp + 1, :], b[NOPE:P, :]))
                feed(23)
                feed(24)
                feed(25)
                kpe_done.wait(act, l, 1)
                act.dma_start(kpe_out[bass.ds(l, 1)].rearrange("l r n -> (l r) n"), kg[NOPE:96, :]).then_inc(kv_st, 16)
                kh_out.send(act.copy(k_h[NOPE:96, :, :], kg[NOPE:96, 0:SEQ].unsqueeze(1).broadcast_to((ROPE, MH, SEQ))))
                act.wait_ge(wslot_free, l * LAYER_U + FFN_U + U_UV + 5)
                gla_fin.wait(act, l, 5)
                for h in range(GH):
                    ohi_out.send(act.copy(o_hi[:, h, :], gog[:, h, :]))
                olo.wait(act, l, 3)
                act.dma_start(uk_t[:], ukT[bass.ds(l, 1)].rearrange("l r h c -> (l r) h c")).then_inc(uk_in, 16)

                def load_past(i):
                    n = i % NPB
                    if i >= NPB:
                        ol_mm.wait(act, l, i - NPB)
                    at = l * NDEC + i
                    for dst, src in ((pk_t[n][:], past_kT[bass.ds(at, 1)].rearrange("a p c n -> (a p) c n")),
                                     (pv[n][:], past_v[bass.ds(at, 1)].rearrange("a p c n -> (a p) c n")),
                                     (pp_t[n][NOPE:96, :], past_pe[bass.ds(at, 1)].rearrange("a p n -> (a p) n"))):
                        act.dma_start(dst, src).then_inc(past_in[n], 16)

                act.wait_ge(gla_st, 64 * l + 64)
                for i in range(NPB):
                    load_past(i)
                rope_done.wait(act, l, 15)
                act.dma_start(w_uv[:], wuv_in[bass.ds(l, 1)].rearrange("l p c n -> (l p) c n")).then_inc(uv_in, 16)
                for n in range(4):
                    qa_mm.wait(act, l, n)
                    if n == 0:
                        gla_fin.wait(act, l, 5)
                    c, hh = n // 2, n % 2
                    qa_out.send(act.copy(q_abs[:, c, :, 4 * hh * DSEQ:(4 * hh + 4) * DSEQ]
                                         .rearrange("p i (h t) -> p h i t", t=DSEQ),
                                         bank[(1, 4, 2, 3)[n]][:, :].rearrange("p (h i t) -> p h i t", h=4, t=DSEQ)))
                for it in range(40 + 6):
                    if it < 40:
                        smp = it < NDEC
                        n, b = it % 4, bank[SBANKS[it % 4]]
                        p_max.wait(act, l, it)
                        if smp:
                            i = it
                            if it >= 4:
                                t_mm.wait(act, l, it - 4)
                            dst = p_s[n][:, 0:PAST]
                            p_exp_a.send(act.activation(dst, b[:, 0:PAST], ACT.Exp, bias=mx[:, n:n + 1],
                                                        accum_out=psums[:, n:n + 1]))
                            p_exp.send(act.activation(p_s[n][:, PAST + DSEQ * i:PAST + DSEQ * (i + 1)],
                                                      b[:, PAST:PAST + DSEQ], ACT.Exp, bias=mx[:, n:n + 1],
                                                      accum_out=psum2[:, n:n + 1]))
                        else:
                            w = P * ((it - NDEC) % 4 + 1)
                            if it >= NDEC + 4:
                                t_mm.wait(act, l, it - 4)
                            if it in (NDEC, NDEC + 2):
                                ol_mm.wait(act, l, 5 if it == NDEC else 6)
                            p_exp.send(act.activation(p_p[n][:, 0:w], b[:, 0:w], ACT.Exp, bias=mx[:, n:n + 1],
                                                      accum_out=psums[:, n:n + 1]))
                    if 2 <= it < 42:
                        jt = it - 2
                        b = bank[TBANKS[jt % 2]]
                        t_mm.wait(act, l, jt)
                        if jt < NDEC:
                            if jt >= 2:
                                ol_mm.wait(act, l, jt - 2)
                            pt_out.send(act.copy(pt_s[jt % 2][:], b[:, 0:3 * P].rearrange("p (c t) -> p c t", t=P)))
                        else:
                            qt = (jt - NDEC) % 4
                            if jt >= NDEC + 3:
                                pv_mm.wait(act, l, jt - NDEC - 3)
                            pt_out.send(act.copy(pt_p[jt % 3][:, 0:qt + 1, :],
                                                 b[:, 0:P * (qt + 1)].rearrange("p (c t) -> p c t", t=P)))
                    if NPB <= it + 1 < NDEC:
                        load_past(it + 1)
                    if it == NDEC + 7:
                        uv_mm.wait(act, l, 0)
                        ohi_out.send(act.copy(o_hi[:, 4:8, SEQ:NT], bank[1][:, :].rearrange("p (c t) -> p c t", t=P)))
                    hp = (it - 5 - NDEC - 7) // 8
                    if it == NDEC + 8 * hp + 12 and 0 <= hp < 4:
                        pv_mm.wait(act, l, 8 * hp + 7)
                        ohi_out.send(act.copy(o_hi[:, 4 + hp, 0:SEQ], bank[(4, 1)[hp % 2]][:, :]))
                for m in range(DC):
                    if m >= 1:
                        square(3 * l + 2, m - 1, lambda: act.wait_ge(x_done, l * OUT_T + 3 * DC + m - 1 + 2))
                    if m < 6:
                        feed(26 + m)
                square(3 * l + 2, DC - 1, lambda: act.wait_ge(x_done, l * OUT_T + 3 * DC + DC - 1 + 2))

            act.sem_inc(warm_done, 1)
            act.wait_ge(const_done, 1)
            act.wait_ge(const_in, 80)
            act.activation(c_sil[:], c_in[:], ACT.Silu).then_inc(csil_done, 1)
            for k in range(8):
                ada_hi(k, k // 4, k % 4, 4)
            for m in range(DC):
                square(0, m, lambda: act.wait_ge(x_in, 16))
            with act.Fori(2, DEPTH * ADA_PRO) as t:
                for k in range(4):
                    ada_hi(4 * t + k, t, k, 4)
            split_hi(0, 0, 0)
            split_hi(1, 0, 1)
            with act.Fori(0, DEPTH) as l:
                norm_rstd(3 * l)
                norm_hi(3 * l)
                ffn(l, 0)
                norm_rstd(3 * l + 1)
                norm_hi(3 * l + 1)
                mix_act(l)
                norm_rstd(3 * l + 2)
                norm_hi(3 * l + 2)
                ffn(l, 1)
            norm_rstd(3 * DEPTH)

        @block.tensor
        def _(pe):
            pe.sem_inc(wslot_free, 4)
            pe.sem_inc(aslot_free, 4)

            def mm3(out, w, c, r_hi, r_lo, first, last):
                pe.matmul(out, w_hi[w][:, c, :], r_hi, start=first, stop=False)
                pe.matmul(out, w_hi[w][:, c, :], r_lo, start=False, stop=False)
                return pe.matmul(out, w_lo[w][:, c, :], r_hi, start=False, stop=last)

            def ada_unit(at, k, s, dst=ADA_ACC):
                pe.wait_ge(alo_done, at + 5)
                for c in range(2):
                    for w in (a_hi, a_lo):
                        mm = pe.matmul(dst[:, :], c_st[:, 2 * k + c, :], w[s][:, c, :],
                                       start=(k == 0 and c == 0 and w is a_hi),
                                       stop=(k == 3 and c == 1 and w is a_lo))
                mm.then_inc(aslot_free, 1)

            def ada_first(t):
                pe.wait_ge(ev_done, t + 1)

            def ada_select(t):
                pe.wait_ge(ev_done, t + 2)
                for j in range(4):
                    mm = pe.matmul(ADA_SEL[:, j * NS:(j + 1) * NS], ev[:, j * P:(j + 1) * P], sel[:],
                                   start=True, stop=True)
                mm.then_inc(sel_done, 1)

            def stats(g):
                pe.wait_ge(acc_done, 7 * g + 7)
                for s in range(2):
                    pe.matmul(bank[4 + s][:, 0:HALF], ones[:], acc[:, cols[s]], start=True, stop=True)\
                        .then_inc(stat_done, 1)

            def tokens_in(g, s, c):
                if s == 1 and c == 0:
                    pe.wait_ge(ns_ready, g + 1)
                pe.wait_ge(n_ready, 2 * DC * g + s * DC + c + 1)

            def ffn(l, f):
                g = 3 * l + 2 * f
                for p in range(3):
                    def body(i, g=None):
                        for q in range(2):
                            t = DEPTH * ADA_PRO + l * ADA_IN + PBASE[p] // 2 + i
                            for s in range(2):
                                pe.wait_ge(gate_free, half_pair(l, f, p, 2 * i + q, s) + 1)
                                if q == 0 and s == 1:
                                    pe.wait_ge(y_free, 4 + 2 * out_tile(l, f, p, 0))
                                for w in range(2):
                                    slot = 2 * q + w
                                    if s == 0:
                                        pe.wait_ge(wlo_done, unit(l, f, p, 0) + 4 * i + 2 * q + w + 1)
                                    for c in range(DC):
                                        if g is not None:
                                            tokens_in(g, s, c)
                                        mm = mm3(bank[2 * s + w][:, 0:HALF], slot, c, n_hi[:, c, cols[s]],
                                                 n_lo[:, c, cols[s]], c == 0, c == DC - 1)
                                    if s == 1:
                                        mm.then_inc(wslot_free, 1)
                                    elif w == 1:
                                        mm.then_inc(gate_done, 1)
                                if s == 1 - q and f == 0:
                                    if q == 0:
                                        ada_first(t)
                                    for k in range(2):
                                        ada_unit(4 * t + 2 * q + k, 2 * q + k, k)
                            if f == 0 and q == 1:
                                ada_select(t)
                    if p == 0:
                        body(0, g)
                    with pe.Fori(int(p == 0), PORT[p] // 2) as i:
                        body(i)
                    for m in range(DC):
                        slot = (2 * PORT[p] + m) % 4
                        pe.wait_ge(wlo_done, unit(l, f, p, 2 * PORT[p] + m) + 1)
                        for s in range(2):
                            pe.wait_ge(y_free, 2 * out_tile(l, f, p, m) + s + 1)
                            dst = bank[4 + s] if m % 2 == 0 else bank[2 + s]
                            for c in range(PORT[p]):
                                if m == 0 and c in (0, PORT[p] - 1):
                                    cc = PORT[p] - 2 if c == 0 else PORT[p] - 1
                                    pe.wait_ge(h_ready, half_pair(l, f, p, cc, s) + 3)
                                mm = mm3(dst[:, 0:HALF], slot, c, h_hi[:, c, cols[s]], h_lo[:, c, cols[s]],
                                         c == 0, c == PORT[p] - 1)
                            mm.then_inc(wslot_free if s else out_done, 1)


            def mix_pe(l):
                def unit_in(k):
                    pe.wait_ge(wlo_done, l * LAYER_U + FFN_U + k + 1)

                def tile(k, n, chunks, first, r_hi, r_lo, banks, waits, s0, fresh=False):
                    slot = k % 4
                    for s in range(2):
                        for sg, w in waits[s]:
                            sg.wait(pe, l, w)
                        for c in range(chunks):
                            if fresh:
                                tokens_in(3 * l + 1, s, c)
                            mm = mm3(bank[banks[s]][:, 0:HALF], slot, first + c, r_hi[:, c, cols[s]], r_lo[:, c, cols[s]],
                                     c == 0, c == chunks - 1)
                        if s == 1 and first + chunks == n:
                            mm.then_inc(wslot_free, 1)
                        else:
                            s0.send(mm)

                def proj(k, banks, waits):
                    unit_in(k)
                    tile(k, DC, DC, 0, n_hi, n_lo, banks, waits, proj_mm, k == U_S)

                no = ((), ())
                proj(U_S, (0, 1), no)
                proj(U_GQ, (2, 3), no)
                proj(U_GQ + 1, (6, 7), no)
                proj(U_GK, (4, 5), no)
                proj(U_GK + 1, (0, 1), (((s_out, 0),), ((s_out, 1),)))
                proj(U_GOG, (2, 3), (((gqk_out, 0),), ((gqk_out, 1),)))
                proj(U_GOG + 1, (6, 7), (((gqk_out, 2),), ((gqk_out, 3),)))
                proj(U_GOG + 2, (4, 5), (((gqk_out, 4),), ((gqk_out, 5),)))
                proj(U_GOG + 3, (0, 1), (((gqk_out, 6),), ((gqk_out, 7),)))
                pe.wait_ge(scan_in, 32 * l + 32)
                for j in range(2):
                    for s in range(2):
                        gog_out.wait(pe, l, 2 * j + s)
                        z_mm.send(pe.matmul(bank[((2, 3), (6, 7))[j][s]][:, 0:HALF], w_gk[:, j * P:(j + 1) * P],
                                            kg[0:GR, cols[s]], start=True, stop=True))
                for q in range(4):
                    unit_in(U_GV + q)
                    slot = (U_GV + q) % 4
                    for t in range(5):
                        if q == 0:
                            sg, w = ((gog_out, 4), (gog_out, 5), (gog_out, 6), (gog_out, 7), (z_out, 0))[t]
                            sg.wait(pe, l, w)
                        out = bank[(4, 5, 0, 1, 2)[t]]
                        tok = slice(t * P, (t + 1) * P)
                        for c in range(2):
                            wh = w_hi[slot][:, 4 * c:4 * c + 4, :]
                            wl = w_lo[slot][:, 4 * c:4 * c + 4, :]
                            pe.matmul(out[:, :], n_hi[:, 2 * q + c, tok], wh, start=(q == 0 and c == 0), stop=False)
                            pe.matmul(out[:, :], n_hi[:, 2 * q + c, tok], wl, start=False, stop=False)
                            mm = pe.matmul(out[:, :], n_lo[:, 2 * q + c, tok], wh, start=False,
                                           stop=(q == 3 and c == 1))
                        if t == 4:
                            mm.then_inc(wslot_free, 1)
                        elif q == 3:
                            gv_mm.send(mm)
                proj(U_CQ, (3, 6), (((z_out, 1),), ((z_out, 2),)))
                proj(U_CQ + 1, (7, 4), (((z_out, 3),), ((gv_out, 0),)))
                proj(U_CQ + 2, (5, 0), (((gv_out, 1),), ((gv_out, 2),)))
                proj(U_CKV, (1, 2), (((gv_out, 3),), ((gv_out, 4),)))
                proj(U_CKV + 1, (3, 6), (((cq_out, 0),), ((cq_out, 1),)))

                def gla_att(j):
                    b = GLA_BANKS[j]
                    qk_ready.wait(pe, l, 4 * j + 1)
                    qk_ready.wait(pe, l, 4 * j + 2)
                    zeroed.wait(pe, l, 0)
                    if j == 0:
                        cq_out.wait(pe, l, 4)
                    else:
                        kdt_out.wait(pe, l, 1)
                        ds_out.wait(pe, l, 3)
                    for n in range(NCH):
                        for i in range(NSUB):
                            ln = SUB * (i + 1)
                            at = NCH * SUB * i * (i + 1) // 2 + n * ln
                            r0, c0 = CH * (n % 2), (n // 2) * P + i * SUB
                            dst = bank[b["A"]][r0:r0 + ln, :].rearrange("p (n h t) -> p n h t", n=4, h=2)[
                                :, n // 2, :, i * SUB:(i + 1) * SUB]
                            t0 = n * CH + i * SUB
                            mm = pe.matmul(dst, k_sub[:, at:at + ln], q_sub[:, :, t0:t0 + SUB], start=True, stop=True)
                    att_mm.send(mm)
                    att_mm.send(pe.matmul(bank[b["AS"]][:, 0:2 * P], k_sub[:, KHAT[NSUB]:KHAT[NSUB] + P],
                                          q_sub[:, :, SEQ:NT], start=True, stop=True))

                def gla_keys(j):
                    b = GLA_BANKS[j]
                    qk_ready.wait(pe, l, 4 * j + 3)
                    if j == 0:
                        cq_out.wait(pe, l, 5)
                    else:
                        orn.wait(pe, l, 0)
                    for t in range(4):
                        mm = pe.transpose(bank[b["KT"]][:, t * P:(t + 1) * P], k_dec[:, t * P:(t + 1) * P], ident[:])
                    kdt_mm.send(mm)
                    k, o = b["KTS"]
                    if j:
                        o_mul.wait(pe, l, 0)
                    kdt_mm.send(pe.transpose(bank[k][:, o:o + P], k_dec[:, SEQ:NT], ident[:]))

                def gla_states(j):
                    b = GLA_BANKS[j]
                    kdt_out.wait(pe, l, 2 * j + 1)
                    gv_out.wait(pe, l, 4)
                    for q in range(2):
                        if j == 0:
                            lat_n.wait(pe, l, (3, 5)[q])
                        else:
                            orn.wait(pe, l, (1, 2)[q])
                        for n in range(4 * q, 4 * q + 4):
                            for hh in range(2):
                                h = 2 * j + hh
                                mm = pe.matmul(bank[b["DS"][q]][GK * hh:GK * hh + GK, (n % 4) * GV:(n % 4 + 1) * GV],
                                               kd_t[:, n // 2, n % 2, GK * hh:GK * hh + GK],
                                               v_g[:, n // 2, h * GV:(h + 1) * GV], start=True, stop=True)
                        ds_mm.send(mm)
                    kds_out.wait(pe, l, j)
                    for q in range(2):
                        if j == 0:
                            lat_n.wait(pe, l, 9)
                        elif q == 1:
                            o_mul.wait(pe, l, 0)
                        for i in range(4 * q, 4 * q + 4):
                            for hh in range(2):
                                h = 2 * j + hh
                                mm = pe.matmul(bank[b["DSS"][q]][GK * hh:GK * hh + GK, (i % 4) * GV:(i % 4 + 1) * GV],
                                               kd_s[:, i, GK * hh:GK * hh + GK], v_g[:, 4, h * GV:(h + 1) * GV],
                                               start=True, stop=True)
                        ds_mm.send(mm)

                def gla_out(j):
                    b = GLA_BANKS[j]
                    qk_ready.wait(pe, l, 4 * j)
                    for q in range(2):
                        att_out.wait(pe, l, 2 * j)
                        ds_out.wait(pe, l, 4 * j + q)
                        if j:
                            o_mul.wait(pe, l, 1 + q)
                        out = bank[b["O"][q]]
                        both = out[:, :].rearrange("p (h t) -> p h t", h=2)
                        first = True
                        for n in (2 * q, 2 * q + 1):
                            for hh in range(2):
                                h = 2 * j + hh
                                c0 = (n % 2) * P
                                pe.matmul(both[:, hh, c0:c0 + P], v_g[:, n, h * GV:(h + 1) * GV], att[:, n, hh, :],
                                          start=first, stop=False, skip_group_check=True)
                                first = False
                        for n in range(max(4 * q, 1), 4 * q + 4):
                            c0 = (n % 4) * CH
                            mm = pe.matmul(both[:, :, c0:c0 + CH], s_p[:, n - 1, :], q_blk[:, :, n * CH:(n + 1) * CH],
                                           start=False, stop=True, skip_group_check=True)
                        o_mm.send(mm)
                    att_out.wait(pe, l, 2 * j + 1)
                    pe.wait_ge(s_in, 32 * l + 16 * j + 16)
                    if j == 0:
                        kds_out.wait(pe, l, 0)
                    both = bank[b["O"][2]][:, 0:2 * P].rearrange("p (h t) -> p h t", h=2)
                    for hh in range(2):
                        h = 2 * j + hh
                        pe.matmul(both[:, hh, :], v_g[:, 4, h * GV:(h + 1) * GV], att[:, 4, hh, :],
                                  start=(hh == 0), stop=False, skip_group_check=True)
                    for i in range(NDEC):
                        mm = pe.matmul(both[:, :, i * DSEQ:(i + 1) * DSEQ], s_s[:, i, :],
                                       q_blk[:, :, SEQ + i * DSEQ:SEQ + (i + 1) * DSEQ],
                                       start=False, stop=True, skip_group_check=True)
                    o_mm.send(mm)

                def gla_stats(j):
                    b = GLA_BANKS[j]
                    for i, (c0, c1) in enumerate(OSPAN):
                        osq.wait(pe, l, 3 * j + i)
                        if j == 0:
                            ds_out.wait(pe, l, (0, 1, 2)[i])
                        else:
                            ds_out.wait(pe, l, (4, 5, 5)[i])
                            att_out.wait(pe, l, 3)
                            kds_out.wait(pe, l, 1)
                        ost_mm.send(pe.matmul(bank[b["ST"][i]][:, 0:c1 - c0], ones[:], o_sq[:, c0:c1],
                                              start=True, stop=True))

                for c in range(QL + KL):
                    lsq.wait(pe, l, c)
                    if c == 0:
                        ckv_ev.wait(pe, l, 3)
                    first, last, b0 = (c == 0, c == QL - 1, (1, 2)) if c < QL else (c == QL, c == QL + KL - 1, (3, 6))
                    for s in range(2):
                        mm = pe.matmul(bank[b0[s]][:, 0:HALF], ones[:], lat_sq[c % 2][:, cols[s]], start=first, stop=last)
                        if last:
                            lat_mm.send(mm)
                    if c < 2:
                        lat_mm_sq.send(mm)
                for j in range(2):
                    gla_att(j)
                    gla_keys(j)
                    gla_states(j)
                    gla_out(j)
                    gla_stats(j)

                for h in range(MH):
                    k = U_UQ + h // 2
                    if h % 2 == 0:
                        unit_in(k)
                    if h == 0:
                        clo.wait(pe, l, 2)
                    w = {0: ((ds_out, 6), (ds_out, 7)), 1: ((orn, 6), (orn, 7)), 2: ((orn, 8), (o_mul, 3)),
                         3: ((o_mul, 4), (o_mul, 5))}.get(h)
                    if w:
                        waits = ((w[0],), (w[1],))
                    else:
                        waits = tuple(((qh_out, 2 * (h - 4) + s), (rope_done, 2 * (h - 4) + s)) for s in range(2))
                    tile(k, 6, QL, 3 * (h % 2), qn_hi, qn_lo, QBANKS[h], waits, q_mm)
                unit_in(U_UK)
                clo.wait(pe, l, 4)
                for hp in range(4):
                    i = (8, 9, 10, 11)[hp]
                    qh_out.wait(pe, l, i)
                    rope_done.wait(pe, l, i)
                    for c in range(KL):
                        mm = mm3(bank[(1, 4, 2, 3)[hp]][:, :], U_UK % 4, KL * hp + c, c_hi[:, c, 0:SEQ], c_lo[:, c, 0:SEQ],
                                 c == 0, c == KL - 1)
                    mm.then_inc(wslot_free, 1) if hp == 3 else k_mm.send(mm)
                unit_in(U_UV)
                slot = U_UV % 4
                for t in range(4):
                    i = (12, 13, 14, 15)[t]
                    qh_out.wait(pe, l, i)
                    rope_done.wait(pe, l, i)
                    out = bank[(6, 5, 7, 0)[t]]
                    for c in range(KL):
                        wh = w_hi[slot][:, 4 * c:4 * c + 4, :]
                        wl = w_lo[slot][:, 4 * c:4 * c + 4, :]
                        tok = slice(t * P, (t + 1) * P)
                        pe.matmul(out[:, :], c_hi[:, c, tok], wh, start=(c == 0), stop=False)
                        pe.matmul(out[:, :], c_hi[:, c, tok], wl, start=False, stop=False)
                        mm = pe.matmul(out[:, :], c_lo[:, c, tok], wh, start=False, stop=(c == KL - 1))
                    mm.then_inc(wslot_free, 1) if t == 3 else v_mm.send(mm)
                vm_out.wait(pe, l, 0)
                for c in range(KL):
                    mm = pe.transpose(bank[6][:, c * P:(c + 1) * P], ckv[:, c, SEQ:NT], ident[:])
                cn_mm.send(mm)
                pe.wait_ge(uk_in, 16 * l + 16)
                for n in range(4):
                    kh_out.wait(pe, l, 2 * n + 1)
                    c, hh = n // 2, n % 2
                    for h in range(4 * hh, 4 * hh + 4):
                        mm = pe.matmul(bank[(1, 4, 2, 3)[n]][:, (h % 4) * P:(h % 4 + 1) * P],
                                       uk_t[:, h, c * P:(c + 1) * P], q_h[0:NOPE, h, SEQ:NT], start=True, stop=True)
                    qa_mm.send(mm)

                def scores(it):
                    b = bank[SBANKS[it % 4]]
                    if it >= 4:
                        p_exp.wait(pe, l, it - 4)
                    else:
                        sg, w = ((cn_out, 0), (vm_out, 1), (qa_out, 2), (qa_out, 3))[it]
                        sg.wait(pe, l, w)
                        qa_out.wait(pe, l, 3)
                    if it < NDEC:
                        n, i = it % NPB, it
                        rounds = len(range(n, NDEC, NPB))
                        pe.wait_ge(past_in[n], 48 * (rounds * l + i // NPB + 1))
                        new = slice(SEQ + DSEQ * i, SEQ + DSEQ * (i + 1))
                        for c in range(KL):
                            q = q_abs[:, c, i, :]
                            pe.matmul(b[:, 0:PAST], q, pk_t[n][:, c, :], start=(c == 0), stop=False,
                                      skip_group_check=True)
                            pe.matmul(b[:, PAST:PAST + DSEQ], q, ckv[:, c, new], start=False, stop=False,
                                      skip_group_check=True)
                        qpe_out.wait(pe, l, 0)
                        q = q_pe[NOPE:96, i, :]
                        pe.matmul(b[:, 0:PAST], q, pp_t[n][NOPE:96, :], start=False, stop=True, skip_group_check=True)
                        s_mm.send(pe.matmul(b[:, PAST:PAST + DSEQ], q, kg[NOPE:96, new], start=False, stop=True,
                                            skip_group_check=True))
                    else:
                        h, qt = (it - NDEC) // 4, (it - NDEC) % 4
                        if it == NDEC:
                            kh_out.wait(pe, l, 8)
                        w = P * (qt + 1)
                        pe.matmul(b[:, 0:w], q_h[:, h, qt * P:(qt + 1) * P], k_h[:, h, 0:w], start=True, stop=False,
                                  skip_group_check=True)
                        s_mm.send(pe.matmul(b[:, w - CH:w], mrow[0:1, 0:P], mrow[0:1, P:P + CH], start=False, stop=True,
                                            skip_group_check=True))

                def transposes(it):
                    b = bank[TBANKS[it % 2]]
                    p_norm.wait(pe, l, it)
                    if it >= 2:
                        pt_out.wait(pe, l, it - 2)
                    else:
                        vm_out.wait(pe, l, 2 + it)
                    src, n = (p_s[it % 4], 3) if it < NDEC else (p_p[it % 4], (it - NDEC) % 4 + 1)
                    for c in range(n):
                        mm = pe.transpose(b[:, c * P:(c + 1) * P], src[:, c * P:(c + 1) * P], ident[:])
                    t_mm.send(mm)

                def values(it):
                    pt_out.wait(pe, l, it)
                    if it < NDEC:
                        b = bank[(1, 4)[it % 2]]
                        if it >= 2:
                            ol_out.wait(pe, l, it - 2)
                        else:
                            qa_out.wait(pe, l, it)
                            cn_out.wait(pe, l, 0)
                        for c in range(KL):
                            for k in range(3):
                                w = pv[it % NPB][:, k, c * P:(c + 1) * P] if k < 2 else cn_t[:, c * P:(c + 1) * P]
                                mm = pe.matmul(b[:, c * P:(c + 1) * P], w, pt_s[it % 2][:, k, :],
                                               start=(k == 0), stop=(k == 2))
                        ol_mm.send(mm)
                        return
                    h, qt = (it - NDEC) // 4, (it - NDEC) % 4
                    hp, r0 = h // 2, MV * (h % 2)
                    if h % 2 == 0 and qt == 0:
                        sg, w = ((ol_out, 7), (olo, 4), (olo, 5), (olo, 6))[hp]
                        sg.wait(pe, l, w)
                    for k in range(qt + 1):
                        mm = pe.matmul(bank[(4, 1)[hp % 2]][r0:r0 + MV, qt * P:(qt + 1) * P],
                                       v_m[:, k, h * MV:(h + 1) * MV], pt_p[it % 3][:, k, :], start=(k == 0), stop=(k == qt))
                    pv_mm.send(mm)
                    return mm

                for it in range(40 + 4):
                    if 3 <= it < 43:
                        transposes(it - 3)
                    if it >= 4:
                        values(it - 4)
                    if it < 40:
                        scores(it)
                    if it == NDEC + 5:
                        ol_out.wait(pe, l, 7)
                        pe.wait_ge(uv_in, 16 * l + 16)
                        for h in range(MH):
                            for c in range(KL):
                                mm = pe.matmul(bank[1][MV * (h % 2):MV * (h % 2) + MV, (h // 2) * P:(h // 2 + 1) * P],
                                               w_uv[:, c, h * MV:(h + 1) * MV], o_lat[:, c, h, :],
                                               start=(c == 0), stop=(c == KL - 1))
                        uv_mm.send(mm)
                for m in range(DC):
                    unit_in(U_OUT + m)
                    if m == 0:
                        olo.wait(pe, l, 8)
                        p_exp.wait(pe, l, 39)
                    for s in range(2):
                        at = l * OUT_T + 3 * DC + m
                        pe.wait_ge(y_free, 2 * at + s + 1)
                        dst = bank[4 + s] if m % 2 == 0 else bank[2 + s]
                        for c in range(DC):
                            mm = mm3(dst[:, 0:HALF], (U_OUT + m) % 4, c, o_hi[:, c, cols[s]], o_lo[:, c, cols[s]],
                                     c == 0, c == DC - 1)
                        mm.then_inc(wslot_free if s else out_done, 1)

            pe.wait_ge(const_done, 1)
            pe.wait_ge(const_in, 80)
            pe.wait_ge(cst_done, 3)

            def ada_pair(i):
                for n in range(DEPTH):
                    t = DEPTH * i + n
                    for k in range(4):
                        ada_unit(4 * t + k, k, k, ADA_FIRST[n])
                        if k == 1 and not (n == 0 and isinstance(i, int)):
                            ada_select(t - 1)

            ada_pair(0)
            with pe.Fori(1, ADA_PRO) as i:
                ada_pair(i)
            ada_select(DEPTH * ADA_PRO - 1)
            pe.wait_ge(cst_in, 16 * 6)
            stats(0)
            with pe.Fori(0, DEPTH) as l:
                ffn(l, 0)
                stats(3 * l + 1)
                mix_pe(l)
                stats(3 * l + 2)
                ffn(l, 1)
                stats(3 * l + 3)

        @block.vector
        def _(dve):
            dve.sem_inc(alo_done, 4)
            dve.sem_inc(gate_free, 2)
            dve.sem_inc(h_ready, 2)
            dve.sem_inc(y_free, 4)
            dve.sem_inc(x_done, 1)
            dve.sem_inc(ev_done, 1)

            def ada_lo(at, s):
                dve.wait_ge(ahi_done, at + 1)
                dve.tensor_tensor(a_lo[s][:], araw[s][:].rearrange("p (c m) -> p c m", m=512),
                                  a_hi[s][:].bitcast(F32), ALU.subtract).then_inc(alo_done, 1)

            def ada_evict(t, src=ADA_ACC):
                dve.wait_ge(aslot_free, 4 * t + 8)
                dve.tensor_copy(ev[:], src[0:2 * NS, :]).then_inc(ev_done, 1)

            def ada_bias(t, l, f4):
                dve.wait_ge(sel_done, t + 1)
                dve.tensor_tensor(mods[:, l, f4, :], ADA_SEL[:, 0:4 * NS].rearrange("p (j n) -> p j n", n=NS),
                                  b_ada[:, l, f4].unsqueeze(2).broadcast_to((P, 4, NS)), ALU.add)\
                    .then_inc(mod_done, 1)

            def root(g, s):
                dve.wait_ge(rms_done, 2 * g + s + 1)
                dve.reciprocal(rstd[:, cols[s]], rms[:, cols[s]]).then_inc(rstd_done, 1)

            def norm_apply(l, k, ready):
                g = 3 * l + k
                dve.wait_ge(mod_done, ready)
                dve.scalar_tensor_tensor(out=mod_a[:], in0=mods[:, l, 24 * k + 8:24 * k + 16, :], scalar=1.0,
                                         in1=ln_g[:, l, k, :].unsqueeze(2).broadcast_to((P, DC, NS)),
                                         op0=ALU.add, op1=ALU.mult).then_inc(mab_done, 1)
                dve.tensor_copy(mod_b[:], mods[:, l, 24 * k:24 * k + 8, :]).then_inc(mab_done, 1)
                dve.tensor_scalar(mod_g[:], mods[:, l, 24 * k + 16:24 * k + 24, :], 1.0, 1.0 if k == 1 else 0.5,
                                  ALU.add, ALU.mult).then_inc(mab_done, 1)
                dve.wait_ge(mab_done, 3 * g + 3)

                def span(k):
                    return slice(0, HALF) if k < DC else slice(HALF, SEQ)

                def lo(k):
                    c = span(k)
                    dve.wait_ge(nhi_done, 2 * DC * g + k + 1)
                    dve.scalar_tensor_tensor(out=n_lo[:, k % DC, c], in0=u[k % 3][:, 0:c.stop - c.start],
                                             scalar=mod_b[:, k % DC, 0:1], in1=n_hi[:, k % DC, c].bitcast(F32),
                                             op0=ALU.add, op1=ALU.subtract).then_inc(n_ready, 1)

                for k2 in range(2 * DC + 1):
                    if k2 in (0, 2):
                        root(g, k2 // 2)
                    if k2 < 2 * DC:
                        c = span(k2)
                        if k2 % DC == 0:
                            dve.wait_ge(rstd_done, 2 * g + k2 // DC + 1)
                        if k2 >= 3:
                            dve.wait_ge(n_ready, 2 * DC * g + k2 - 2)
                        dve.scalar_tensor_tensor(out=u[k2 % 3][:, 0:c.stop - c.start], in0=x[:, k2 % DC, c],
                                                 scalar=mod_a[:, k2 % DC, 0:1], in1=rstd[:, c],
                                                 op0=ALU.mult, op1=ALU.mult).then_inc(u_done, 1)
                    if k2 >= 1:
                        lo(k2 - 1)

            def residual(at, m, y0, y1, last_unit):
                dve.wait_ge(out_done, at + 1)
                dve.scalar_tensor_tensor(out=x[:, m, cols[0]], in0=y0[:, 0:HALF], scalar=mod_g[:, m, 0:1],
                                         in1=x[:, m, cols[0]], op0=ALU.mult, op1=ALU.add).then_inc(y_free, 1)
                dve.wait_ge(wslot_free, last_unit + 5)
                dve.scalar_tensor_tensor(out=x[:, m, HALF:SEQ], in0=y1[:, 0:HP1], scalar=mod_g[:, m, 0:1],
                                         in1=x[:, m, HALF:SEQ], op0=ALU.mult, op1=ALU.add)
                dve.wait_ge(x_done, at + 1)
                dve.tensor_tensor(ytmp[:], y1[:, HP1:HALF].rearrange("p (i t) -> p i t", t=DSEQ),
                                  mod_g[:, m, 1:NS].unsqueeze(2).broadcast_to((P, NDEC, DSEQ)), ALU.mult)\
                    .then_inc(y_free, 1)
                dve.wait_ge(y_free, 2 * at + 6)
                xs = x[:, m, SEQ:NT].rearrange("p (i t) -> p i t", t=DSEQ)
                dve.tensor_tensor(xs, xs, ytmp[:], ALU.add).then_inc(x_done, 1)

            def add_square(g, m):
                dve.wait_ge(sq_done, 8 * g + m + 1)
                if m > 1:
                    dve.wait_ge(acc_done, 7 * g + m - 1)
                dve.tensor_tensor(acc[:], acc[:], sq[m % 2][:], ALU.add).then_inc(acc_done, 1)

            def ffn(l, f):
                for p in range(3):
                    with dve.Fori(0, PORT[p] // 2) as i:
                        t = DEPTH * ADA_PRO + l * ADA_IN + PBASE[p] // 2 + i
                        for q in range(2):
                            if f == 0:
                                for k in range(2):
                                    ada_lo(4 * t + 2 * q + k, k)
                            for s in range(2):
                                if f == 0 and q == 1 and s == 1:
                                    ada_evict(t)
                                hp = half_pair(l, f, p, 2 * i + q, s)
                                dve.wait_ge(sil_done, hp + 1)
                                dve.wait_ge(h_ready, hp + 1)
                                dve.tensor_tensor(hf[s][:], sil[s][:], bank[2 * s + 1][:, 0:HALF], ALU.mult)\
                                    .then_inc(gate_free, 1)
                                dve.wait_ge(gate_free, hp + 3)
                                hid = bass.ds(2 * i + q, 1)
                                dve.tensor_copy(h_hi[:, hid, cols[s]], hf[s][:].unsqueeze(1)).then_inc(hhi_done, 1)
                                dve.wait_ge(hhi_done, hp + 1)
                                dve.tensor_tensor(h_lo[:, hid, cols[s]], hf[s][:].unsqueeze(1),
                                                  h_hi[:, hid, cols[s]].bitcast(F32), ALU.subtract)\
                                    .then_inc(h_ready, 1)
                        if f == 0:
                            ada_bias(t, l, bass.ds(4 * ADA_PRO + 4 * (PBASE[p] // 2) + 4 * i, 4))
                    for m in range(DC):
                        y = bank[4:6] if m % 2 == 0 else bank[2:4]
                        residual(out_tile(l, f, p, m), m, *y, unit(l, f, p, 2 * PORT[p] + m))
                        if p == 2 and m >= 2:
                            add_square(3 * l + 2 * f + 1, m - 1)
                add_square(3 * l + 2 * f + 1, DC - 1)


            def mix_dve(l):
                def own(ins):
                    dv.send(ins)
                    dv.last(dve, l)

                def used(k):
                    dve.wait_ge(wslot_free, l * LAYER_U + FFN_U + k + 5)

                own(dve.tensor_copy(gain[:].unsqueeze(1), gains[:, bass.ds(l, 1), :]))
                dve.wait_ge(n_ready, 2 * DC * (3 * l + 1) + 2 * DC)
                dve.wait_ge(ns_ready, 3 * l + 2)
                for t in (q_sub, q_blk):
                    dve.memset(t[GK:P, 0, :], 0.0)
                    dve.memset(t[0:GK, 1, :], 0.0)
                dve.memset(att[:], 0.0)
                zeroed.send(dve.memset(kd_t[:], 0.0))
                for s in range(2):
                    if s == 0:
                        proj_mm.wait(dve, l, 0)
                    else:
                        used(U_S)
                    s_out.send(dve.tensor_copy(kg[:, cols[s]], bank[s][:, 0:HALF]))
                for j in range(2):
                    for s in range(2):
                        z_mm.wait(dve, l, 2 * j + s)
                        z_out.send(dve.tensor_scalar(gb[:, j, cols[s]], bank[((2, 3), (6, 7))[j][s]][:, 0:HALF],
                                                     gain[:, j:j + 1], None, ALU.add))
                z_out.last(dve, l)
                own(dve.tensor_scalar(soft[:], gb[:], -1.0, None, ALU.mult))
                zabs.send(dve.tensor_tensor(soft[:], gb[:], soft[:], ALU.min))
                soft_e.wait(dve, l, 1)
                own(dve.scalar_tensor_tensor(out=gb[:], in0=gb[:], scalar=0.0, in1=soft[:], op0=ALU.min,
                                             op1=ALU.subtract))
                dve.wait_ge(scan_in, 32 * l + 32)
                for j in range(2):
                    scan_done.send(dve.tensor_tensor_scan(gb[:, j, :], scan_m[:], gb[:, j, :], 0.0, ALU.mult, ALU.add))
                scan_done.last(dve, l)

                def decays_in(j):
                    b = gb[:, j, :]
                    if j:
                        kdt_mm.wait(dve, l, 1)
                        att_mm.wait(dve, l, 1)
                    v = b.rearrange("p (n t) -> p n t", t=SUB)
                    ref = v[:, :, SUB // 2 - 1:SUB // 2]
                    dec.send(dve.tensor_tensor(k_dec[:].rearrange("p (n t) -> p n t", t=SUB), v,
                                               ref.broadcast_to((P, NT // SUB, SUB)), ALU.subtract))
                    blk = b[:, 0:SEQ].rearrange("p (n t) -> p n t", t=CH)
                    for i in range(NSUB):
                        ln, r = SUB * (i + 1), SUB * i + SUB // 2 - 1
                        dst = k_sub[:, KHAT[i]:KHAT[i + 1]].rearrange("p (n t) -> p n t", t=ln)
                        dve.tensor_tensor(dst, blk[:, :, r:r + 1].broadcast_to((P, NCH, ln)), blk[:, :, 0:ln],
                                          ALU.subtract)
                    sv = b[:, SEQ:NT].rearrange("p (n t) -> p n t", t=DSEQ)
                    dec.send(dve.tensor_tensor(k_sub[:, KHAT[NSUB]:KHAT[NSUB] + P].rearrange("p (n t) -> p n t", t=DSEQ),
                                               sv[:, :, SUB // 2 - 1:SUB // 2].broadcast_to((P, NDEC, DSEQ)), sv,
                                               ALU.subtract))

                def decays_out(j):
                    b = gb[:, j, :]
                    blk = b[:, 0:SEQ].rearrange("p (n t) -> p n t", t=CH)
                    sv = b[:, SEQ:NT].rearrange("p (n t) -> p n t", t=DSEQ)
                    e_done.wait(dve, l, 4 * j)
                    if j:
                        ds_out.wait(dve, l, 3)
                        o_mm.wait(dve, l, 2)
                    dve.tensor_copy(elast[:, 0:NCH].unsqueeze(2),
                                    e_b[:, 0:SEQ].rearrange("p (n t) -> p n t", t=CH)[:, :, CH - 1:CH])
                    dve.tensor_copy(elast[:, NCH:NCH + NDEC].unsqueeze(2),
                                    e_b[:, SEQ:NT].rearrange("p (n t) -> p n t", t=DSEQ)[:, :, DSEQ - 1:DSEQ])
                    zeroed.wait(dve, l, 0)
                    dve.tensor_tensor(q_blk[0:GK, 0, :], gq[0:GK, j, :], e_b[0:GK, :], ALU.mult)
                    qk_ready.send(dve.tensor_tensor(q_blk[GK:P, 1, :], gq[GK:P, j, :], e_b[GK:P, :], ALU.mult))
                    e_done.wait(dve, l, 4 * j + 1)
                    dve.tensor_tensor(q_sub[0:GK, 0, :], gq[0:GK, j, :], k_dec[0:GK, :], ALU.mult)
                    qk_ready.send(dve.tensor_tensor(q_sub[GK:P, 1, :], gq[GK:P, j, :], k_dec[GK:P, :], ALU.mult))
                    qk_ready.last(dve, l)
                    dve.tensor_tensor(k_dec[:, 0:SEQ].rearrange("p (n t) -> p n t", t=CH),
                                      blk[:, :, CH - 1:CH].broadcast_to((P, NCH, CH)), blk, ALU.subtract)
                    dec.send(dve.tensor_tensor(k_dec[:, SEQ:NT].rearrange("p (n t) -> p n t", t=DSEQ),
                                               sv[:, :, DSEQ - 1:DSEQ].broadcast_to((P, NDEC, DSEQ)), sv, ALU.subtract))
                    e_done.wait(dve, l, 4 * j + 2)
                    kb = gk[:, j, 0:SEQ].rearrange("p (n t) -> p n t", t=CH)
                    for i in range(NSUB):
                        ln = SUB * (i + 1)
                        dst = k_sub[:, KHAT[i]:KHAT[i + 1]].rearrange("p (n t) -> p n t", t=ln)
                        dve.tensor_tensor(dst, dst, kb[:, :, 0:ln], ALU.mult)
                    dst = k_sub[:, KHAT[NSUB]:KHAT[NSUB] + P]
                    qk_ready.send(dve.tensor_tensor(dst, dst, gk[:, j, SEQ:NT], ALU.mult))
                    e_done.wait(dve, l, 4 * j + 3)
                    qk_ready.send(dve.tensor_tensor(k_dec[:], k_dec[:], gk[:, j, :], ALU.mult))

                decays_in(0)
                for t in range(5):
                    if t < 4:
                        gv_mm.wait(dve, l, t)
                    else:
                        used(U_GV + 3)
                    gv_out.send(dve.tensor_copy(v_g[:, t, :], bank[(4, 5, 0, 1, 2)[t]][:, :]))
                gqk_out.wait(dve, l, 7)
                decays_out(0)
                for c in range(KL):
                    for s in range(2):
                        if s == 0:
                            proj_mm.wait(dve, l, 12 + c)
                        else:
                            used(U_CKV + c)
                        ckv_ev.send(dve.tensor_copy(ckv[:, c, cols[s]], bank[((1, 2), (3, 6))[c][s]][:, 0:HALF]))
                ckv_ev.last(dve, l)
                lsq.wait(dve, l, 4)
                for c in range(QL + KL):
                    for s in range(2):
                        i = s if c < QL else 2 + s
                        lrs.wait(dve, l, 4 + i)
                        t = cq[:, c, cols[s]] if c < QL else ckv[:, c - QL, cols[s]]
                        lat_n.send(dve.scalar_tensor_tensor(out=t, in0=t, scalar=gain[:, 3 + c:4 + c],
                                                            in1=bank[(1, 2, 3, 6)[i]][:, 0:HALF],
                                                            op0=ALU.mult, op1=ALU.mult))
                for c in range(QL + KL):
                    chi_out.wait(dve, l, c)
                    t, hi, lo = (cq[:, c, :], qn_hi[:, c, :], qn_lo[:, c, :]) if c < QL else \
                        (ckv[:, c - QL, :], c_hi[:, c - QL, :], c_lo[:, c - QL, :])
                    if c == 0:
                        lat_n.last(dve, l)
                    clo.send(dve.tensor_tensor(lo, t, hi.bitcast(F32), ALU.subtract))

                def gla_scores(j):
                    b = GLA_BANKS[j]
                    att_mm.wait(dve, l, 2 * j)
                    if j:
                        o_mm.wait(dve, l, 2)
                    src = bank[b["A"]][:, :].rearrange("p (n h t) -> p n h t", n=4, h=2)
                    for par in range(2):
                        for i in range(NSUB):
                            r = slice(CH * par, CH * par + SUB * (i + 1))
                            t = slice(i * SUB, (i + 1) * SUB)
                            ta = slice(CH * par + i * SUB, CH * par + (i + 1) * SUB)
                            ln = SUB * (i + 1)
                            m = tri[r, t].unsqueeze(1).unsqueeze(1).broadcast_to((ln, 4, 2, SUB))
                            ins = dve.tensor_tensor(att[r, 0:4, :, ta], src[r, :, :, t], m, ALU.mult)
                    att_out.send(ins)
                    att_mm.wait(dve, l, 2 * j + 1)
                    att_out.send(dve.tensor_tensor(att[:, 4, :, :],
                                                   bank[b["AS"]][:, 0:2 * P].rearrange("p (h t) -> p h t", h=2),
                                                   bd[:].unsqueeze(1).broadcast_to((P, 2, P)), ALU.mult))
                    kdt_mm.wait(dve, l, 2 * j + 1)
                    if j:
                        ds_mm.wait(dve, l, 3)
                    k, o = b["KTS"]
                    kds_out.send(dve.tensor_tensor(kd_s[:], bank[k][:, o:o + P].unsqueeze(1).broadcast_to((P, NDEC, P)),
                                                   seqm[:].unsqueeze(2).broadcast_to((P, NDEC, P)), ALU.mult))

                def gla_carry(j):
                    b = GLA_BANKS[j]
                    if j:
                        o_mm.wait(dve, l, 1)
                        dve.wait_ge(gla_st, 64 * l + 32)
                    for n in range(NCH):
                        if n % 4 == 0:
                            ds_mm.wait(dve, l, 4 * j + n // 4)
                        add = bank[b["DS"][n // 4]][:, (n % 4) * GV:(n % 4 + 1) * GV]
                        if n == 0:
                            ins = dve.tensor_copy(s_p[:, 0, :], add)
                        else:
                            ins = dve.scalar_tensor_tensor(out=s_p[:, n, :], in0=s_p[:, n - 1, :],
                                                           scalar=elast[:, n:n + 1], in1=add, op0=ALU.mult, op1=ALU.add)
                        if n % 4 == 3:
                            ds_out.send(ins)
                            ds_out.last(dve, l)
                        else:
                            own(ins)
                    o_mm.wait(dve, l, 3 * j + 2)
                    dve.wait_ge(s_in, 32 * l + 16 * j + 16)
                    own(dve.tensor_tensor(s_s[:], s_s[:], elast[:, NCH:NCH + NDEC].unsqueeze(2)
                                          .broadcast_to((P, NDEC, GV)), ALU.mult))
                    for q in range(2):
                        ds_mm.wait(dve, l, 4 * j + 2 + q)
                        t = s_s[:, 4 * q:4 * q + 4, :]
                        ds_out.send(dve.tensor_tensor(t, t, bank[b["DSS"][q]][:, :].rearrange("p (i v) -> p i v", v=GV),
                                                      ALU.add))

                def gla_finish(j):
                    b = GLA_BANKS[j]
                    for i, (c0, c1) in enumerate(OSPAN):
                        orn.wait(dve, l, 6 * j + 3 + i)
                        o_mul.send(dve.tensor_tensor(o_sq[:, c0:c1], bank[b["O"][i]][:, 0:c1 - c0], o_rs[:, c0:c1],
                                                     ALU.mult))
                        o_mul.last(dve, l)
                        t0, n = (0, 256, 512)[i], (c1 - c0) // 2
                        t = gog[:, 2 * j:2 * j + 2, t0:t0 + n]
                        gla_fin.send(dve.scalar_tensor_tensor(out=t, in0=o_sq[:, c0:c1].rearrange("p (h t) -> p h t", h=2),
                                                              scalar=gain[:, 2:3], in1=t, op0=ALU.mult, op1=ALU.mult))

                gog_out.wait(dve, l, 7)
                gla_scores(0)
                gla_carry(0)
                decays_in(1)
                decays_out(1)
                gla_finish(0)
                gla_scores(1)
                gla_carry(1)
                gla_finish(1)

                dve.wait_ge(cs_ld, 16 * l + 16)
                gla_st_all = 64 * l + 64
                dve.wait_ge(gla_st, gla_st_all)

                def rope(lo, hi, c, dst, scale, sg):
                    own(dve.scalar_tensor_tensor(out=r_t[NOPE:96, 0:HALF], in0=hi, scalar=scale, in1=cs[96:P, c],
                                                 op0=ALU.mult, op1=ALU.mult))
                    own(dve.scalar_tensor_tensor(out=dst, in0=lo, scalar=scale, in1=cs[NOPE:96, c],
                                                 op0=ALU.mult, op1=ALU.mult))
                    sg.send(dve.tensor_tensor(dst, dst, r_t[NOPE:96, 0:HALF], ALU.add))
                    sg.last(dve, l)

                for s in range(2):
                    rope(kg[NOPE:96, cols[s]], kg[96:P, cols[s]], cols[s], kg[NOPE:96, cols[s]], 1.0, kpe_done)
                for h in range(MH):
                    for s in range(2):
                        if h % 2 and s:
                            used(U_UQ + h // 2)
                        else:
                            q_mm.wait(dve, l, 3 * (h // 2) + 2 * (h % 2) + s)
                        b = bank[QBANKS[h][s]]
                        rope(b[NOPE:96, 0:HALF], b[96:P, 0:HALF], cols[s], q_h[NOPE:96, h, cols[s]], MLA_SCALE, rope_done)
                qpe_out.send(dve.tensor_copy(q_pe[NOPE:96, :, :].rearrange("p i (h t) -> p h i t", t=DSEQ),
                                             q_h[NOPE:96, :, SEQ:NT].rearrange("p h (i t) -> p h i t", t=DSEQ)))
                for t in range(4):
                    if t < 3:
                        v_mm.wait(dve, l, t)
                    else:
                        used(U_UV)
                    vm_out.send(dve.tensor_copy(v_m[:, t, :], bank[(6, 5, 7, 0)[t]][:, :]))
                for h in range(GH):
                    ohi_out.wait(dve, l, h)
                    olo.send(dve.tensor_tensor(o_lo[:, h, :], gog[:, h, :], o_hi[:, h, :].bitcast(F32), ALU.subtract))
                olo.last(dve, l)
                cn_mm.wait(dve, l, 0)
                cn_out.send(dve.tensor_copy(cn_t[:], bank[6][:, 0:KL * P]))
                qa_mm.wait(dve, l, 3)
                for it in range(40 + 6):
                    if it < 40:
                        n, b = it % 4, bank[SBANKS[it % 4]]
                        if it >= 4:
                            t_mm.wait(dve, l, it - 4)
                        if it < NDEC:
                            if it >= 4:
                                p_norm.wait(dve, l, it - 4)
                            dve.memset(p_s[n][:, PAST:3 * P], 0.0)
                            w = PAST + DSEQ
                        else:
                            w = P * ((it - NDEC) % 4 + 1)
                        s_mm.wait(dve, l, it)
                        p_max.send(dve.tensor_reduce(mx[:, n:n + 1], b[:, 0:w], AX.X, ALU.max, negate=True))
                    if 1 <= it < 41:
                        jt = it - 1
                        n = jt % 4
                        p_exp.wait(dve, l, jt)
                        if jt >= 4:
                            p_norm.wait(dve, l, jt - 4)
                        if jt < NDEC:
                            own(dve.tensor_tensor(psum2[:, n:n + 1], psums[:, n:n + 1], psum2[:, n:n + 1], ALU.add))
                            own(dve.reciprocal(rsum[:, n:n + 1], psum2[:, n:n + 1]))
                            t = p_s[n][:]
                        else:
                            own(dve.reciprocal(rsum[:, n:n + 1], psums[:, n:n + 1]))
                            t = p_p[n][:, 0:P * ((jt - NDEC) % 4 + 1)]
                        p_norm.send(dve.tensor_scalar(t, t, rsum[:, n:n + 1], None, ALU.mult))
                    jo = it - 4
                    if 0 <= jo < NDEC:
                        ol_mm.wait(dve, l, jo)
                        ol_out.send(dve.tensor_copy(o_lat[:, :, :, DSEQ * jo:DSEQ * (jo + 1)],
                                                    bank[(1, 4)[jo % 2]][:, 0:KL * P]
                                                    .rearrange("p (c h t) -> p c h t", c=KL, t=DSEQ)))
                    if it == NDEC + 7:
                        ohi_out.wait(dve, l, 4)
                        olo.send(dve.tensor_tensor(o_lo[:, 4:8, SEQ:NT], bank[1][:, :].rearrange("p (c t) -> p c t", t=P),
                                                   o_hi[:, 4:8, SEQ:NT].bitcast(F32), ALU.subtract))
                    hp = (it - 5 - NDEC - 7) // 8
                    if it == NDEC + 8 * hp + 12 and 0 <= hp < 4:
                        ohi_out.wait(dve, l, 5 + hp)
                        olo.send(dve.tensor_tensor(o_lo[:, 4 + hp, 0:SEQ], bank[(4, 1)[hp % 2]][:, :],
                                                   o_hi[:, 4 + hp, 0:SEQ].bitcast(F32), ALU.subtract))
                for m in range(DC):
                    y = bank[4:6] if m % 2 == 0 else bank[2:4]
                    residual(l * OUT_T + 3 * DC + m, m, *y, l * LAYER_U + FFN_U + U_OUT + m)
                    if m >= 2:
                        add_square(3 * l + 2, m - 1)
                add_square(3 * l + 2, DC - 1)

            dve.memset(ones[:], 1.0)
            dve.memset(eps[:], EPS).then_inc(const_done, 1)
            dve.memset(c_st[:].bitcast(F32), 0.0).then_inc(cst_done, 1)
            dve.wait_ge(cst_done, 1)
            dve.wait_ge(csil_done, 1)
            dve.tensor_copy(c_st[:, :, 0:NS], c_sil[:]).then_inc(cst_done, 1)
            dve.wait_ge(cst_done, 2)
            dve.tensor_tensor(c_st[:, :, NS:2 * NS], c_sil[:], c_st[:, :, 0:NS].bitcast(F32), ALU.subtract)\
                .then_inc(cst_done, 1)

            def ada_pair(i):
                for n in range(DEPTH):
                    t = DEPTH * i + n
                    late = not (n == 0 and isinstance(i, int))
                    for k in range(4):
                        ada_lo(4 * t + k, k)
                        if k == 1 and late:
                            ada_evict(t - 1, ADA_FIRST[1 - n])
                    if late:
                        ada_bias(t - 1, 1 - n, bass.ds(4 * (i - 1 + n), 4))

            ada_pair(0)
            for m in range(1, DC):
                add_square(0, m)
            with dve.Fori(1, ADA_PRO) as i:
                ada_pair(i)
            ada_evict(DEPTH * ADA_PRO - 1, ADA_FIRST[1])
            ada_bias(DEPTH * ADA_PRO - 1, 1, slice(4 * ADA_PRO - 4, 4 * ADA_PRO))
            dve.wait_ge(cst_in, 16 * 6)
            with dve.Fori(0, DEPTH) as l:
                norm_apply(l, 0, DEPTH * ADA_PRO)
                ffn(l, 0)
                norm_apply(l, 1, DEPTH * ADA_PRO + ADA_IN + l * ADA_IN)
                mix_dve(l)
                norm_apply(l, 2, DEPTH * ADA_PRO + ADA_IN + l * ADA_IN)
                ffn(l, 1)
            g = 3 * DEPTH
            root(g, 0)
            root(g, 1)
            for m in range(DC):
                for s in range(2):
                    dve.wait_ge(rstd_done, 2 * g + s + 1)
                    dve.scalar_tensor_tensor(out=y_sb[:, m, cols[s]], in0=x[:, m, cols[s]], scalar=fin_g[:, m:m + 1],
                                             in1=rstd[:, cols[s]], op0=ALU.mult, op1=ALU.mult).then_inc(y_done, 1)
    for sg in signals:
        assert sg.sent == sg.per_layer, (sg.sem, sg.sent, sg.per_layer)
    return nc


def layout(inputs):
    import numpy as np
    f = {k: np.ascontiguousarray(np.asarray(v)) for k, v in inputs.items()}

    def feat(a):
        return np.ascontiguousarray(a.T.reshape(-1, P, a.shape[0]).transpose(1, 0, 2))

    def chunked(w):
        return w.reshape(-1, P, w.shape[1]).transpose(1, 0, 2)

    def tiles(w):
        c = chunked(w)
        k = c.shape[1]
        u = c.reshape(P, k, -1, P).transpose(2, 0, 1, 3).reshape(-1, P, k * P)
        return np.pad(u, ((0, 0), (0, 0), (0, UW - k * P)))

    a = {}
    a["xT"] = feat(np.concatenate([f["x_prompt"].reshape(SEQ, D), f["x_sample"].reshape(-1, D)]))
    a["cT"] = feat(np.concatenate([f["c_prompt"], f["c_sample"]]))
    a["lng"] = np.ascontiguousarray(f["ln_g"].reshape(DEPTH, 3, DC, P).transpose(3, 0, 1, 2))
    a["bada"] = np.ascontiguousarray(f["b_ada"].reshape(DEPTH, NMOD, P).transpose(2, 0, 1))
    a["fing"] = np.ascontiguousarray(f["final_g"].reshape(DC, P).T)
    a["selc"] = np.tile(np.eye(NS, dtype=np.float32), (2, 1))
    main, ada, uvs, ukts = [], [], [], []
    for l in range(DEPTH):
        for nm in ("1", "mix", "2"):
            if nm == "mix":
                w = f["w_in"][l]
                o = np.cumsum([0, GH * GK, GH * GK, GH * GV, GR, GH * GV, QL * P, KL * P, ROPE])
                gq, gk, gv, glr, gog, cq, ckv, kpe = (w[:, o[i]:o[i + 1]] for i in range(8))
                s_tile = np.zeros((D, P), np.float32)
                s_tile[:, 0:GR] = glr
                s_tile[:, NOPE:96] = kpe
                s_tile[:, 96:P] = kpe[:, SWAP]
                main += [tiles(np.concatenate([s_tile, gq, gk, gog], 1)),
                         chunked(gv).reshape(P, 4, 2 * GH * GV).transpose(1, 0, 2),
                         tiles(np.concatenate([cq, ckv], 1))]
                uq = f["w_uq"][l].reshape(QL * P, MH, NOPE + ROPE)
                uq = np.concatenate([uq, uq[:, :, NOPE + np.array(SWAP)]], 2)
                uq = uq.reshape(QL, P, MH // 2, 2, P).transpose(2, 1, 3, 0, 4).reshape(MH // 2, P, 2 * QL * P)
                main.append(np.pad(uq, ((0, 0), (0, 0), (0, UW - 2 * QL * P))))
                ukv = f["w_ukv"][l].reshape(KL * P, MH, NOPE + MV)
                uk = np.ascontiguousarray(ukv[:, :, :NOPE]).reshape(KL, P, 4, P)
                main.append(uk.transpose(1, 2, 0, 3).reshape(1, P, UW))
                uv = np.ascontiguousarray(ukv[:, :, NOPE:]).reshape(KL, P, MH * MV)
                main.append(uv.transpose(1, 0, 2).reshape(1, P, UW))
                uvs.append(uv.transpose(1, 0, 2))
                ukts.append(ukv[:, :, :NOPE].transpose(2, 1, 0))
                main.append(tiles(f["w_out"][l]))
                continue
            w_in = f[f"w_ffn{nm}_in"][l]
            gate_up = np.stack([tiles(w_in[:, :NFF * P]), tiles(w_in[:, NFF * P:])], 1)
            w_out = f[f"w_ffn{nm}_out"][l]
            for p in range(3):
                main.append(gate_up[PBASE[p]:PBASE[p] + PORT[p]].reshape(-1, P, UW))
                main.append(tiles(w_out[PBASE[p] * P:(PBASE[p] + PORT[p]) * P]))
        w = f["w_ada"][l].reshape(4, 2, P, 18, 512).transpose(3, 0, 2, 1, 4).reshape(18, 4, P, UW)
        ada.append(w)
    main.append(np.zeros((LEAD, P, UW), np.float32))
    a["wmain"] = np.concatenate(main)
    a["wada"] = np.concatenate([np.stack([w[:ADA_PRO] for w in ada], 1).reshape(-1, P, UW)]
                               + [w[ADA_PRO:].reshape(-1, P, UW) for w in ada])
    a["ukT"], a["wuv"] = np.stack(ukts), np.stack(uvs)
    a["gk2"] = f["w_gk2"]
    feat2 = lambda v: v.reshape(DEPTH, -1, P).transpose(2, 0, 1)
    a["gains"] = np.concatenate([feat2(f["b_gk2"]), feat2(f["gla_norm_g"]), feat2(f["mla_qnorm_g"]),
                                 feat2(f["mla_kvnorm_g"])], 2)
    ckv, kpe = f["cache_ckv"], f["cache_kpe"]
    a["pastkT"] = ckv.reshape(DEPTH * NDEC, PAST, KL, P).transpose(0, 3, 2, 1)
    a["pastv"] = ckv.reshape(DEPTH * NDEC, 2, P, KL * P).transpose(0, 2, 1, 3)
    a["pastpe"] = kpe.reshape(DEPTH * NDEC, PAST, ROPE).transpose(0, 2, 1)
    a["s0"] = f["state_gla"].reshape(DEPTH, NDEC, 2, P, GV).transpose(0, 2, 3, 1, 4).reshape(2 * DEPTH, P, NDEC, GV)
    a.update(shape_constants())
    return a


SWAP = list(range(ROPE // 2, ROPE)) + list(range(ROPE // 2))


def shape_constants():
    import numpy as np
    i = np.arange(P)
    one = np.float32
    t = np.arange(NT)
    start = np.where(t < SEQ, t % CH == 0, (t - SEQ) % DSEQ == 0)
    pos = np.where(t < SEQ, t, PAST + (t - SEQ) % DSEQ).astype(one)
    half = ROPE // 2
    inv = (one(10000.0) ** (-np.arange(half, dtype=one) / one(half))).astype(one)
    ang = (pos[None, :] * inv[:, None]).astype(one)
    cs = np.zeros((P, NT), one)
    cs[NOPE:96] = np.tile(np.cos(ang), (2, 1))
    cs[96:P] = np.concatenate([-np.sin(ang), np.sin(ang)])
    mrow = np.zeros((1, P + CH), one)
    mrow[0, :CH] = SHARP
    mrow[0, P:] = 1.0
    return {
        "scanm": np.ascontiguousarray(np.broadcast_to(1.0 - start, (P, NT)).astype(one)),
        "tri": (i[:, None] % CH <= i[None, :CH]).astype(one),
        "bd": ((i[:, None] // DSEQ == i[None] // DSEQ) & (i[:, None] <= i[None])).astype(one),
        "seqm": (i[:, None] // DSEQ == np.arange(NDEC)[None]).astype(one),
        "ident": np.eye(P, dtype=one), "mrow": mrow, "cs": cs,
    }


_INS = ["xT", "cT", "lng", "bada", "fing", "selc", "wmain", "wada", "scanm", "gk2", "gains", "tri",
        "bd", "seqm", "ident", "mrow", "cs", "ukT", "wuv", "pastkT", "pastv", "pastpe", "s0"]


def kernel(**inputs):
    import numpy as np
    import concourse.bacc as bacc
    from concourse import mybir as mb
    from concourse.bass_utils import run_bass_kernel_spmd as run

    nc = bacc.Bacc("TRN2", target_bir_lowering=False, num_devices=1)
    a = layout(inputs)
    arrays = {f"in_{n}": np.ascontiguousarray(a[n]) for n in _INS}
    args = [nc.dram_tensor(f"in_{n}", a[n].shape, mb.dt.from_np(a[n].dtype), kind="ExternalInput").ap() for n in _INS]
    outs = (("y", (P, DC, NT)), ("ckv", (DEPTH, P, KL, NT)), ("kpe", (DEPTH, ROPE, NT)),
            ("glap", (2 * DEPTH, P, GV)), ("glas", (2 * DEPTH, P, NDEC, GV)))
    out_aps = [nc.dram_tensor(n, s, mb.dt.float32, kind="ExternalOutput").ap() for n, s in outs]
    build(nc, *args, *out_aps)
    r = run(nc, [arrays], core_ids=[0]).results[0]
    c = np.ascontiguousarray
    y = r["y"].transpose(2, 1, 0).reshape(NT, D)
    ckv = r["ckv"].transpose(0, 3, 2, 1).reshape(DEPTH, NT, KL * P)
    kpe = r["kpe"].transpose(0, 2, 1)
    glap = r["glap"].reshape(DEPTH, 1, GH, GK, GV)
    glas = r["glas"].reshape(DEPTH, 2, 2, GK, NDEC, GV).transpose(0, 4, 1, 2, 3, 5).reshape(DEPTH, NDEC, GH, GK, GV)
    return (c(y[:SEQ]).reshape(1, SEQ, D), c(y[SEQ:]).reshape(NDEC, DSEQ, D),
            c(ckv[:, :SEQ]).reshape(DEPTH, 1, SEQ, KL * P), c(kpe[:, :SEQ]).reshape(DEPTH, 1, SEQ, ROPE), c(glap),
            c(ckv[:, SEQ:]).reshape(DEPTH, NDEC, DSEQ, KL * P), c(kpe[:, SEQ:]).reshape(DEPTH, NDEC, DSEQ, ROPE), c(glas))
```

```python
from contextlib import ExitStack

import concourse.bass as bass
from concourse import mybir

F32 = mybir.dt.float32
F32R = mybir.dt.float32r
ALU = mybir.AluOpType
ACT = mybir.ActivationFunctionType
AX = mybir.AxisListType

P = 128
D = 1024
DC = D // P
SEQ, NDEC, DSEQ, PAST = 512, 8, 16, 256
NT = SEQ + NDEC * DSEQ
HALF = NT // 2
HP1 = SEQ - HALF
NS = 1 + NDEC
DEPTH = 2
NFF = 22
PORT = (8, 8, 6)
PBASE = (0, 8, 16)
FFN_U = 2 * NFF + 3 * DC
MIX_U = 32
MIX_T = DC
OUT_T = 6 * DC + MIX_T
LAYER_U = 2 * FFN_U + MIX_U
TOTAL_U = DEPTH * LAYER_U
LEAD = 4
UW = 8 * P
DV_STEPS = 101
ADA_PRO = 7
ADA_IN = 11
NMOD = 72
EPS = 1e-6
CH, SUB = 64, 16
NCH, NSUB = SEQ // CH, CH // SUB
GH, GK, GV, GR = 4, 64, 128, 16
MH, NOPE, ROPE, MV = 8, 64, 32, 64
QL, KL = 3, 2
MLA_SCALE = (NOPE + ROPE) ** -0.5
GATE_NORM = 16.0
KHAT = [NCH * SUB * i * (i + 1) // 2 for i in range(NSUB + 1)]
SHARP = -1e30
T4 = NT * 4
NPB = 5
U_S, U_GQ, U_GK, U_GOG, U_GV, U_CQ, U_CKV, U_UQ, U_UK, U_UV, U_OUT = 0, 1, 3, 5, 9, 13, 16, 18, 22, 23, 24


class Signal:

    def __init__(self, sem, per_layer):
        self.sem, self.per_layer, self.sent = sem, per_layer, 0

    def send(self, ins):
        ins.then_inc(self.sem, 1)
        self.sent += 1

    def wait(self, eng, l, k):
        assert 0 <= k < self.per_layer
        eng.wait_ge(self.sem, l * self.per_layer + (k + 1))

    def last(self, eng, l):
        self.wait(eng, l, self.sent - 1)


def build(nc, xT, cT, lng, bada, fing, selc, wmain, wada, scanm, gk2_in, gains_in, tri_in, bd_in, seqm_in,
          ident_in, mrow_in, cs_in, ukT, wuv_in, past_kT, past_v, past_pe, s0_in,
          y_out, ckv_out, kpe_out, glap_out, glas_out):
    with ExitStack() as ctx:
        where = [16512]

        def sb(name, shape, dt=F32, at=None):
            n = 4
            for d in shape[1:]:
                n *= d
            if at is None:
                at = where[0]
                where[0] += (n + 31) // 32 * 32
            return nc.alloc_sbuf_tensor_at(name, shape, dt, offset=at), at + (n + 31) // 32 * 32

        def new(name, shape, dt=F32):
            return sb(name, shape, dt)[0]

        def sem(name):
            return ctx.enter_context(nc.semaphore(name))

        bank = [ctx.enter_context(nc.psum_tensor(f"bank{i}", [P, 512], F32)) for i in range(8)]
        ADA_ACC, ADA_SEL = bank[6], bank[7]
        ADA_FIRST = (bank[6], bank[5])

        x = new("x", [P, DC, NT])
        n_at = where[0]
        n_hi = new("n_hi", [P, DC, NT], F32R)
        n_lo = new("n_lo", [P, DC, NT], F32R)
        arena_a = where[0]
        h_hi = new("h_hi", [P, 8, NT], F32R)
        h_lo = new("h_lo", [P, 8, NT], F32R)
        raw = [new(f"raw{i}", [P, UW]) for i in range(2)]
        w_hi = [new(f"w_hi{i}", [P, 8, P], F32R) for i in range(4)]
        w_lo = [new(f"w_lo{i}", [P, 8, P], F32R) for i in range(4)]
        c_st = new("c_st", [P, DC, P], F32R)
        c_in = sb("c_in", [P, DC, NS], at=arena_a)[0]
        c_sil = sb("c_sil", [P, DC, NS], at=arena_a + 512)[0]
        sel = new("sel", [2 * NS, NS])
        ones = new("ones", [P, P])
        eps = new("eps", [P, 1])
        warm = new("warm", [P, 1])
        mods = new("mods", [P, DEPTH, NMOD, NS])
        b_ada = new("b_ada", [P, DEPTH, NMOD])
        ln_g = new("ln_g", [P, DEPTH, 3, DC])
        fin_g = new("fin_g", [P, DC])
        mod_a = new("mod_a", [P, DC, NS])
        mod_b = new("mod_b", [P, DC, NS])
        mod_g = new("mod_g", [P, DC, NS])
        gains = new("gains", [P, DEPTH, 8])
        gain = new("gain", [P, 8])
        tri = new("tri", [P, CH])
        bd = new("bd", [P, P])
        seqm = new("seqm", [P, NDEC])
        ident = new("ident", [P, P])
        mrow = new("mrow", [1, P + CH])
        elast = new("elast", [P, NCH + NDEC])
        mx = new("mx", [P, 4])
        psums = new("psums", [P, 4])
        psum2 = new("psum2", [P, 4])
        rsum = new("rsum", [P, 4])

        arena_b = where[0]
        araw = [new(f"araw{i}", [P, UW]) for i in range(2)]
        a_hi = [new(f"a_hi{i}", [P, 2, 512], F32R) for i in range(2)]
        a_lo = [new(f"a_lo{i}", [P, 2, 512], F32R) for i in range(2)]
        for i in (2, 3):
            at = arena_a + 1024 + 12288 * (i - 2)
            araw.append(sb(f"araw{i}", [P, UW], at=at)[0])
            a_hi.append(sb(f"a_hi{i}", [P, 2, 512], F32R, at=at + 4096)[0])
            a_lo.append(sb(f"a_lo{i}", [P, 2, 512], F32R, at=at + 8192)[0])
        for i in range(4, 8):
            araw.append(sb(f"araw{i}", [P, UW], at=n_at + 4096 * (i - 4))[0])
        sq = [new(f"sq{i}", [P, NT]) for i in range(2)]
        ln_s = new("ln_s", [P, NT])
        rstd = new("rstd", [P, NT])
        acc = new("acc", [P, NT])
        us = sb("us", [P, DC, P], at=where[0])[0]
        sil = [new(f"sil{i}", [P, HALF]) for i in range(2)]
        hf = [new(f"hf{i}", [P, HALF]) for i in range(2)]
        u = [new(f"u{i}", [P, HALF]) for i in range(3)]
        ev = new("ev", [2 * NS, 512])
        ytmp = new("ytmp", [P, NDEC, DSEQ])
        assert arena_b + 55296 <= 229368, arena_b + 55296
        y_sb = sb("y_sb", [P, DC, NT], at=n_at)[0]

        def in_a(name, shape, at, dt=F32):
            return sb(name, shape, dt, at=arena_a + at)[0]

        def in_b(name, shape, at, dt=F32):
            return sb(name, shape, dt, at=arena_b + at)[0]

        def in_n(name, shape, half, tiles, dt=F32):
            return sb(name, shape, dt, at=n_at + half * DC * T4 + tiles * T4)[0]

        cq = in_a("cq", [P, QL, NT], 0)
        ckv = in_a("ckv", [P, KL, NT], 8192)
        gq = in_a("gq", [P, 2, NT], 15360)
        gk = in_a("gk", [P, 2, NT], 20480)
        gb = in_a("gb", [P, 2, NT], 25600)
        gog = in_a("gog", [P, GH, NT], 30720)
        v_m = in_a("v_m", [P, 4, MH * MV], 13312)
        q_abs = in_a("q_abs", [P, KL, NDEC, MH * DSEQ], 21504)
        uk_t = in_a("uk_t", [NOPE, MH, KL * P], 0)
        p_s = [in_a(f"p_s{i}", [P, 3 * P], 30720 + 1536 * i) for i in range(4)]
        pt_s = [in_a(f"pt_s{i}", [P, 3, P], 36864 + 1536 * i) for i in range(2)]
        cn_t = in_a("cn_t", [P, KL * P], 39936)
        o_lat = in_a("o_lat", [P, KL, MH, P], 0)
        pt_p = [in_a(f"pt_p{i}", [P, 4, P], 30720 + 2048 * i) for i in range(3)]
        v_g = in_b("v_g", [P, 5, GH * GV], 0)
        q_sub = in_b("q_sub", [P, 2, NT], 10240)
        q_blk = in_b("q_blk", [P, 2, NT], 15360)
        att = in_b("att", [P, 5, 2, P], 20480)
        kd_t = in_b("kd_t", [P, 4, 2, P], 25600)
        kd_s = in_b("kd_s", [P, NDEC, P], 29696)
        k_sub = in_b("k_sub", [P, KHAT[NSUB] + P], 33792)
        soft = in_b("soft", [P, 2, NT], 33792)
        k_dec = in_b("k_dec", [P, NT], 39424)
        scan_m = in_b("scan_m", [P, NT], 39424)
        e_b = in_b("e_b", [P, NT], 41984)
        s_p = in_b("s_p", [P, NCH, GV], 44544)
        w_gk = in_b("w_gk", [GR, 2 * P], 44544)
        s_s = in_b("s_s", [P, NDEC, GV], 48640)
        kg = in_b("kg", [P, NT], 52736)
        q_h = in_b("q_h", [96, MH, NT], 0)
        k_h = in_b("k_h", [96, MH, SEQ], 20480)
        cs = in_b("cs", [P, NT], 36864)
        w_uv = in_b("w_uv", [P, KL, MH * MV], 36864)
        p_p = [in_b(f"p_p{i}", [P, SEQ], 40960 + 2048 * i) for i in range(4)]
        r_t = in_b("r_t", [96, HALF], 51200)
        c_hi = in_n("c_hi", [P, KL, NT], 0, 0, F32R)
        c_lo = in_n("c_lo", [P, KL, NT], 1, 0, F32R)
        o_sq = in_n("o_sq", [P, 2 * NT], 0, 2)
        o_rs = in_n("o_rs", [P, 2 * NT], 1, 2)
        qn_hi = in_n("qn_hi", [P, QL, NT], 0, 4, F32R)
        qn_lo = in_n("qn_lo", [P, QL, NT], 1, 4, F32R)
        lat_sq = [in_n(f"lat_sq{i}", [P, NT], i, 7) for i in range(2)]
        past_at = [arena_b + 40960, arena_b + 46080, n_at + (DC + 6) * T4, n_at + 4 * T4, n_at + (DC + 4) * T4]
        pk_t = [sb(f"pk_t{i}", [P, KL, PAST], at=a)[0] for i, a in enumerate(past_at)]
        pv = [sb(f"pv{i}", [P, 2, KL * P], at=a + 2048)[0] for i, a in enumerate(past_at)]
        pp_t = [sb(f"pp_t{i}", [96, PAST], at=a + 4096)[0] for i, a in enumerate(past_at)]
        q_pe = in_n("q_pe", [96, NDEC, MH * DSEQ], 0, 6)
        o_hi = in_n("o_hi", [P, DC, NT], 0, 0, F32R)
        o_lo = in_n("o_lo", [P, DC, NT], 1, 0, F32R)

        raw_full = [sem(f"raw_full{i}") for i in range(2)]
        whi_done = sem("whi_done")
        wlo_done = sem("wlo_done")
        wslot_free = sem("wslot_free")
        ada_full = [sem(f"ada_full{i}") for i in range(8)]
        ahi_done = sem("ahi_done")
        alo_done = sem("alo_done")
        aslot_free = sem("aslot_free")
        ev_done = sem("ev_done")
        sel_done = sem("sel_done")
        mod_done = sem("mod_done")
        const_in = sem("const_in")
        x_in = sem("x_in")
        csil_done = sem("csil_done")
        cst_done = sem("cst_done")
        const_done = sem("const_done")
        gate_done = sem("gate_done")
        sil_done = sem("sil_done")
        gate_free = sem("gate_free")
        hhi_done = sem("hhi_done")
        h_ready = sem("h_ready")
        out_done = sem("out_done")
        y_free = sem("y_free")
        x_done = sem("x_done")
        sq_done = sem("sq_done")
        acc_done = sem("acc_done")
        stat_done = sem("stat_done")
        ln_done = sem("ln_done")
        warm_done = sem("warm_done")
        rstd_done = sem("rstd_done")
        mab_done = sem("mab_done")
        modg_done = sem("modg_done")
        u_done = sem("u_done")
        us_step = sem("us_step")
        nhi_s_done = sem("nhi_s_done")
        ns_ready = sem("ns_ready")
        nhi_done = sem("nhi_done")
        n_ready = sem("n_ready")
        y_done = sem("y_done")
        y_stored = sem("y_stored")

        signals = []

        def signal(name, per_layer):
            signals.append(Signal(sem(name), per_layer))
            return signals[-1]

        cst_in = sem("cst_in")
        proj_mm = signal("proj_mm", 14)
        z_mm = signal("z_mm", 4)
        gv_mm = signal("gv_mm", 4)
        lat_mm = signal("lat_mm", 4)
        lat_mm_sq = signal("lat_mm_sq", 2)
        pv_mm = signal("pv_mm", 32)
        att_mm = signal("att_mm", 4)
        kdt_mm = signal("kdt_mm", 4)
        ds_mm = signal("ds_mm", 8)
        o_mm = signal("o_mm", 6)
        ost_mm = signal("ost_mm", 6)
        q_mm = signal("q_mm", 12)
        k_mm = signal("k_mm", 3)
        v_mm = signal("v_mm", 3)
        qa_mm = signal("qa_mm", 4)
        cn_mm = signal("cn_mm", 1)
        s_mm = signal("s_mm", 40)
        t_mm = signal("t_mm", 40)
        ol_mm = signal("ol_mm", 8)
        uv_mm = signal("uv_mm", 1)
        gqk_out = signal("gqk_out", 8)
        gog_out = signal("gog_out", 8)
        soft_e = signal("soft_e", 2)
        e_done = signal("e_done", 8)
        cq_out = signal("cq_out", 6)
        lsq = signal("lsq", 5)
        lrs = signal("lrs", 8)
        kdt_out = signal("kdt_out", 4)
        osq = signal("osq", 6)
        orn = signal("orn", 12)
        qh_out = signal("qh_out", 16)
        kh_out = signal("kh_out", 8)
        kpe_copied = signal("kpe_copied", 1)
        qa_out = signal("qa_out", 4)
        p_exp = signal("p_exp", 40)
        p_exp_a = signal("p_exp_a", 8)
        pt_out = signal("pt_out", 40)
        chi_out = signal("chi_out", 5)
        ohi_out = signal("ohi_out", 9)
        s_out = signal("s_out", 2)
        z_out = signal("z_out", 4)
        gv_out = signal("gv_out", 5)
        ckv_ev = signal("ckv_ev", 4)
        dv = signal("dv", DV_STEPS)
        zabs = signal("zabs", 1)
        scan_done = signal("scan_done", 2)
        kds_out = signal("kds_out", 2)
        dec = signal("dec", 6)
        qk_ready = signal("qk_ready", 8)
        zeroed = signal("zeroed", 1)
        att_out = signal("att_out", 4)
        ds_out = signal("ds_out", 8)
        o_mul = signal("o_mul", 6)
        gla_fin = signal("gla_fin", 6)
        lat_n = signal("lat_n", 10)
        clo = signal("clo", 5)
        rope_done = signal("rope_done", 16)
        kpe_done = signal("kpe_done", 2)
        qpe_out = signal("qpe_out", 1)
        vm_out = signal("vm_out", 4)
        cn_out = signal("cn_out", 1)
        p_max = signal("p_max", 40)
        p_norm = signal("p_norm", 40)
        ol_out = signal("ol_out", 8)
        olo = signal("olo", 9)
        scan_in, cs_ld, uk_in, uv_in, kv_st, gla_st, s_in = (
            sem(n) for n in ("scan_in", "cs_ld", "uk_in", "uv_in", "kv_st", "gla_st", "s_in"))
        keys_in = [sem(f"keys_in{i}") for i in range(NPB)]
        vals_in = [sem(f"vals_in{i}") for i in range(NPB)]

        block = ctx.enter_context(nc.Block())

        def unit(l, f, p, k):
            at = 0 if f == 0 else FFN_U + MIX_U
            at += sum(2 * PORT[q] + DC for q in range(p))
            return l * LAYER_U + at + k

        def half_pair(l, f, p, c, s):
            return (l * 2 + f) * 2 * NFF + 2 * (PBASE[p] + c) + s

        def pair(l, f, p, c):
            return (l * 2 + f) * NFF + PBASE[p] + c

        OSPAN = ((0, 512), (512, 1024), (1024, 1280))
        GLA_BANKS = (dict(A=4, AS=5, KT=0, KTS=(7, 0), DS=(1, 2), DSS=(3, 6), O=(4, 5, 7), ST=(1, 2, 3)),
                     dict(A=0, AS=6, KT=1, KTS=(4, 0), DS=(2, 3), DSS=(1, 4), O=(5, 7, 0), ST=(2, 3, 6)))
        QBANKS = ((1, 4), (2, 3), (6, 5), (7, 0)) * 2
        SBANKS, TBANKS = (6, 5, 2, 3), (7, 0)

        def out_tile(l, f, p, m):
            return l * OUT_T + f * (3 * DC + MIX_T) + p * DC + m

        cols = (slice(0, HALF), slice(HALF, NT))

        @block.sync
        def _(sp):
            def load_main(at, s):
                sp.dma_start(raw[s][:], wmain[at]).then_inc(raw_full[s], 16)

            def load_next(at, s):
                sp.wait_ge(wlo_done, at - 1)
                load_main(at, s)

            def load_ada(at, s, ring):
                if ring:
                    sp.wait_ge(alo_done, at + 5 - ring)
                sp.dma_start(araw[s][:], wada[at]).then_inc(ada_full[s], 16)

            sp.dma_start(c_in[:], cT).then_inc(const_in, 16)
            sp.dma_start(b_ada[:], bada).then_inc(const_in, 16)
            sp.dma_start(ln_g[:], lng).then_inc(const_in, 16)
            sp.dma_start(fin_g[:], fing).then_inc(const_in, 16)
            sp.dma_start(sel[:], selc).then_inc(const_in, 16)
            for k in range(8):
                load_ada(k, k, 0)
            sp.dma_start(x[:], xT).then_inc(x_in, 16)
            load_main(0, 0)
            load_main(1, 1)
            for dst, src in ((gains, gains_in), (tri, tri_in), (bd, bd_in),
                             (seqm, seqm_in), (ident, ident_in), (mrow, mrow_in)):
                sp.dma_start(dst[:], src).then_inc(cst_in, 16)
            with sp.Fori(1, ADA_PRO) as i:
                for k in range(8):
                    load_ada(8 * i + k, k, 8)
            for k in (2, 3):
                load_next(k, k % 2)
            with sp.Fori(0, DEPTH) as l:
                for f in range(2):
                    for p in range(3):
                        with sp.Fori(0, PORT[p] // 2) as i:
                            if f == 0:
                                for k in range(4):
                                    load_ada(DEPTH * ADA_PRO * 4 + l * ADA_IN * 4 + (PBASE[p] * 2 + 4 * i) + k, k % 2, 2)
                            for k in range(4):
                                load_next(unit(l, f, p, 0) + 4 * i + k + LEAD, k % 2)
                        with sp.Fori(0, DC // 2) as i:
                            for k in range(2):
                                load_next(unit(l, f, p, 2 * PORT[p]) + 2 * i + k + LEAD, k)
                    if f == 0:
                        with sp.Fori(0, MIX_U // 2) as i:
                            for k in range(2):
                                load_next(l * LAYER_U + FFN_U + 2 * i + k + LEAD, k)
            sp.wait_ge(y_done, 2 * DC)
            sp.dma_start(y_out, y_sb[:]).then_inc(y_stored, 16)
            sp.wait_ge(y_stored, 16)
            sp.wait_ge(kv_st, 32 * DEPTH)
            sp.wait_ge(gla_st, 64 * DEPTH)

        @block.gpsimd
        def _(pool):
            def low(at, slot):
                pool.wait_ge(whi_done, at + 1)
                pool.tensor_tensor(w_lo[slot][:], raw[slot % 2][:].rearrange("p (c m) -> p c m", m=P),
                                   w_hi[slot][:].bitcast(F32), ALU.subtract).then_inc(wlo_done, 1)

            def norm_samples(g, wait_x):
                sv = us[:].rearrange("p m (i t) -> p m i t", t=DSEQ)
                wait_x()
                pool.wait_ge(mab_done, 2 * g + 2)
                pool.tensor_tensor(sv, x[:, :, SEQ:NT].rearrange("p m (i t) -> p m i t", t=DSEQ),
                                   mod_a[:, :, 1:NS].unsqueeze(3).broadcast_to((P, DC, NDEC, DSEQ)),
                                   ALU.mult).then_inc(us_step, 1)
                pool.wait_ge(rstd_done, 2 * g + 2)
                pool.wait_ge(us_step, 3 * g + 1)
                pool.tensor_tensor(us[:], us[:], rstd[:, SEQ:NT].unsqueeze(1).broadcast_to((P, DC, P)),
                                   ALU.mult).then_inc(us_step, 1)
                pool.wait_ge(us_step, 3 * g + 2)
                pool.tensor_tensor(sv, sv, mod_b[:, :, 1:NS].unsqueeze(3).broadcast_to((P, DC, NDEC, DSEQ)),
                                   ALU.add).then_inc(us_step, 1)

            for k in range(LEAD):
                low(k, k)
            with pool.Fori(0, DEPTH) as l:
                for n, (first, count) in enumerate(((0, FFN_U), (FFN_U, MIX_U), (FFN_U + MIX_U, FFN_U))):
                    def wait_x():
                        if n == 0:
                            pool.wait_ge(x_in, 16)
                        pool.wait_ge(x_done, l * OUT_T + (0, 3 * DC, 3 * DC + MIX_T)[n] + 1)

                    norm_samples(3 * l + n, wait_x)
                    with pool.Fori(0, count // 4) as i:
                        for k in range(4):
                            low(l * LAYER_U + first + 4 * i + k + LEAD, (k + LEAD) % 4)

        @block.scalar
        def _(act):
            def split_hi(at, at2, slot):
                act.wait_ge(raw_full[slot % 2], 16 * (at2 + 1))
                act.wait_ge(wslot_free, at + 1)
                act.copy(w_hi[slot][:], raw[slot % 2][:].rearrange("p (c m) -> p c m", m=P)).then_inc(whi_done, 1)

            def ada_hi(at, nth, s, ring):
                act.wait_ge(ada_full[s], 16 * (nth + 1))
                act.wait_ge(aslot_free, at + 5 - ring)
                act.copy(a_hi[s % 4][:], araw[s][:].rearrange("p (c m) -> p c m", m=512)).then_inc(ahi_done, 1)

            def square(g, m, wait_x):
                wait_x()
                if m >= 3:
                    act.wait_ge(acc_done, 8 * g + m - 2)
                dst = acc if m == 0 else sq[m % 2]
                act.activation(dst[:], x[:, m, :], ACT.Square).then_inc(sq_done, 1)

            def last_squares(g, at):
                act.wait_ge(warm_done, g + 1)
                act.activation(warm[:], eps[:], ACT.Ln).then_inc(warm_done, 1)
                act.wait_ge(acc_done, 8 * g + DC - 3)
                for s in range(2):
                    if at is None:
                        act.wait_ge(x_in, 16)
                    elif s == 0:
                        act.wait_ge(y_free, 2 * at + 5)
                    else:
                        act.wait_ge(x_done, at + 2)
                    act.activation(sq[(DC - 1) % 2][:, cols[s]], x[:, DC - 1, cols[s]], ACT.Square).then_inc(sq_done, 1)

            def norm_rstd(g):
                for s in range(2):
                    act.wait_ge(stat_done, 2 * g + s + 1)
                    act.activation(ln_s[:, cols[s]], bank[4 + s][:, 0:HALF], ACT.Ln,
                                   bias=eps[:, 0:1], scale=1.0 / D).then_inc(ln_done, 1)
                for s in range(2):
                    act.wait_ge(ln_done, 2 * g + s + 1)
                    act.activation(rstd[:, cols[s]], ln_s[:, cols[s]], ACT.Exp, scale=-0.5).then_inc(rstd_done, 1)

            def norm_hi(g):
                for k in range(2 * DC):
                    m, c = k % DC, slice(0, HALF) if k < DC else slice(HALF, SEQ)
                    act.wait_ge(u_done, 2 * DC * g + k + 1)
                    act.activation(n_hi[:, m, c], u[k % 3][:, 0:c.stop - c.start], ACT.Identity,
                                   bias=mod_b[:, m, 0:1]).then_inc(nhi_done, 1)
                    if k == DC:
                        act.wait_ge(us_step, 3 * g + 3)
                        act.copy(n_hi[:, :, SEQ:NT], us[:]).then_inc(nhi_s_done, 1)

            def ffn(l, f):
                for p in range(3):
                    def ada_in(i, q):
                        for k in range(2):
                            ada_hi(4 * i + 2 * q + k + l * ADA_IN * 4 + PBASE[p] * 2 + DEPTH * ADA_PRO * 4,
                                   2 * i + q + l * ADA_IN * 2 + PBASE[p] + ADA_PRO, k, 2)

                    with act.Fori(0, PORT[p] // 2) as i:
                        for q in range(2):
                            if f == 0 and q == 0:
                                ada_in(i, 0)
                            for s in range(2):
                                hp = half_pair(l, f, p, 2 * i + q, s)
                                if s == 0:
                                    act.wait_ge(gate_done, pair(l, f, p, 2 * i + q) + 1)
                                else:
                                    act.wait_ge(wslot_free, unit(l, f, p, 0) + 4 * i + 2 * q + 6)
                                act.wait_ge(gate_free, hp + 1)
                                act.activation(sil[s][:], bank[2 * s][:, 0:HALF], ACT.Silu).then_inc(sil_done, 1)
                            if f == 0 and q == 0:
                                ada_in(i, 1)
                            for k in range(2):
                                split_hi(unit(l, f, p, 0) + 4 * i + 2 * q + k + LEAD,
                                         l * (LAYER_U // 2) + (unit(0, f, p, 0) + LEAD) // 2 + 2 * i + q, 2 * q + k)
                    for m in range(DC):
                        if p == 2:
                            if m >= 1:
                                square(3 * l + 2 * f + 1, m - 1,
                                       lambda: act.wait_ge(x_done, out_tile(l, f, p, m - 1) + 2))
                            if m == DC - 1:
                                last_squares(3 * l + 2 * f + 1, out_tile(l, f, 2, m))
                                norm_rstd(3 * l + 2 * f + 1)
                        k = 2 * PORT[p] + m
                        split_hi(unit(l, f, p, k) + LEAD, l * (LAYER_U // 2) + (unit(0, f, p, k) + LEAD) // 2, k % 4)

            def mix_act(l):
                def feed(k):
                    split_hi(l * LAYER_U + FFN_U + k + LEAD, l * (LAYER_U // 2) + (FFN_U + k + LEAD) // 2, k % 4)

                def tile_done(s, n, k):
                    if s == 0:
                        proj_mm.wait(act, l, n)
                    else:
                        act.wait_ge(wslot_free, l * LAYER_U + FFN_U + k + 5)

                def exp_decay(dst, src):
                    e_done.send(act.activation(dst, src, ACT.Exp, scale=1.0 / GATE_NORM))

                def query_exps(j):
                    scan_done.wait(act, l, j)
                    if j:
                        qk_ready.wait(act, l, 3)
                    exp_decay(e_b[:], gb[:, j, :])
                    dec.wait(act, l, 3 * j)
                    exp_decay(k_dec[:], k_dec[:])

                def key_exps(j):
                    dec.wait(act, l, 3 * j + 1)
                    exp_decay(k_sub[:], k_sub[:])
                    dec.wait(act, l, 3 * j + 2)
                    exp_decay(k_dec[:], k_dec[:])

                act.wait_ge(n_ready, 2 * DC * (3 * l + 1) + 2 * DC)
                act.wait_ge(ns_ready, 3 * l + 2)
                act.dma_start(scan_m[:], scanm).then_inc(scan_in, 16)
                act.dma_start(w_gk[:], gk2_in[bass.ds(l, 1)].rearrange("l r c -> (l r) c")).then_inc(scan_in, 16)
                act.dma_start(s_s[:], s0_in[bass.ds(2 * l, 1)].rearrange("l p i v -> (l p) i v")).then_inc(s_in, 16)
                bank_of = {U_GQ: (2, 3), U_GQ + 1: (6, 7), U_GK: (4, 5), U_GK + 1: (0, 1)}
                for k in range(U_GQ, U_GOG):
                    if k >= 2:
                        feed(k - 2)
                    dst, j = (gq, k - U_GQ) if k < U_GK else (gk, k - U_GK)
                    for s in range(2):
                        tile_done(s, k, k)
                        gqk_out.send(act.mul(dst[:, j, cols[s]], bank[bank_of[k][s]][:, 0:HALF],
                                             GK ** -0.5 if k < U_GK else 1.0))
                for h in range(GH):
                    feed(U_GOG + h - 2)
                    for s in range(2):
                        tile_done(s, 5 + h, U_GOG + h)
                        b = ((2, 3), (6, 7), (4, 5), (0, 1))[h][s]
                        gog_out.send(act.activation(gog[:, h, cols[s]], bank[b][:, 0:HALF], ACT.Silu))
                feed(7)
                feed(8)
                zabs.wait(act, l, 0)
                soft_e.send(act.activation(soft[:], soft[:], ACT.Exp))
                soft_e.last(act, l)
                soft_e.send(act.activation(soft[:], soft[:], ACT.Ln, bias=ones[:, 0:1]))
                feed(9)
                feed(10)
                query_exps(0)
                feed(11)
                for c in range(QL):
                    if c:
                        feed(U_CQ + c - 2)
                    for s in range(2):
                        tile_done(s, 9 + c, U_CQ + c)
                        b = ((3, 6), (7, 4), (5, 0))[c][s]
                        cq_out.send(act.copy(cq[:, c, cols[s]], bank[b][:, 0:HALF]))
                feed(U_CKV - 2)
                key_exps(0)
                feed(U_CKV - 1)
                act.wait_ge(wslot_free, l * LAYER_U + FFN_U + U_CKV + 1 + 5)
                for c in range(QL + KL):
                    if c < QL:
                        cq_out.wait(act, l, 5)
                        src = cq[:, c, :]
                    else:
                        ckv_ev.wait(act, l, 3)
                        src = ckv[:, c - QL, :]
                    if c in (2, 3):
                        lat_mm_sq.wait(act, l, c - 2)
                    elif c == 4:
                        lat_mm.wait(act, l, 1)
                    lsq.send(act.activation(lat_sq[c % 2][:], src, ACT.Square))
                for i in range(4):
                    b = bank[(1, 2, 3, 6)[i]][:, 0:HALF]
                    lat_mm.wait(act, l, i)
                    lrs.send(act.activation(b, b, ACT.Ln, bias=eps[:, 0:1], scale=1.0 / ((QL if i < 2 else KL) * P)))
                for i in range(4):
                    b = bank[(1, 2, 3, 6)[i]][:, 0:HALF]
                    lrs.wait(act, l, i)
                    lrs.send(act.activation(b, b, ACT.Exp, scale=-0.5))

                def block_keys(j):
                    kdt_mm.wait(act, l, 2 * j)
                    zeroed.wait(act, l, 0)
                    if j:
                        ds_mm.wait(act, l, 1)
                    src = bank[GLA_BANKS[j]["KT"]][:, :].rearrange("p (t k) -> p t k", k=P)
                    kdt_out.send(act.copy(kd_t[0:CH, :, 0, :], src[0:CH]))
                    kdt_out.send(act.copy(kd_t[CH:P, :, 1, :], src[CH:P]))

                def out_squares(j):
                    for i, (c0, c1) in enumerate(OSPAN):
                        o_mm.wait(act, l, 3 * j + i)
                        if j:
                            gla_fin.wait(act, l, i)
                        osq.send(act.activation(o_sq[:, c0:c1], bank[GLA_BANKS[j]["O"][i]][:, 0:c1 - c0], ACT.Square))

                block_keys(0)
                query_exps(1)
                key_exps(1)
                out_squares(0)
                feed(16)
                feed(17)
                for c in range(QL):
                    lat_n.wait(act, l, 2 * c + 1)
                    chi_out.send(act.copy(qn_hi[:, c, :], cq[:, c, :]))
                for c in range(KL):
                    lat_n.wait(act, l, 6 + 2 * c + 1)
                    chi_out.send(act.copy(c_hi[:, c, :], ckv[:, c, :]))
                clo.wait(act, l, 2)
                act.dma_start(uk_t[:], ukT[bass.ds(l, 1)].rearrange("l r h c -> (l r) h c")).then_inc(uk_in, 16)
                lat_n.wait(act, l, 9)
                act.dma_start(ckv_out[bass.ds(l, 1)].rearrange("l p c n -> (l p) c n"), ckv[:]).then_inc(kv_st, 16)
                for j in range(2):
                    g = GLA_BANKS[j]
                    if j:
                        block_keys(1)
                        out_squares(1)
                    for i, (c0, c1) in enumerate(OSPAN):
                        ost_mm.wait(act, l, 3 * j + i)
                        if j:
                            o_mul.wait(act, l, i)
                        orn.send(act.activation(o_rs[:, c0:c1], bank[g["ST"][i]][:, 0:c1 - c0], ACT.Ln,
                                                bias=eps[:, 0:1], scale=1.0 / GV))
                    for i, (c0, c1) in enumerate(OSPAN):
                        orn.wait(act, l, 6 * j + i)
                        orn.send(act.activation(o_rs[:, c0:c1], o_rs[:, c0:c1], ACT.Exp, scale=-0.5))
                    ds_out.wait(act, l, 4 * j + 3)
                    at = bass.ds(2 * l + j, 1)
                    act.dma_start(glap_out[at].rearrange("l p v -> (l p) v"), s_p[:, NCH - 1, :]).then_inc(gla_st, 16)
                    act.dma_start(glas_out[at].rearrange("l p i v -> (l p) i v"), s_s[:]).then_inc(gla_st, 16)
                    if j == 0:
                        act.wait_ge(gla_st, 64 * l + 32)
                        act.dma_start(s_s[:], s0_in[bass.ds(2 * l + 1, 1)].rearrange("l p i v -> (l p) i v"))\
                            .then_inc(s_in, 16)
                ds_out.wait(act, l, 7)
                qk_ready.wait(act, l, 7)
                ds_mm.wait(act, l, 7)
                kdt_mm.wait(act, l, 3)
                att_mm.wait(act, l, 3)
                act.dma_start(cs[:], cs_in).then_inc(cs_ld, 16)
                for h in range(MH):
                    if h % 2 == 0:
                        if h < 4:
                            feed(U_UQ + h // 2)
                    for s in range(2):
                        if h % 2 and s:
                            act.wait_ge(wslot_free, l * LAYER_U + FFN_U + U_UQ + h // 2 + 5)
                        else:
                            q_mm.wait(act, l, 3 * (h // 2) + 2 * (h % 2) + s)
                        if h == 0 and s == 0:
                            o_mm.wait(act, l, 5)
                        qh_out.send(act.mul(q_h[0:NOPE, h, cols[s]], bank[QBANKS[h][s]][0:NOPE, 0:HALF], MLA_SCALE))
                    if h == 2:
                        kpe_done.wait(act, l, 1)
                        act.dma_start(kpe_out[bass.ds(l, 1)].rearrange("l r n -> (l r) n"), kg[NOPE:96, :])\
                            .then_inc(kv_st, 16)
                    if h == 7:
                        kpe_copied.send(act.copy(k_h[NOPE:96, :, :], kg[NOPE:96, 0:SEQ].unsqueeze(1)
                                                   .broadcast_to((ROPE, MH, SEQ))))
                def load_keys(i):
                    n = i % NPB
                    if i >= NPB:
                        s_mm.wait(act, l, i - NPB)
                    at = l * NDEC + i
                    for dst, src in ((pk_t[n][:], past_kT[bass.ds(at, 1)].rearrange("a p c n -> (a p) c n")),
                                     (pp_t[n][NOPE:96, :], past_pe[bass.ds(at, 1)].rearrange("a p n -> (a p) n"))):
                        act.dma_start(dst, src).then_inc(keys_in[n], 16)

                def load_values(i):
                    n = i % NPB
                    if i >= NPB:
                        ol_mm.wait(act, l, i - NPB)
                    act.dma_start(pv[n][:], past_v[bass.ds(l * NDEC + i, 1)].rearrange("a p c n -> (a p) c n"))\
                        .then_inc(vals_in[n], 16)

                act.wait_ge(gla_st, 64 * l + 64)
                for i in range(NPB):
                    load_keys(i)
                    load_values(i)
                gla_fin.wait(act, l, 5)
                for h in (2, 3):
                    ohi_out.send(act.copy(o_hi[:, h, :], gog[:, h, :]))
                feed(20)
                for hp in range(4):
                    if hp < 3:
                        k_mm.wait(act, l, hp)
                    else:
                        act.wait_ge(wslot_free, l * LAYER_U + FFN_U + U_UK + 5)
                    b = bank[(1, 4, 2, 3)[hp]]
                    kh_out.send(act.copy(k_h[0:NOPE, 2 * hp, :], b[0:NOPE, :]))
                    kh_out.send(act.copy(k_h[0:NOPE, 2 * hp + 1, :], b[NOPE:P, :]))
                feed(21)
                act.wait_ge(wslot_free, l * LAYER_U + FFN_U + U_UV + 5)
                for h in (0, 1):
                    ohi_out.send(act.copy(o_hi[:, h, :], gog[:, h, :]))
                rope_done.wait(act, l, 15)
                act.dma_start(w_uv[:], wuv_in[bass.ds(l, 1)].rearrange("l p c n -> (l p) c n")).then_inc(uv_in, 16)
                for n in range(4):
                    qa_mm.wait(act, l, n)
                    c, hh = n // 2, n % 2
                    qa_out.send(act.copy(q_abs[:, c, :, 4 * hh * DSEQ:(4 * hh + 4) * DSEQ]
                                         .rearrange("p i (h t) -> p h i t", t=DSEQ),
                                         bank[(1, 4, 2, 3)[n]][:, :].rearrange("p (h i t) -> p h i t", h=4, t=DSEQ)))
                feed(22)
                feed(23)

                for it in range(40 + 6):
                    if it < 40:
                        smp = it < NDEC
                        n, b = it % 4, bank[SBANKS[it % 4]]
                        p_max.wait(act, l, it)
                        if smp:
                            i = it
                            if it >= 4:
                                t_mm.wait(act, l, it - 4)
                            dst = p_s[n][:, 0:PAST]
                            p_exp_a.send(act.activation(dst, b[:, 0:PAST], ACT.Exp, bias=mx[:, n:n + 1],
                                                        accum_out=psums[:, n:n + 1]))
                            p_exp.send(act.activation(p_s[n][:, PAST + DSEQ * i:PAST + DSEQ * (i + 1)],
                                                      b[:, PAST:PAST + DSEQ], ACT.Exp, bias=mx[:, n:n + 1],
                                                      accum_out=psum2[:, n:n + 1]))
                        else:
                            w = P * ((it - NDEC) % 4 + 1)
                            if it >= NDEC + 4:
                                t_mm.wait(act, l, it - 4)
                            if it in (NDEC, NDEC + 2):
                                ol_mm.wait(act, l, 5 if it == NDEC else 6)
                            p_exp.send(act.activation(p_p[n][:, 0:w], b[:, 0:w], ACT.Exp, bias=mx[:, n:n + 1],
                                                      accum_out=psums[:, n:n + 1]))
                    if 2 <= it < 42:
                        jt = it - 2
                        b = bank[TBANKS[jt % 2]]
                        t_mm.wait(act, l, jt)
                        if jt < NDEC:
                            if jt >= 2:
                                ol_mm.wait(act, l, jt - 2)
                            pt_out.send(act.copy(pt_s[jt % 2][:], b[:, 0:3 * P].rearrange("p (c t) -> p c t", t=P)))
                        else:
                            qt = (jt - NDEC) % 4
                            if jt >= NDEC + 3:
                                pv_mm.wait(act, l, jt - NDEC - 3)
                            pt_out.send(act.copy(pt_p[jt % 3][:, 0:qt + 1, :],
                                                 b[:, 0:P * (qt + 1)].rearrange("p (c t) -> p c t", t=P)))
                    if NPB <= it + 4 < NDEC:
                        load_keys(it + 4)
                    if NPB <= it + 1 < NDEC:
                        load_values(it + 1)
                    if it == NDEC + 7:
                        uv_mm.wait(act, l, 0)
                        ohi_out.send(act.copy(o_hi[:, 4:8, SEQ:NT], bank[1][:, :].rearrange("p (c t) -> p c t", t=P)))
                    hp = (it - 5 - NDEC - 7) // 8
                    if it == NDEC + 8 * hp + 12 and 0 <= hp < 4:
                        pv_mm.wait(act, l, 8 * hp + 7)
                        ohi_out.send(act.copy(o_hi[:, 4 + hp, 0:SEQ], bank[(4, 1)[hp % 2]][:, :]))
                for m in range(DC):
                    if m >= 1:
                        square(3 * l + 2, m - 1, lambda: act.wait_ge(x_done, l * OUT_T + 3 * DC + m - 1 + 2))
                    if m < 6:
                        feed(24 + m)
                feed(30)
                last_squares(3 * l + 2, l * OUT_T + 3 * DC + DC - 1)
                norm_rstd(3 * l + 2)
                feed(31)

            act.sem_inc(warm_done, 1)
            act.wait_ge(const_done, 1)
            act.wait_ge(const_in, 80)
            act.activation(c_sil[:], c_in[:], ACT.Silu).then_inc(csil_done, 1)
            for k in range(8):
                ada_hi(k, 0, k, 4)
            for m in range(DC - 1):
                square(0, m, lambda: act.wait_ge(x_in, 16))
            last_squares(0, None)
            for k in range(2):
                split_hi(k, 0, k)
            with act.Fori(1, ADA_PRO) as i:
                for k in range(8):
                    ada_hi(8 * i + k, i, k, 4)
            for k in range(2, LEAD):
                split_hi(k, k // 2, k)
            norm_rstd(0)
            with act.Fori(0, DEPTH) as l:
                norm_hi(3 * l)
                ffn(l, 0)
                norm_hi(3 * l + 1)
                mix_act(l)
                norm_hi(3 * l + 2)
                ffn(l, 1)

        @block.tensor
        def _(pe):
            pe.sem_inc(wslot_free, 4)
            pe.sem_inc(aslot_free, 4)

            def mm3(out, w, c, r_hi, r_lo, first, last):
                pe.matmul(out, w_hi[w][:, c, :], r_hi, start=first, stop=False)
                pe.matmul(out, w_hi[w][:, c, :], r_lo, start=False, stop=False)
                return pe.matmul(out, w_lo[w][:, c, :], r_hi, start=False, stop=last)

            def ada_unit(at, k, s, dst=ADA_ACC):
                pe.wait_ge(alo_done, at + 5)
                for c in range(2):
                    for w in (a_hi, a_lo):
                        mm = pe.matmul(dst[:, :], c_st[:, 2 * k + c, :], w[s][:, c, :],
                                       start=(k == 0 and c == 0 and w is a_hi),
                                       stop=(k == 3 and c == 1 and w is a_lo))
                mm.then_inc(aslot_free, 1)

            def ada_first(t):
                pe.wait_ge(ev_done, t + 1)

            def ada_select(t):
                pe.wait_ge(ev_done, t + 2)
                for j in range(4):
                    mm = pe.matmul(ADA_SEL[:, j * NS:(j + 1) * NS], ev[:, j * P:(j + 1) * P], sel[:],
                                   start=True, stop=True)
                mm.then_inc(sel_done, 1)

            def stats(g):
                for s in range(2):
                    pe.wait_ge(acc_done, 8 * g + 7 + s)
                    pe.matmul(bank[4 + s][:, 0:HALF], ones[:], acc[:, cols[s]], start=True, stop=True)\
                        .then_inc(stat_done, 1)

            def tokens_in(g, s, c):
                if s == 1 and c == 0:
                    pe.wait_ge(ns_ready, g + 1)
                pe.wait_ge(n_ready, 2 * DC * g + s * DC + c + 1)

            def ffn(l, f):
                g = 3 * l + 2 * f
                for p in range(3):
                    def body(i, g=None):
                        for q in range(2):
                            t = DEPTH * ADA_PRO + l * ADA_IN + PBASE[p] // 2 + i
                            for s in range(2):
                                pe.wait_ge(gate_free, half_pair(l, f, p, 2 * i + q, s) + 1)
                                if q == 0 and s == 1:
                                    pe.wait_ge(y_free, 4 + 2 * out_tile(l, f, p, 0))
                                order = [(w, c) for w in range(2) for c in range(DC)]
                                if g is not None and q == 0:
                                    order.sort(key=lambda wc: wc[1])
                                for w, c in order:
                                    if s == 0 and c == 0:
                                        pe.wait_ge(wlo_done, unit(l, f, p, 0) + 4 * i + 2 * q + w + 1)
                                    if g is not None and q == 0 and w == 0:
                                        tokens_in(g, s, c)
                                    mm = mm3(bank[2 * s + w][:, 0:HALF], 2 * q + w, c, n_hi[:, c, cols[s]],
                                             n_lo[:, c, cols[s]], c == 0, c == DC - 1)
                                    if c == DC - 1 and s == 1:
                                        mm.then_inc(wslot_free, 1)
                                    elif c == DC - 1 and w == 1:
                                        mm.then_inc(gate_done, 1)
                                if s == 1 - q and f == 0:
                                    if q == 0:
                                        ada_first(t)
                                    for k in range(2):
                                        ada_unit(4 * t + 2 * q + k, 2 * q + k, k)
                            if f == 0 and q == 1:
                                ada_select(t)
                    if p == 0:
                        body(0, g)
                    with pe.Fori(int(p == 0), PORT[p] // 2) as i:
                        body(i)
                    for m in range(DC):
                        slot = (2 * PORT[p] + m) % 4
                        pe.wait_ge(wlo_done, unit(l, f, p, 2 * PORT[p] + m) + 1)
                        for s in range(2):
                            pe.wait_ge(y_free, 2 * out_tile(l, f, p, m) + s + 1)
                            dst = bank[4 + s] if m % 2 == 0 else bank[2 + s]
                            for c in range(PORT[p]):
                                if m == 0 and c in (0, PORT[p] - 1):
                                    cc = PORT[p] - 2 if c == 0 else PORT[p] - 1
                                    pe.wait_ge(h_ready, half_pair(l, f, p, cc, s) + 3)
                                mm = mm3(dst[:, 0:HALF], slot, c, h_hi[:, c, cols[s]], h_lo[:, c, cols[s]],
                                         c == 0, c == PORT[p] - 1)
                            mm.then_inc(wslot_free if s else out_done, 1)


            def mix_pe(l):
                def unit_in(k):
                    pe.wait_ge(wlo_done, l * LAYER_U + FFN_U + k + 1)

                def tile(k, n, chunks, first, r_hi, r_lo, banks, waits, signal_done):
                    slot = k % 4
                    for s in range(2):
                        for sg, w in waits[s]:
                            sg.wait(pe, l, w)
                        for c in range(chunks):
                            mm = mm3(bank[banks[s]][:, 0:HALF], slot, first + c, r_hi[:, c, cols[s]], r_lo[:, c, cols[s]],
                                     c == 0, c == chunks - 1)
                        if s == 1 and first + chunks == n:
                            mm.then_inc(wslot_free, 1)
                        else:
                            signal_done.send(mm)

                def proj(k, banks, waits):
                    unit_in(k)
                    tile(k, DC, DC, 0, n_hi, n_lo, banks, waits, proj_mm)

                no = ((), ())
                for k in (U_S, U_GQ):
                    unit_in(k)
                for s in range(2):
                    for c in range(DC):
                        tokens_in(3 * l + 1, s, c)
                        for k in (U_S, U_GQ):
                            mm = mm3(bank[2 * k + s][:, 0:HALF], k % 4, c, n_hi[:, c, cols[s]], n_lo[:, c, cols[s]],
                                     c == 0, c == DC - 1)
                            if c == DC - 1:
                                mm.then_inc(wslot_free, 1) if s else proj_mm.send(mm)
                proj(U_GQ + 1, (6, 7), no)
                proj(U_GK, (4, 5), no)
                proj(U_GK + 1, (0, 1), (((s_out, 0),), ((s_out, 1),)))
                proj(U_GOG, (2, 3), (((gqk_out, 0),), ((gqk_out, 1),)))
                proj(U_GOG + 1, (6, 7), (((gqk_out, 2),), ((gqk_out, 3),)))
                proj(U_GOG + 2, (4, 5), (((gqk_out, 4),), ((gqk_out, 5),)))
                proj(U_GOG + 3, (0, 1), (((gqk_out, 6),), ((gqk_out, 7),)))
                pe.wait_ge(scan_in, 32 * l + 32)
                for j in range(2):
                    for s in range(2):
                        gog_out.wait(pe, l, 2 * j + s)
                        z_mm.send(pe.matmul(bank[((2, 3), (6, 7))[j][s]][:, 0:HALF], w_gk[:, j * P:(j + 1) * P],
                                            kg[0:GR, cols[s]], start=True, stop=True))
                for q in range(4):
                    unit_in(U_GV + q)
                    slot = (U_GV + q) % 4
                    for t in range(5):
                        if q == 0:
                            sg, w = ((gog_out, 4), (gog_out, 5), (gog_out, 6), (gog_out, 7), (z_out, 0))[t]
                            sg.wait(pe, l, w)
                        out = bank[(4, 5, 0, 1, 2)[t]]
                        tok = slice(t * P, (t + 1) * P)
                        for c in range(2):
                            wh = w_hi[slot][:, 4 * c:4 * c + 4, :]
                            wl = w_lo[slot][:, 4 * c:4 * c + 4, :]
                            pe.matmul(out[:, :], n_hi[:, 2 * q + c, tok], wh, start=(q == 0 and c == 0), stop=False)
                            pe.matmul(out[:, :], n_hi[:, 2 * q + c, tok], wl, start=False, stop=False)
                            mm = pe.matmul(out[:, :], n_lo[:, 2 * q + c, tok], wh, start=False,
                                           stop=(q == 3 and c == 1))
                        if t == 4:
                            mm.then_inc(wslot_free, 1)
                        elif q == 3:
                            gv_mm.send(mm)
                proj(U_CQ, (3, 6), (((z_out, 1),), ((z_out, 2),)))
                proj(U_CQ + 1, (7, 4), (((z_out, 3),), ((gv_out, 0),)))
                proj(U_CQ + 2, (5, 0), (((gv_out, 1),), ((gv_out, 2),)))
                proj(U_CKV, (1, 2), (((gv_out, 3),), ((gv_out, 4),)))
                proj(U_CKV + 1, (3, 6), (((cq_out, 0),), ((cq_out, 1),)))

                def gla_att(j):
                    b = GLA_BANKS[j]
                    qk_ready.wait(pe, l, 4 * j + 1)
                    zeroed.wait(pe, l, 0)
                    if j == 0:
                        cq_out.wait(pe, l, 4)
                    else:
                        kdt_out.wait(pe, l, 1)
                        ds_out.wait(pe, l, 3)
                    for n in range(NCH):
                        for i in range(NSUB):
                            ln = SUB * (i + 1)
                            at = NCH * SUB * i * (i + 1) // 2 + n * ln
                            r0, c0 = CH * (n % 2), (n // 2) * P + i * SUB
                            dst = bank[b["A"]][r0:r0 + ln, :].rearrange("p (n h t) -> p n h t", n=4, h=2)[
                                :, n // 2, :, i * SUB:(i + 1) * SUB]
                            t0 = n * CH + i * SUB
                            mm = pe.matmul(dst, k_sub[:, at:at + ln], q_sub[:, :, t0:t0 + SUB], start=True, stop=True)
                    att_mm.send(mm)
                    att_mm.send(pe.matmul(bank[b["AS"]][:, 0:2 * P], k_sub[:, KHAT[NSUB]:KHAT[NSUB] + P],
                                          q_sub[:, :, SEQ:NT], start=True, stop=True))

                def gla_keys(j):
                    b = GLA_BANKS[j]
                    qk_ready.wait(pe, l, 4 * j + 2)
                    if j == 0:
                        cq_out.wait(pe, l, 5)
                    else:
                        orn.wait(pe, l, 0)
                    for t in range(4):
                        mm = pe.transpose(bank[b["KT"]][:, t * P:(t + 1) * P], k_dec[:, t * P:(t + 1) * P], ident[:])
                    kdt_mm.send(mm)
                    k, o = b["KTS"]
                    if j:
                        o_mul.wait(pe, l, 0)
                    kdt_mm.send(pe.transpose(bank[k][:, o:o + P], k_dec[:, SEQ:NT], ident[:]))

                def gla_states(j):
                    b = GLA_BANKS[j]
                    kdt_out.wait(pe, l, 2 * j + 1)
                    gv_out.wait(pe, l, 4)
                    for q in range(2):
                        if j == 0:
                            lat_n.wait(pe, l, (4, 5)[q])
                        else:
                            orn.wait(pe, l, (1, 2)[q])
                        for n in range(4 * q, 4 * q + 4):
                            for hh in range(2):
                                h = 2 * j + hh
                                mm = pe.matmul(bank[b["DS"][q]][GK * hh:GK * hh + GK, (n % 4) * GV:(n % 4 + 1) * GV],
                                               kd_t[:, n // 2, n % 2, GK * hh:GK * hh + GK],
                                               v_g[:, n // 2, h * GV:(h + 1) * GV], start=True, stop=True)
                        ds_mm.send(mm)
                    kds_out.wait(pe, l, j)
                    for q in range(2):
                        if j == 0:
                            lat_n.wait(pe, l, 9)
                        elif q == 1:
                            o_mul.wait(pe, l, 0)
                        for i in range(4 * q, 4 * q + 4):
                            for hh in range(2):
                                h = 2 * j + hh
                                mm = pe.matmul(bank[b["DSS"][q]][GK * hh:GK * hh + GK, (i % 4) * GV:(i % 4 + 1) * GV],
                                               kd_s[:, i, GK * hh:GK * hh + GK], v_g[:, 4, h * GV:(h + 1) * GV],
                                               start=True, stop=True)
                        ds_mm.send(mm)

                def gla_out(j):
                    b = GLA_BANKS[j]
                    qk_ready.wait(pe, l, 4 * j + 3)
                    for q in range(2):
                        att_out.wait(pe, l, 2 * j)
                        ds_out.wait(pe, l, 4 * j + q)
                        if j:
                            o_mul.wait(pe, l, 1 + q)
                        out = bank[b["O"][q]]
                        both = out[:, :].rearrange("p (h t) -> p h t", h=2)
                        first = True
                        for n in (2 * q, 2 * q + 1):
                            for hh in range(2):
                                h = 2 * j + hh
                                c0 = (n % 2) * P
                                pe.matmul(both[:, hh, c0:c0 + P], v_g[:, n, h * GV:(h + 1) * GV], att[:, n, hh, :],
                                          start=first, stop=False, skip_group_check=True)
                                first = False
                        for n in range(max(4 * q, 1), 4 * q + 4):
                            c0 = (n % 4) * CH
                            mm = pe.matmul(both[:, :, c0:c0 + CH], s_p[:, n - 1, :], q_blk[:, :, n * CH:(n + 1) * CH],
                                           start=False, stop=True, skip_group_check=True)
                        o_mm.send(mm)
                    att_out.wait(pe, l, 2 * j + 1)
                    pe.wait_ge(s_in, 32 * l + 16 * j + 16)
                    if j == 0:
                        kds_out.wait(pe, l, 0)
                    both = bank[b["O"][2]][:, 0:2 * P].rearrange("p (h t) -> p h t", h=2)
                    for hh in range(2):
                        h = 2 * j + hh
                        pe.matmul(both[:, hh, :], v_g[:, 4, h * GV:(h + 1) * GV], att[:, 4, hh, :],
                                  start=(hh == 0), stop=False, skip_group_check=True)
                    for i in range(NDEC):
                        mm = pe.matmul(both[:, :, i * DSEQ:(i + 1) * DSEQ], s_s[:, i, :],
                                       q_blk[:, :, SEQ + i * DSEQ:SEQ + (i + 1) * DSEQ],
                                       start=False, stop=True, skip_group_check=True)
                    o_mm.send(mm)

                def gla_stats(j):
                    b = GLA_BANKS[j]
                    for i, (c0, c1) in enumerate(OSPAN):
                        osq.wait(pe, l, 3 * j + i)
                        if j == 0:
                            ds_out.wait(pe, l, (0, 1, 2)[i])
                        else:
                            ds_out.wait(pe, l, (4, 5, 5)[i])
                            att_out.wait(pe, l, 3)
                            kds_out.wait(pe, l, 1)
                        ost_mm.send(pe.matmul(bank[b["ST"][i]][:, 0:c1 - c0], ones[:], o_sq[:, c0:c1],
                                              start=True, stop=True))

                gla_att(0)
                gla_keys(0)
                for c in range(QL + KL):
                    lsq.wait(pe, l, c)
                    if c == 0:
                        ckv_ev.wait(pe, l, 3)
                    first, last, b0 = (c == 0, c == QL - 1, (1, 2)) if c < QL else (c == QL, c == QL + KL - 1, (3, 6))
                    for s in range(2):
                        mm = pe.matmul(bank[b0[s]][:, 0:HALF], ones[:], lat_sq[c % 2][:, cols[s]], start=first, stop=last)
                        if last:
                            lat_mm.send(mm)
                    if c < 2:
                        lat_mm_sq.send(mm)
                gla_states(0)
                gla_out(0)
                gla_stats(0)
                gla_att(1)
                gla_keys(1)
                gla_states(1)
                gla_out(1)
                gla_stats(1)

                for h in range(MH):
                    k = U_UQ + h // 2
                    if h % 2 == 0:
                        unit_in(k)
                    if h == 0:
                        clo.wait(pe, l, 2)
                    w = {0: ((ds_out, 6), (ds_out, 7)), 1: ((orn, 6), (orn, 7)), 2: ((orn, 8), (o_mul, 3)),
                         3: ((o_mul, 4), (o_mul, 5))}.get(h)
                    if w:
                        waits = ((w[0],), (w[1],))
                    else:
                        waits = tuple(((qh_out, 2 * (h - 4) + s), (rope_done, 2 * (h - 4) + s)) for s in range(2))
                    tile(k, 6, QL, 3 * (h % 2), qn_hi, qn_lo, QBANKS[h], waits, q_mm)
                unit_in(U_UK)
                clo.wait(pe, l, 4)
                for hp in range(4):
                    i = (8, 9, 10, 11)[hp]
                    qh_out.wait(pe, l, i)
                    rope_done.wait(pe, l, i)
                    for c in range(KL):
                        mm = mm3(bank[(1, 4, 2, 3)[hp]][:, :], U_UK % 4, KL * hp + c, c_hi[:, c, 0:SEQ], c_lo[:, c, 0:SEQ],
                                 c == 0, c == KL - 1)
                    mm.then_inc(wslot_free, 1) if hp == 3 else k_mm.send(mm)
                unit_in(U_UV)
                slot = U_UV % 4
                for t in range(4):
                    i = (12, 13, 14, 15)[t]
                    qh_out.wait(pe, l, i)
                    rope_done.wait(pe, l, i)
                    out = bank[(6, 5, 7, 0)[t]]
                    for c in range(KL):
                        wh = w_hi[slot][:, 4 * c:4 * c + 4, :]
                        wl = w_lo[slot][:, 4 * c:4 * c + 4, :]
                        tok = slice(t * P, (t + 1) * P)
                        pe.matmul(out[:, :], c_hi[:, c, tok], wh, start=(c == 0), stop=False)
                        pe.matmul(out[:, :], c_hi[:, c, tok], wl, start=False, stop=False)
                        mm = pe.matmul(out[:, :], c_lo[:, c, tok], wh, start=False, stop=(c == KL - 1))
                    mm.then_inc(wslot_free, 1) if t == 3 else v_mm.send(mm)
                vm_out.wait(pe, l, 0)
                for c in range(KL):
                    mm = pe.transpose(bank[6][:, c * P:(c + 1) * P], ckv[:, c, SEQ:NT], ident[:])
                cn_mm.send(mm)
                pe.wait_ge(uk_in, 16 * l + 16)
                for n in range(4):
                    kh_out.wait(pe, l, 2 * n + 1)
                    c, hh = n // 2, n % 2
                    for h in range(4 * hh, 4 * hh + 4):
                        mm = pe.matmul(bank[(1, 4, 2, 3)[n]][:, (h % 4) * P:(h % 4 + 1) * P],
                                       uk_t[:, h, c * P:(c + 1) * P], q_h[0:NOPE, h, SEQ:NT], start=True, stop=True)
                    qa_mm.send(mm)

                def scores(it):
                    b = bank[SBANKS[it % 4]]
                    if it >= 4:
                        p_exp.wait(pe, l, it - 4)
                    else:
                        sg, w = ((cn_out, 0), (vm_out, 1), (qa_out, 2), (qa_out, 3))[it]
                        sg.wait(pe, l, w)
                        qa_out.wait(pe, l, 3)
                    if it < NDEC:
                        n, i = it % NPB, it
                        rounds = len(range(n, NDEC, NPB))
                        pe.wait_ge(keys_in[n], 32 * (rounds * l + i // NPB + 1))
                        new = slice(SEQ + DSEQ * i, SEQ + DSEQ * (i + 1))
                        for c in range(KL):
                            q = q_abs[:, c, i, :]
                            pe.matmul(b[:, 0:PAST], q, pk_t[n][:, c, :], start=(c == 0), stop=False,
                                      skip_group_check=True)
                            pe.matmul(b[:, PAST:PAST + DSEQ], q, ckv[:, c, new], start=False, stop=False,
                                      skip_group_check=True)
                        qpe_out.wait(pe, l, 0)
                        q = q_pe[NOPE:96, i, :]
                        pe.matmul(b[:, 0:PAST], q, pp_t[n][NOPE:96, :], start=False, stop=True, skip_group_check=True)
                        s_mm.send(pe.matmul(b[:, PAST:PAST + DSEQ], q, kg[NOPE:96, new], start=False, stop=True,
                                            skip_group_check=True))
                    else:
                        h, qt = (it - NDEC) // 4, (it - NDEC) % 4
                        if it == NDEC:
                            kpe_copied.wait(pe, l, 0)
                        w = P * (qt + 1)
                        pe.matmul(b[:, 0:w], q_h[:, h, qt * P:(qt + 1) * P], k_h[:, h, 0:w], start=True, stop=False,
                                  skip_group_check=True)
                        s_mm.send(pe.matmul(b[:, w - CH:w], mrow[0:1, 0:P], mrow[0:1, P:P + CH], start=False, stop=True,
                                            skip_group_check=True))

                def transposes(it):
                    b = bank[TBANKS[it % 2]]
                    p_norm.wait(pe, l, it)
                    if it >= 2:
                        pt_out.wait(pe, l, it - 2)
                    else:
                        vm_out.wait(pe, l, 2 + it)
                    src, n = (p_s[it % 4], 3) if it < NDEC else (p_p[it % 4], (it - NDEC) % 4 + 1)
                    for c in range(n):
                        mm = pe.transpose(b[:, c * P:(c + 1) * P], src[:, c * P:(c + 1) * P], ident[:])
                    t_mm.send(mm)

                def values(it):
                    pt_out.wait(pe, l, it)
                    if it < NDEC:
                        b = bank[(1, 4)[it % 2]]
                        if it >= 2:
                            ol_out.wait(pe, l, it - 2)
                        else:
                            qa_out.wait(pe, l, it)
                            cn_out.wait(pe, l, 0)
                        n = it % NPB
                        pe.wait_ge(vals_in[n], 16 * (len(range(n, NDEC, NPB)) * l + it // NPB + 1))
                        for c in range(KL):
                            for k in range(3):
                                w = pv[it % NPB][:, k, c * P:(c + 1) * P] if k < 2 else cn_t[:, c * P:(c + 1) * P]
                                mm = pe.matmul(b[:, c * P:(c + 1) * P], w, pt_s[it % 2][:, k, :],
                                               start=(k == 0), stop=(k == 2))
                        ol_mm.send(mm)
                        return
                    h, qt = (it - NDEC) // 4, (it - NDEC) % 4
                    hp, r0 = h // 2, MV * (h % 2)
                    if h % 2 == 0 and qt == 0:
                        sg, w = ((ol_out, 7), (olo, 4), (olo, 5), (olo, 6))[hp]
                        sg.wait(pe, l, w)
                    for k in range(qt + 1):
                        mm = pe.matmul(bank[(4, 1)[hp % 2]][r0:r0 + MV, qt * P:(qt + 1) * P],
                                       v_m[:, k, h * MV:(h + 1) * MV], pt_p[it % 3][:, k, :], start=(k == 0), stop=(k == qt))
                    pv_mm.send(mm)
                    return mm

                for it in range(40 + 4):
                    if 3 <= it < 43:
                        transposes(it - 3)
                    if it >= 4:
                        values(it - 4)
                    if it < 40:
                        scores(it)
                    if it == NDEC + 5:
                        ol_out.wait(pe, l, 7)
                        pe.wait_ge(uv_in, 16 * l + 16)
                        for h in range(MH):
                            for c in range(KL):
                                mm = pe.matmul(bank[1][MV * (h % 2):MV * (h % 2) + MV, (h // 2) * P:(h // 2 + 1) * P],
                                               w_uv[:, c, h * MV:(h + 1) * MV], o_lat[:, c, h, :],
                                               start=(c == 0), stop=(c == KL - 1))
                        uv_mm.send(mm)
                for m in range(DC):
                    unit_in(U_OUT + m)
                    if m == 0:
                        olo.wait(pe, l, 8)
                        p_exp.wait(pe, l, 39)
                    for s in range(2):
                        at = l * OUT_T + 3 * DC + m
                        pe.wait_ge(y_free, 2 * at + s + 1)
                        dst = bank[4 + s] if m % 2 == 0 else bank[2 + s]
                        for c in range(DC):
                            mm = mm3(dst[:, 0:HALF], (U_OUT + m) % 4, c, o_hi[:, c, cols[s]], o_lo[:, c, cols[s]],
                                     c == 0, c == DC - 1)
                        mm.then_inc(wslot_free if s else out_done, 1)

            pe.wait_ge(const_done, 1)
            pe.wait_ge(const_in, 80)
            pe.wait_ge(cst_done, 3)

            def ada_pair(i, start=False):
                for n in range(DEPTH):
                    t = DEPTH * i + n
                    for k in range(4):
                        ada_unit(4 * t + k, k, k, ADA_FIRST[n])
                        if k == 1 and not (start and n == 0):
                            ada_select(t - 1)

            ada_pair(0, start=True)
            with pe.Fori(1, ADA_PRO) as i:
                ada_pair(i)
            ada_select(DEPTH * ADA_PRO - 1)
            pe.wait_ge(cst_in, 16 * 6)
            stats(0)
            with pe.Fori(0, DEPTH) as l:
                ffn(l, 0)
                stats(3 * l + 1)
                mix_pe(l)
                stats(3 * l + 2)
                ffn(l, 1)
                stats(3 * l + 3)

        @block.vector
        def _(dve):
            dve.sem_inc(alo_done, 4)
            dve.sem_inc(gate_free, 2)
            dve.sem_inc(h_ready, 2)
            dve.sem_inc(y_free, 4)
            dve.sem_inc(x_done, 1)
            dve.sem_inc(ev_done, 1)

            def ada_lo(at, s):
                dve.wait_ge(ahi_done, at + 1)
                dve.tensor_tensor(a_lo[s % 4][:], araw[s][:].rearrange("p (c m) -> p c m", m=512),
                                  a_hi[s % 4][:].bitcast(F32), ALU.subtract).then_inc(alo_done, 1)

            def ada_evict(t, src=ADA_ACC):
                dve.wait_ge(aslot_free, 4 * t + 8)
                dve.tensor_copy(ev[:], src[0:2 * NS, :]).then_inc(ev_done, 1)

            def ada_bias(t, l, f4):
                dve.wait_ge(sel_done, t + 1)
                dve.tensor_tensor(mods[:, l, f4, :], ADA_SEL[:, 0:4 * NS].rearrange("p (j n) -> p j n", n=NS),
                                  b_ada[:, l, f4].unsqueeze(2).broadcast_to((P, 4, NS)), ALU.add)\
                    .then_inc(mod_done, 1)

            def mod_ab(l, k, ready):
                dve.wait_ge(mod_done, ready)
                dve.scalar_tensor_tensor(out=mod_a[:], in0=mods[:, l, 24 * k + 8:24 * k + 16, :], scalar=1.0,
                                         in1=ln_g[:, l, k, :].unsqueeze(2).broadcast_to((P, DC, NS)),
                                         op0=ALU.add, op1=ALU.mult).then_inc(mab_done, 1)
                dve.tensor_copy(mod_b[:], mods[:, l, 24 * k:24 * k + 8, :]).then_inc(mab_done, 1)

            def norm_apply(l, k, ready):
                g = 3 * l + k
                if k == 0:
                    mod_ab(l, k, ready)
                dve.tensor_scalar(mod_g[:], mods[:, l, 24 * k + 16:24 * k + 24, :], 1.0, 1.0 if k == 1 else 0.5,
                                  ALU.add, ALU.mult).then_inc(modg_done, 1)
                dve.wait_ge(mab_done, 2 * g + 2)

                def span(k):
                    return slice(0, HALF) if k < DC else slice(HALF, SEQ)

                def lo(k):
                    c = span(k)
                    dve.wait_ge(nhi_done, 2 * DC * g + k + 1)
                    dve.scalar_tensor_tensor(out=n_lo[:, k % DC, c], in0=u[k % 3][:, 0:c.stop - c.start],
                                             scalar=mod_b[:, k % DC, 0:1], in1=n_hi[:, k % DC, c].bitcast(F32),
                                             op0=ALU.add, op1=ALU.subtract).then_inc(n_ready, 1)

                for k2 in range(2 * DC + 1):
                    if k2 < 2 * DC:
                        c = span(k2)
                        if k2 % DC == 0:
                            dve.wait_ge(rstd_done, 2 * g + k2 // DC + 1)
                        if k2 >= 3:
                            dve.wait_ge(n_ready, 2 * DC * g + k2 - 2)
                        dve.scalar_tensor_tensor(out=u[k2 % 3][:, 0:c.stop - c.start], in0=x[:, k2 % DC, c],
                                                 scalar=mod_a[:, k2 % DC, 0:1], in1=rstd[:, c],
                                                 op0=ALU.mult, op1=ALU.mult).then_inc(u_done, 1)
                    if k2 >= 1:
                        lo(k2 - 1)
                    if k2 == DC + 1:
                        dve.wait_ge(nhi_s_done, g + 1)
                        dve.tensor_tensor(n_lo[:, :, SEQ:NT], us[:], n_hi[:, :, SEQ:NT].bitcast(F32), ALU.subtract)\
                            .then_inc(ns_ready, 1)

            def residual(at, m, y0, y1, last_unit, between=()):
                dve.wait_ge(out_done, at + 1)
                dve.scalar_tensor_tensor(out=x[:, m, cols[0]], in0=y0[:, 0:HALF], scalar=mod_g[:, m, 0:1],
                                         in1=x[:, m, cols[0]], op0=ALU.mult, op1=ALU.add).then_inc(y_free, 1)
                for add in between:
                    add()
                dve.wait_ge(wslot_free, last_unit + 5)
                dve.scalar_tensor_tensor(out=x[:, m, HALF:SEQ], in0=y1[:, 0:HP1], scalar=mod_g[:, m, 0:1],
                                         in1=x[:, m, HALF:SEQ], op0=ALU.mult, op1=ALU.add)
                dve.wait_ge(x_done, at + 1)
                dve.tensor_tensor(ytmp[:], y1[:, HP1:HALF].rearrange("p (i t) -> p i t", t=DSEQ),
                                  mod_g[:, m, 1:NS].unsqueeze(2).broadcast_to((P, NDEC, DSEQ)), ALU.mult)\
                    .then_inc(y_free, 1)
                dve.wait_ge(y_free, 2 * at + 6)
                xs = x[:, m, SEQ:NT].rearrange("p (i t) -> p i t", t=DSEQ)
                dve.tensor_tensor(xs, xs, ytmp[:], ALU.add).then_inc(x_done, 1)

            def add_square(g, m):
                dve.wait_ge(sq_done, 9 * g + m + 1)
                if m > 1:
                    dve.wait_ge(acc_done, 8 * g + m - 1)
                dve.tensor_tensor(acc[:], acc[:], sq[m % 2][:], ALU.add).then_inc(acc_done, 1)

            def add_last_square(g, s):
                dve.wait_ge(sq_done, 9 * g + DC + s)
                dve.wait_ge(acc_done, 8 * g + DC - 2 + s)
                dve.tensor_tensor(acc[:, cols[s]], acc[:, cols[s]], sq[(DC - 1) % 2][:, cols[s]], ALU.add)\
                    .then_inc(acc_done, 1)

            def ffn(l, f):
                for p in range(3):
                    with dve.Fori(0, PORT[p] // 2) as i:
                        t = DEPTH * ADA_PRO + l * ADA_IN + PBASE[p] // 2 + i
                        for q in range(2):
                            if f == 0:
                                for k in range(2):
                                    ada_lo(4 * t + 2 * q + k, k)
                            for s in range(2):
                                if f == 0 and q == 1 and s == 1:
                                    ada_evict(t)
                                hp = half_pair(l, f, p, 2 * i + q, s)
                                dve.wait_ge(sil_done, hp + 1)
                                dve.wait_ge(h_ready, hp + 1)
                                dve.tensor_tensor(hf[s][:], sil[s][:], bank[2 * s + 1][:, 0:HALF], ALU.mult)\
                                    .then_inc(gate_free, 1)
                                dve.wait_ge(gate_free, hp + 3)
                                hid = bass.ds(2 * i + q, 1)
                                dve.tensor_copy(h_hi[:, hid, cols[s]], hf[s][:].unsqueeze(1)).then_inc(hhi_done, 1)
                                dve.wait_ge(hhi_done, hp + 1)
                                dve.tensor_tensor(h_lo[:, hid, cols[s]], hf[s][:].unsqueeze(1),
                                                  h_hi[:, hid, cols[s]].bitcast(F32), ALU.subtract)\
                                    .then_inc(h_ready, 1)
                        if f == 0:
                            ada_bias(t, l, bass.ds(4 * ADA_PRO + 4 * (PBASE[p] // 2) + 4 * i, 4))
                    if p == 0:
                        dve.wait_ge(modg_done, 3 * l + 2 * f + 1)
                    if p == 2 and f == 0:
                        mod_ab(l, 1, DEPTH * ADA_PRO + ADA_IN + l * ADA_IN)
                    for m in range(DC):
                        y = bank[4:6] if m % 2 == 0 else bank[2:4]
                        g = 3 * l + 2 * f + 1
                        residual(out_tile(l, f, p, m), m, *y, unit(l, f, p, 2 * PORT[p] + m),
                                 (lambda: add_square(g, DC - 2), lambda: add_last_square(g, 0))
                                 if p == 2 and m == DC - 1 else ())
                        if p == 2 and 2 <= m < DC - 1:
                            add_square(g, m - 1)
                add_last_square(g, 1)


            def mix_dve(l):
                def own(ins):
                    dv.send(ins)
                    dv.last(dve, l)

                def used(k):
                    dve.wait_ge(wslot_free, l * LAYER_U + FFN_U + k + 5)

                own(dve.tensor_copy(gain[:].unsqueeze(1), gains[:, bass.ds(l, 1), :]))
                dve.wait_ge(n_ready, 2 * DC * (3 * l + 1) + 2 * DC)
                dve.wait_ge(ns_ready, 3 * l + 2)
                for t in (q_sub, q_blk):
                    dve.memset(t[GK:P, 0, :], 0.0)
                    dve.memset(t[0:GK, 1, :], 0.0)
                dve.memset(att[:], 0.0)
                zeroed.send(dve.memset(kd_t[:], 0.0))
                for s in range(2):
                    if s == 0:
                        proj_mm.wait(dve, l, 0)
                    else:
                        used(U_S)
                    s_out.send(dve.tensor_copy(kg[:, cols[s]], bank[s][:, 0:HALF]))
                for j in range(2):
                    for s in range(2):
                        z_mm.wait(dve, l, 2 * j + s)
                        z_out.send(dve.tensor_scalar(gb[:, j, cols[s]], bank[((2, 3), (6, 7))[j][s]][:, 0:HALF],
                                                     gain[:, j:j + 1], None, ALU.add))
                z_out.last(dve, l)
                own(dve.tensor_scalar(soft[:], gb[:], -1.0, None, ALU.mult))
                zabs.send(dve.tensor_tensor(soft[:], gb[:], soft[:], ALU.min))
                soft_e.wait(dve, l, 1)
                own(dve.scalar_tensor_tensor(out=gb[:], in0=gb[:], scalar=0.0, in1=soft[:], op0=ALU.min,
                                             op1=ALU.subtract))
                dve.wait_ge(scan_in, 32 * l + 32)
                for j in range(2):
                    scan_done.send(dve.tensor_tensor_scan(gb[:, j, :], scan_m[:], gb[:, j, :], 0.0, ALU.mult, ALU.add))
                scan_done.last(dve, l)

                def decays_in(j):
                    b = gb[:, j, :]
                    if j:
                        kdt_mm.wait(dve, l, 1)
                        att_mm.wait(dve, l, 1)
                    v = b.rearrange("p (n t) -> p n t", t=SUB)
                    ref = v[:, :, SUB // 2 - 1:SUB // 2]
                    dec.send(dve.tensor_tensor(k_dec[:].rearrange("p (n t) -> p n t", t=SUB), v,
                                               ref.broadcast_to((P, NT // SUB, SUB)), ALU.subtract))
                    blk = b[:, 0:SEQ].rearrange("p (n t) -> p n t", t=CH)
                    for i in range(NSUB):
                        ln, r = SUB * (i + 1), SUB * i + SUB // 2 - 1
                        dst = k_sub[:, KHAT[i]:KHAT[i + 1]].rearrange("p (n t) -> p n t", t=ln)
                        dve.tensor_tensor(dst, blk[:, :, r:r + 1].broadcast_to((P, NCH, ln)), blk[:, :, 0:ln],
                                          ALU.subtract)
                    sv = b[:, SEQ:NT].rearrange("p (n t) -> p n t", t=DSEQ)
                    dec.send(dve.tensor_tensor(k_sub[:, KHAT[NSUB]:KHAT[NSUB] + P].rearrange("p (n t) -> p n t", t=DSEQ),
                                               sv[:, :, SUB // 2 - 1:SUB // 2].broadcast_to((P, NDEC, DSEQ)), sv,
                                               ALU.subtract))

                def block_queries(j):
                    e_done.wait(dve, l, 4 * j)
                    if j:
                        ds_out.wait(dve, l, 3)
                        o_mm.wait(dve, l, 2)
                    dve.tensor_copy(elast[:, 0:NCH].unsqueeze(2),
                                    e_b[:, 0:SEQ].rearrange("p (n t) -> p n t", t=CH)[:, :, CH - 1:CH])
                    dve.tensor_copy(elast[:, NCH:NCH + NDEC].unsqueeze(2),
                                    e_b[:, SEQ:NT].rearrange("p (n t) -> p n t", t=DSEQ)[:, :, DSEQ - 1:DSEQ])
                    zeroed.wait(dve, l, 0)
                    dve.tensor_tensor(q_blk[0:GK, 0, :], gq[0:GK, j, :], e_b[0:GK, :], ALU.mult)
                    qk_ready.send(dve.tensor_tensor(q_blk[GK:P, 1, :], gq[GK:P, j, :], e_b[GK:P, :], ALU.mult))

                def decays_out(j):
                    b = gb[:, j, :]
                    blk = b[:, 0:SEQ].rearrange("p (n t) -> p n t", t=CH)
                    sv = b[:, SEQ:NT].rearrange("p (n t) -> p n t", t=DSEQ)
                    zeroed.wait(dve, l, 0)
                    e_done.wait(dve, l, 4 * j + 1)
                    dve.tensor_tensor(q_sub[0:GK, 0, :], gq[0:GK, j, :], k_dec[0:GK, :], ALU.mult)
                    qk_ready.send(dve.tensor_tensor(q_sub[GK:P, 1, :], gq[GK:P, j, :], k_dec[GK:P, :], ALU.mult))
                    qk_ready.last(dve, l)
                    dve.tensor_tensor(k_dec[:, 0:SEQ].rearrange("p (n t) -> p n t", t=CH),
                                      blk[:, :, CH - 1:CH].broadcast_to((P, NCH, CH)), blk, ALU.subtract)
                    dec.send(dve.tensor_tensor(k_dec[:, SEQ:NT].rearrange("p (n t) -> p n t", t=DSEQ),
                                               sv[:, :, DSEQ - 1:DSEQ].broadcast_to((P, NDEC, DSEQ)), sv, ALU.subtract))
                    e_done.wait(dve, l, 4 * j + 2)
                    kb = gk[:, j, 0:SEQ].rearrange("p (n t) -> p n t", t=CH)
                    for i in range(NSUB):
                        ln = SUB * (i + 1)
                        dst = k_sub[:, KHAT[i]:KHAT[i + 1]].rearrange("p (n t) -> p n t", t=ln)
                        dve.tensor_tensor(dst, dst, kb[:, :, 0:ln], ALU.mult)
                    dst = k_sub[:, KHAT[NSUB]:KHAT[NSUB] + P]
                    qk_ready.send(dve.tensor_tensor(dst, dst, gk[:, j, SEQ:NT], ALU.mult))
                    e_done.wait(dve, l, 4 * j + 3)
                    qk_ready.send(dve.tensor_tensor(k_dec[:], k_dec[:], gk[:, j, :], ALU.mult))

                def gla_scores(j):
                    b = GLA_BANKS[j]
                    att_mm.wait(dve, l, 2 * j)
                    if j:
                        o_mm.wait(dve, l, 2)
                    src = bank[b["A"]][:, :].rearrange("p (n h t) -> p n h t", n=4, h=2)
                    for par in range(2):
                        for i in range(NSUB):
                            r = slice(CH * par, CH * par + SUB * (i + 1))
                            t = slice(i * SUB, (i + 1) * SUB)
                            ta = slice(CH * par + i * SUB, CH * par + (i + 1) * SUB)
                            ln = SUB * (i + 1)
                            m = tri[r, t].unsqueeze(1).unsqueeze(1).broadcast_to((ln, 4, 2, SUB))
                            ins = dve.tensor_tensor(att[r, 0:4, :, ta], src[r, :, :, t], m, ALU.mult)
                    att_out.send(ins)
                    att_mm.wait(dve, l, 2 * j + 1)
                    att_out.send(dve.tensor_tensor(att[:, 4, :, :],
                                                   bank[b["AS"]][:, 0:2 * P].rearrange("p (h t) -> p h t", h=2),
                                                   bd[:].unsqueeze(1).broadcast_to((P, 2, P)), ALU.mult))
                    kdt_mm.wait(dve, l, 2 * j + 1)
                    if j:
                        ds_mm.wait(dve, l, 3)
                    k, o = b["KTS"]
                    kds_out.send(dve.tensor_tensor(kd_s[:], bank[k][:, o:o + P].unsqueeze(1).broadcast_to((P, NDEC, P)),
                                                   seqm[:].unsqueeze(2).broadcast_to((P, NDEC, P)), ALU.mult))

                def gla_carry(j):
                    b = GLA_BANKS[j]
                    if j:
                        o_mm.wait(dve, l, 1)
                        dve.wait_ge(gla_st, 64 * l + 32)
                    for n in range(NCH):
                        if n % 4 == 0:
                            ds_mm.wait(dve, l, 4 * j + n // 4)
                        add = bank[b["DS"][n // 4]][:, (n % 4) * GV:(n % 4 + 1) * GV]
                        if n == 0:
                            ins = dve.tensor_copy(s_p[:, 0, :], add)
                        else:
                            ins = dve.scalar_tensor_tensor(out=s_p[:, n, :], in0=s_p[:, n - 1, :],
                                                           scalar=elast[:, n:n + 1], in1=add, op0=ALU.mult, op1=ALU.add)
                        if n % 4 == 3:
                            ds_out.send(ins)
                            ds_out.last(dve, l)
                        else:
                            own(ins)

                def sample_states(j):
                    b = GLA_BANKS[j]
                    o_mm.wait(dve, l, 3 * j + 2)
                    dve.wait_ge(s_in, 32 * l + 16 * j + 16)
                    own(dve.tensor_tensor(s_s[:], s_s[:], elast[:, NCH:NCH + NDEC].unsqueeze(2)
                                          .broadcast_to((P, NDEC, GV)), ALU.mult))
                    for q in range(2):
                        ds_mm.wait(dve, l, 4 * j + 2 + q)
                        t = s_s[:, 4 * q:4 * q + 4, :]
                        ds_out.send(dve.tensor_tensor(t, t, bank[b["DSS"][q]][:, :].rearrange("p (i v) -> p i v", v=GV),
                                                      ALU.add))

                def gla_finish(j):
                    b = GLA_BANKS[j]
                    for i, (c0, c1) in enumerate(OSPAN):
                        orn.wait(dve, l, 6 * j + 3 + i)
                        o_mul.send(dve.tensor_tensor(o_sq[:, c0:c1], bank[b["O"][i]][:, 0:c1 - c0], o_rs[:, c0:c1],
                                                     ALU.mult))
                        o_mul.last(dve, l)
                        t0, n = (0, 256, 512)[i], (c1 - c0) // 2
                        t = gog[:, 2 * j:2 * j + 2, t0:t0 + n]
                        gla_fin.send(dve.scalar_tensor_tensor(out=t, in0=o_sq[:, c0:c1].rearrange("p (h t) -> p h t", h=2),
                                                              scalar=gain[:, 2:3], in1=t, op0=ALU.mult, op1=ALU.mult))

                decays_in(0)
                for t in range(5):
                    if t < 4:
                        gv_mm.wait(dve, l, t)
                    else:
                        used(U_GV + 3)
                    gv_out.send(dve.tensor_copy(v_g[:, t, :], bank[(4, 5, 0, 1, 2)[t]][:, :]))
                gqk_out.wait(dve, l, 7)
                decays_out(0)
                block_queries(0)
                for c in range(KL):
                    for s in range(2):
                        if s == 0:
                            proj_mm.wait(dve, l, 12 + c)
                        else:
                            used(U_CKV + c)
                        ckv_ev.send(dve.tensor_copy(ckv[:, c, cols[s]], bank[((1, 2), (3, 6))[c][s]][:, 0:HALF]))
                ckv_ev.last(dve, l)
                gla_scores(0)
                decays_in(1)
                lsq.wait(dve, l, 4)
                for c in range(QL + KL):
                    for s in range(2):
                        i = s if c < QL else 2 + s
                        lrs.wait(dve, l, 4 + i)
                        t = cq[:, c, cols[s]] if c < QL else ckv[:, c - QL, cols[s]]
                        lat_n.send(dve.scalar_tensor_tensor(out=t, in0=t, scalar=gain[:, 3 + c:4 + c],
                                                            in1=bank[(1, 2, 3, 6)[i]][:, 0:HALF],
                                                            op0=ALU.mult, op1=ALU.mult))
                gla_carry(0)
                decays_out(1)
                sample_states(0)
                block_queries(1)
                for c in range(QL + KL):
                    chi_out.wait(dve, l, c)
                    t, hi, lo = (cq[:, c, :], qn_hi[:, c, :], qn_lo[:, c, :]) if c < QL else \
                        (ckv[:, c - QL, :], c_hi[:, c - QL, :], c_lo[:, c - QL, :])
                    if c == 0:
                        lat_n.last(dve, l)
                    clo.send(dve.tensor_tensor(lo, t, hi.bitcast(F32), ALU.subtract))

                gog_out.wait(dve, l, 7)
                gla_finish(0)
                gla_scores(1)
                gla_carry(1)
                sample_states(1)
                gla_finish(1)

                dve.wait_ge(cs_ld, 16 * l + 16)
                dve.wait_ge(gla_st, 64 * l + 64)

                def rope(lo, hi, c, dst, scale, sg):
                    own(dve.scalar_tensor_tensor(out=r_t[NOPE:96, 0:HALF], in0=hi, scalar=scale, in1=cs[96:P, c],
                                                 op0=ALU.mult, op1=ALU.mult))
                    own(dve.scalar_tensor_tensor(out=dst, in0=lo, scalar=scale, in1=cs[NOPE:96, c],
                                                 op0=ALU.mult, op1=ALU.mult))
                    sg.send(dve.tensor_tensor(dst, dst, r_t[NOPE:96, 0:HALF], ALU.add))
                    sg.last(dve, l)

                for s in range(2):
                    rope(kg[NOPE:96, cols[s]], kg[96:P, cols[s]], cols[s], kg[NOPE:96, cols[s]], 1.0, kpe_done)
                for h in range(MH):
                    for s in range(2):
                        if h % 2 and s:
                            used(U_UQ + h // 2)
                        else:
                            q_mm.wait(dve, l, 3 * (h // 2) + 2 * (h % 2) + s)
                        b = bank[QBANKS[h][s]]
                        rope(b[NOPE:96, 0:HALF], b[96:P, 0:HALF], cols[s], q_h[NOPE:96, h, cols[s]], MLA_SCALE, rope_done)
                qpe_out.send(dve.tensor_copy(q_pe[NOPE:96, :, :].rearrange("p i (h t) -> p h i t", t=DSEQ),
                                             q_h[NOPE:96, :, SEQ:NT].rearrange("p h (i t) -> p h i t", t=DSEQ)))

                def gla_low(n, h):
                    ohi_out.wait(dve, l, n)
                    olo.send(dve.tensor_tensor(o_lo[:, h, :], gog[:, h, :], o_hi[:, h, :].bitcast(F32), ALU.subtract))

                gla_low(0, 2)
                gla_low(1, 3)
                for t in range(4):
                    if t < 3:
                        v_mm.wait(dve, l, t)
                    else:
                        used(U_UV)
                    vm_out.send(dve.tensor_copy(v_m[:, t, :], bank[(6, 5, 7, 0)[t]][:, :]))
                gla_low(2, 0)
                gla_low(3, 1)
                olo.last(dve, l)
                cn_mm.wait(dve, l, 0)
                cn_out.send(dve.tensor_copy(cn_t[:], bank[6][:, 0:KL * P]))
                qa_mm.wait(dve, l, 3)
                for it in range(40 + 6):
                    if it < 40:
                        n, b = it % 4, bank[SBANKS[it % 4]]
                        if it >= 4:
                            t_mm.wait(dve, l, it - 4)
                        if it < NDEC:
                            if it >= 4:
                                p_norm.wait(dve, l, it - 4)
                            dve.memset(p_s[n][:, PAST:3 * P], 0.0)
                            w = PAST + DSEQ
                        else:
                            w = P * ((it - NDEC) % 4 + 1)
                        s_mm.wait(dve, l, it)
                        p_max.send(dve.tensor_reduce(mx[:, n:n + 1], b[:, 0:w], AX.X, ALU.max, negate=True))
                    if 1 <= it < 41:
                        jt = it - 1
                        n = jt % 4
                        p_exp.wait(dve, l, jt)
                        if jt >= 4:
                            p_norm.wait(dve, l, jt - 4)
                        if jt < NDEC:
                            own(dve.tensor_tensor(psum2[:, n:n + 1], psums[:, n:n + 1], psum2[:, n:n + 1], ALU.add))
                            own(dve.reciprocal(rsum[:, n:n + 1], psum2[:, n:n + 1]))
                            t = p_s[n][:]
                        else:
                            own(dve.reciprocal(rsum[:, n:n + 1], psums[:, n:n + 1]))
                            t = p_p[n][:, 0:P * ((jt - NDEC) % 4 + 1)]
                        p_norm.send(dve.tensor_scalar(t, t, rsum[:, n:n + 1], None, ALU.mult))
                    jo = it - 4
                    if 0 <= jo < NDEC:
                        ol_mm.wait(dve, l, jo)
                        ol_out.send(dve.tensor_copy(o_lat[:, :, :, DSEQ * jo:DSEQ * (jo + 1)],
                                                    bank[(1, 4)[jo % 2]][:, 0:KL * P]
                                                    .rearrange("p (c h t) -> p c h t", c=KL, t=DSEQ)))
                    if it == NDEC + 7:
                        ohi_out.wait(dve, l, 4)
                        olo.send(dve.tensor_tensor(o_lo[:, 4:8, SEQ:NT], bank[1][:, :].rearrange("p (c t) -> p c t", t=P),
                                                   o_hi[:, 4:8, SEQ:NT].bitcast(F32), ALU.subtract))
                    hp = (it - 5 - NDEC - 7) // 8
                    if it == NDEC + 8 * hp + 12 and 0 <= hp < 4:
                        ohi_out.wait(dve, l, 5 + hp)
                        olo.send(dve.tensor_tensor(o_lo[:, 4 + hp, 0:SEQ], bank[(4, 1)[hp % 2]][:, :],
                                                   o_hi[:, 4 + hp, 0:SEQ].bitcast(F32), ALU.subtract))
                dve.wait_ge(modg_done, 3 * l + 2)
                mod_ab(l, 2, DEPTH * ADA_PRO + ADA_IN + l * ADA_IN)
                for m in range(DC):
                    y = bank[4:6] if m % 2 == 0 else bank[2:4]
                    g = 3 * l + 2
                    residual(l * OUT_T + 3 * DC + m, m, *y, l * LAYER_U + FFN_U + U_OUT + m,
                             (lambda: add_square(g, DC - 2), lambda: add_last_square(g, 0)) if m == DC - 1 else ())
                    if 2 <= m < DC - 1:
                        add_square(g, m - 1)
                add_last_square(g, 1)

            dve.memset(ones[:], 1.0)
            dve.memset(eps[:], EPS).then_inc(const_done, 1)
            dve.memset(c_st[:].bitcast(F32), 0.0).then_inc(cst_done, 1)
            dve.wait_ge(cst_done, 1)
            dve.wait_ge(csil_done, 1)
            dve.tensor_copy(c_st[:, :, 0:NS], c_sil[:]).then_inc(cst_done, 1)
            dve.wait_ge(cst_done, 2)
            dve.tensor_tensor(c_st[:, :, NS:2 * NS], c_sil[:], c_st[:, :, 0:NS].bitcast(F32), ALU.subtract)\
                .then_inc(cst_done, 1)

            def ada_pair(i, start=False):
                for n in range(DEPTH):
                    t = DEPTH * i + n
                    late = not (start and n == 0)
                    for k in range(4):
                        ada_lo(4 * t + k, 4 * n + k)
                        if k == 1 and late:
                            ada_evict(t - 1, ADA_FIRST[1 - n])
                    if late:
                        ada_bias(t - 1, 1 - n, bass.ds(4 * (i - 1 + n), 4))

            ada_pair(0, start=True)
            for m in range(1, DC - 1):
                add_square(0, m)
            for s in range(2):
                add_last_square(0, s)
            with dve.Fori(1, ADA_PRO) as i:
                ada_pair(i)
            ada_evict(DEPTH * ADA_PRO - 1, ADA_FIRST[1])
            ada_bias(DEPTH * ADA_PRO - 1, 1, slice(4 * ADA_PRO - 4, 4 * ADA_PRO))
            dve.wait_ge(cst_in, 16 * 6)
            with dve.Fori(0, DEPTH) as l:
                norm_apply(l, 0, DEPTH * ADA_PRO)
                ffn(l, 0)
                norm_apply(l, 1, DEPTH * ADA_PRO + ADA_IN + l * ADA_IN)
                mix_dve(l)
                norm_apply(l, 2, DEPTH * ADA_PRO + ADA_IN + l * ADA_IN)
                ffn(l, 1)
            g = 3 * DEPTH
            for m in range(DC):
                for s in range(2):
                    dve.wait_ge(rstd_done, 2 * g + s + 1)
                    dve.scalar_tensor_tensor(out=y_sb[:, m, cols[s]], in0=x[:, m, cols[s]], scalar=fin_g[:, m:m + 1],
                                             in1=rstd[:, cols[s]], op0=ALU.mult, op1=ALU.mult).then_inc(y_done, 1)
    for sg in signals:
        assert sg.sent == sg.per_layer, (sg.sem, sg.sent, sg.per_layer)
    return nc


def layout(inputs):
    import numpy as np
    f = {k: np.ascontiguousarray(np.asarray(v)) for k, v in inputs.items()}

    def feat(a):
        return np.ascontiguousarray(a.T.reshape(-1, P, a.shape[0]).transpose(1, 0, 2))

    def chunked(w):
        return w.reshape(-1, P, w.shape[1]).transpose(1, 0, 2)

    def tiles(w):
        c = chunked(w)
        k = c.shape[1]
        u = c.reshape(P, k, -1, P).transpose(2, 0, 1, 3).reshape(-1, P, k * P)
        return np.pad(u, ((0, 0), (0, 0), (0, UW - k * P)))

    a = {}
    a["xT"] = feat(np.concatenate([f["x_prompt"].reshape(SEQ, D), f["x_sample"].reshape(-1, D)]))
    a["cT"] = feat(np.concatenate([f["c_prompt"], f["c_sample"]]))
    a["lng"] = np.ascontiguousarray(f["ln_g"].reshape(DEPTH, 3, DC, P).transpose(3, 0, 1, 2))
    a["bada"] = np.ascontiguousarray(f["b_ada"].reshape(DEPTH, NMOD, P).transpose(2, 0, 1))
    a["fing"] = np.ascontiguousarray(f["final_g"].reshape(DC, P).T)
    a["selc"] = np.tile(np.eye(NS, dtype=np.float32), (2, 1))
    main, ada, uvs, ukts = [], [], [], []
    for l in range(DEPTH):
        for nm in ("1", "mix", "2"):
            if nm == "mix":
                w = f["w_in"][l]
                o = np.cumsum([0, GH * GK, GH * GK, GH * GV, GR, GH * GV, QL * P, KL * P, ROPE])
                gq, gk, gv, glr, gog, cq, ckv, kpe = (w[:, o[i]:o[i + 1]] for i in range(8))
                s_tile = np.zeros((D, P), np.float32)
                s_tile[:, 0:GR] = glr
                s_tile[:, NOPE:96] = kpe
                s_tile[:, 96:P] = kpe[:, SWAP]
                main += [tiles(np.concatenate([s_tile, gq, gk, gog], 1)),
                         chunked(gv).reshape(P, 4, 2 * GH * GV).transpose(1, 0, 2),
                         tiles(np.concatenate([cq, ckv], 1))]
                uq = f["w_uq"][l].reshape(QL * P, MH, NOPE + ROPE)
                uq = np.concatenate([uq, uq[:, :, NOPE + np.array(SWAP)]], 2)
                uq = uq.reshape(QL, P, MH // 2, 2, P).transpose(2, 1, 3, 0, 4).reshape(MH // 2, P, 2 * QL * P)
                main.append(np.pad(uq, ((0, 0), (0, 0), (0, UW - 2 * QL * P))))
                ukv = f["w_ukv"][l].reshape(KL * P, MH, NOPE + MV)
                uk = np.ascontiguousarray(ukv[:, :, :NOPE]).reshape(KL, P, 4, P)
                main.append(uk.transpose(1, 2, 0, 3).reshape(1, P, UW))
                uv = np.ascontiguousarray(ukv[:, :, NOPE:]).reshape(KL, P, MH * MV)
                main.append(uv.transpose(1, 0, 2).reshape(1, P, UW))
                uvs.append(uv.transpose(1, 0, 2))
                ukts.append(ukv[:, :, :NOPE].transpose(2, 1, 0))
                main.append(tiles(f["w_out"][l]))
                continue
            w_in = f[f"w_ffn{nm}_in"][l]
            gate_up = np.stack([tiles(w_in[:, :NFF * P]), tiles(w_in[:, NFF * P:])], 1)
            w_out = f[f"w_ffn{nm}_out"][l]
            for p in range(3):
                main.append(gate_up[PBASE[p]:PBASE[p] + PORT[p]].reshape(-1, P, UW))
                main.append(tiles(w_out[PBASE[p] * P:(PBASE[p] + PORT[p]) * P]))
        w = f["w_ada"][l].reshape(4, 2, P, 18, 512).transpose(3, 0, 2, 1, 4).reshape(18, 4, P, UW)
        ada.append(w)
    main.append(np.zeros((LEAD, P, UW), np.float32))
    a["wmain"] = np.concatenate(main)
    a["wada"] = np.concatenate([np.stack([w[:ADA_PRO] for w in ada], 1).reshape(-1, P, UW)]
                               + [w[ADA_PRO:].reshape(-1, P, UW) for w in ada])
    a["ukT"], a["wuv"] = np.stack(ukts), np.stack(uvs)
    a["gk2"] = f["w_gk2"]
    feat2 = lambda v: v.reshape(DEPTH, -1, P).transpose(2, 0, 1)
    a["gains"] = np.concatenate([feat2(f["b_gk2"]), feat2(f["gla_norm_g"]), feat2(f["mla_qnorm_g"]),
                                 feat2(f["mla_kvnorm_g"])], 2)
    ckv, kpe = f["cache_ckv"], f["cache_kpe"]
    a["pastkT"] = ckv.reshape(DEPTH * NDEC, PAST, KL, P).transpose(0, 3, 2, 1)
    a["pastv"] = ckv.reshape(DEPTH * NDEC, 2, P, KL * P).transpose(0, 2, 1, 3)
    a["pastpe"] = kpe.reshape(DEPTH * NDEC, PAST, ROPE).transpose(0, 2, 1)
    a["s0"] = f["state_gla"].reshape(DEPTH, NDEC, 2, P, GV).transpose(0, 2, 3, 1, 4).reshape(2 * DEPTH, P, NDEC, GV)
    a.update(shape_constants())
    return a


SWAP = list(range(ROPE // 2, ROPE)) + list(range(ROPE // 2))


def shape_constants():
    import numpy as np
    i = np.arange(P)
    one = np.float32
    t = np.arange(NT)
    start = np.where(t < SEQ, t % CH == 0, (t - SEQ) % DSEQ == 0)
    pos = np.where(t < SEQ, t, PAST + (t - SEQ) % DSEQ).astype(one)
    half = ROPE // 2
    inv = (one(10000.0) ** (-np.arange(half, dtype=one) / one(half))).astype(one)
    ang = (pos[None, :] * inv[:, None]).astype(one)
    cs = np.zeros((P, NT), one)
    cs[NOPE:96] = np.tile(np.cos(ang), (2, 1))
    cs[96:P] = np.concatenate([-np.sin(ang), np.sin(ang)])
    mrow = np.zeros((1, P + CH), one)
    mrow[0, :CH] = SHARP
    mrow[0, P:] = 1.0
    return {
        "scanm": np.ascontiguousarray(np.broadcast_to(1.0 - start, (P, NT)).astype(one)),
        "tri": (i[:, None] % CH <= i[None, :CH]).astype(one),
        "bd": ((i[:, None] // DSEQ == i[None] // DSEQ) & (i[:, None] <= i[None])).astype(one),
        "seqm": (i[:, None] // DSEQ == np.arange(NDEC)[None]).astype(one),
        "ident": np.eye(P, dtype=one), "mrow": mrow, "cs": cs,
    }


_INS = ["xT", "cT", "lng", "bada", "fing", "selc", "wmain", "wada", "scanm", "gk2", "gains", "tri",
        "bd", "seqm", "ident", "mrow", "cs", "ukT", "wuv", "pastkT", "pastv", "pastpe", "s0"]


def kernel(**inputs):
    import numpy as np
    import concourse.bacc as bacc
    from concourse import mybir as mb
    from concourse.bass_utils import run_bass_kernel_spmd as run

    nc = bacc.Bacc("TRN2", target_bir_lowering=False, num_devices=1)
    a = layout(inputs)
    arrays = {f"in_{n}": np.ascontiguousarray(a[n]) for n in _INS}
    args = [nc.dram_tensor(f"in_{n}", a[n].shape, mb.dt.from_np(a[n].dtype), kind="ExternalInput").ap() for n in _INS]
    outs = (("y", (P, DC, NT)), ("ckv", (DEPTH, P, KL, NT)), ("kpe", (DEPTH, ROPE, NT)),
            ("glap", (2 * DEPTH, P, GV)), ("glas", (2 * DEPTH, P, NDEC, GV)))
    out_aps = [nc.dram_tensor(n, s, mb.dt.float32, kind="ExternalOutput").ap() for n, s in outs]
    build(nc, *args, *out_aps)
    r = run(nc, [arrays], core_ids=[0]).results[0]
    c = np.ascontiguousarray
    y = r["y"].transpose(2, 1, 0).reshape(NT, D)
    ckv = r["ckv"].transpose(0, 3, 2, 1).reshape(DEPTH, NT, KL * P)
    kpe = r["kpe"].transpose(0, 2, 1)
    glap = r["glap"].reshape(DEPTH, 1, GH, GK, GV)
    glas = r["glas"].reshape(DEPTH, 2, 2, GK, NDEC, GV).transpose(0, 4, 1, 2, 3, 5).reshape(DEPTH, NDEC, GH, GK, GV)
    return (c(y[:SEQ]).reshape(1, SEQ, D), c(y[SEQ:]).reshape(NDEC, DSEQ, D),
            c(ckv[:, :SEQ]).reshape(DEPTH, 1, SEQ, KL * P), c(kpe[:, :SEQ]).reshape(DEPTH, 1, SEQ, ROPE), c(glap),
            c(ckv[:, SEQ:]).reshape(DEPTH, NDEC, DSEQ, KL * P), c(kpe[:, SEQ:]).reshape(DEPTH, NDEC, DSEQ, ROPE), c(glas))
```
